# Optimizing a Trainium2 kernel written in Bass

```python
import math
import jax
import jax.numpy as jnp
from jax import lax
import numpy as np

D_MODEL = 1024
BATCH = 1
SEQ = 512
DEPTH = 1
DEC_BATCH = 8
DEC_SEQ = 8
PAST_LEN = 1024
PAGE_SIZE = 128

N_ATT_HEADS = 16
ATT_HEAD_DIM = 64
N_KV_HEADS = 4
GQA = N_ATT_HEADS // N_KV_HEADS
ATT_WIDTH = N_ATT_HEADS * ATT_HEAD_DIM
KV_WIDTH = 2 * N_KV_HEADS * ATT_HEAD_DIM
BLK = 64
N_SEL = 16
WINDOW = 512
N_BRANCH = 3
Q_BLOCK = 128
N_BUCKETS = 32
MAX_DISTANCE = 128
SSD_HEADS = 16
SSD_HEAD_DIM = 64
SSD_INNER = SSD_HEADS * SSD_HEAD_DIM
SSD_GROUPS = 2
SSD_STATE = 128
CONV_W = 4
CONV_DIM = SSD_INNER + 2 * SSD_GROUPS * SSD_STATE
CHUNK = 128
D_MIX = ATT_WIDTH + SSD_INNER
D_FF = 2816
IN_SPLITS = (ATT_WIDTH, KV_WIDTH, KV_WIDTH, KV_WIDTH, N_BRANCH * N_ATT_HEADS, SSD_INNER, CONV_DIM, SSD_HEADS)
D_IN = ATT_WIDTH + 3 * KV_WIDTH + N_BRANCH * N_ATT_HEADS + SSD_INNER + CONV_DIM + SSD_HEADS
EPS = 1e-6

kernel_name = 'hymba_nsa_ssd_macaron_step'

def rmsnorm(x, g):
    xf = x.astype(jnp.float32)
    y = xf * lax.rsqrt(jnp.mean(xf * xf, axis=-1, keepdims=True) + EPS)
    return (y * g.astype(jnp.float32)).astype(x.dtype)

def swiglu(x, w_in, w_out):
    gate, up = jnp.split(x @ w_in, 2, axis=-1)
    return (jax.nn.silu(gate) * up) @ w_out

def ffn_sublayer(x, pre_g, post_g, w_in, w_out):
    return x + 0.5 * rmsnorm(swiglu(rmsnorm(x, pre_g), w_in, w_out), post_g)

def masked_softmax(s, mask):
    s = jnp.where(mask, s, -jnp.inf)
    m = jnp.max(s, axis=-1, keepdims=True)
    m = jnp.where(jnp.isfinite(m), m, 0.0)
    p = jnp.exp(s - m)
    return p / jnp.maximum(jnp.sum(p, axis=-1, keepdims=True), 1e-30)

def rel_bucket(dist):
    n = jnp.maximum(dist, 0)
    max_exact = N_BUCKETS // 2
    nf = jnp.maximum(n, 1).astype(jnp.float32)
    log_b = max_exact + (jnp.log(nf / max_exact) / math.log(MAX_DISTANCE / max_exact)
                         * (N_BUCKETS - max_exact)).astype(jnp.int32)
    return jnp.where(n < max_exact, n, jnp.minimum(log_b, N_BUCKETS - 1))

def split_in_proj(u):
    offs, acc = [], 0
    for s in IN_SPLITS[:-1]:
        acc += s
        offs.append(acc)
    return jnp.split(u, offs, axis=-1)

def mixer_inputs(x, pre_g, w_in):
    b, t = x.shape[0], x.shape[1]
    q, ckv, skv, wkv, gates, z, xbc, dt = split_in_proj(rmsnorm(x, pre_g) @ w_in)
    kv_shape = (b, t, N_KV_HEADS, 2, ATT_HEAD_DIM)
    return (q.reshape(b, t, N_KV_HEADS, GQA, ATT_HEAD_DIM), ckv.reshape(kv_shape), skv.reshape(kv_shape),
            wkv.reshape(kv_shape), gates, z, xbc, dt)

def mixer_output(x, o_att, o_ssd, att_out_norm, post_g, w_out):
    o = jnp.concatenate([rmsnorm(o_att, att_out_norm), o_ssd.astype(o_att.dtype)], axis=-1) @ w_out
    return x + rmsnorm(o, post_g)

def compress_blocks(kv_blocks, cmp_pe, w_cmp):
    out = jnp.einsum('bnlhcd,lcde->bnhce', kv_blocks, w_cmp, preferred_element_type=jnp.float32)
    return out + jnp.einsum('lcd,lcde->ce', cmp_pe, w_cmp, preferred_element_type=jnp.float32)

def nsa_query_block(q, pos, gates, kc, vc, fetch_sel, wkv, wpos, rel_table):
    b, t = q.shape[0], q.shape[1]
    nb = kc.shape[1]
    f32 = jnp.float32
    scale = ATT_HEAD_DIM ** -0.5
    table = rel_table.astype(f32)

    def head_bias(dist):
        bias = table[rel_bucket(dist)]
        return bias.reshape(dist.shape + (N_KV_HEADS, GQA)).transpose(2, 3, 0, 1)

    blk = jnp.arange(nb, dtype=jnp.int32)
    c_dist = pos[:, None] - ((blk + 1) * BLK - 1)[None, :]
    s_c = jnp.einsum('btkgd,bnkd->bkgtn', q, kc, preferred_element_type=f32) * scale + head_bias(c_dist)
    p_c = masked_softmax(s_c, c_dist >= 0)
    o_c = jnp.einsum('bkgtn,bnkd->btkgd', p_c, vc.astype(f32))

    cur = (pos // BLK)[:, None]
    forced = (blk[None] == 0) | (blk[None] == cur) | (blk[None] == cur - 1)
    imp = jnp.sum(p_c, axis=2)
    score = jnp.where(forced, jnp.inf, jnp.where(blk[None] <= cur, imp, -jnp.inf))
    top_s, idx = lax.top_k(score, min(N_SEL, nb))
    idx = idx.transpose(0, 2, 1, 3)
    sel_ok = (top_s > -jnp.inf).transpose(0, 2, 1, 3)
    k_sel, v_sel = fetch_sel(idx)
    n = idx.shape[-1]
    kpos = idx[..., None] * BLK + jnp.arange(BLK, dtype=jnp.int32)
    s_dist = pos[None, :, None, None, None] - kpos
    s_mask = sel_ok[..., None] & (s_dist >= 0)
    kv_ix = jnp.arange(N_KV_HEADS)[None, None, :, None, None]
    s_bias = table.reshape(N_BUCKETS, N_KV_HEADS, GQA)[rel_bucket(s_dist), kv_ix]
    s_s = jnp.einsum('btkgd,btknld->btkgnl', q, k_sel, preferred_element_type=f32) * scale \
        + jnp.moveaxis(s_bias, -1, 3)
    p_s = masked_softmax(s_s.reshape(b, t, N_KV_HEADS, GQA, n * BLK),
                         s_mask.reshape(b, t, N_KV_HEADS, 1, n * BLK))
    o_s = jnp.einsum('btkgm,btkmd->btkgd', p_s,
                     v_sel.reshape(b, t, N_KV_HEADS, n * BLK, ATT_HEAD_DIM).astype(f32))

    w_dist = pos[:, None] - wpos[None, :]
    w_mask = (w_dist >= 0) & (w_dist < WINDOW) & (wpos[None, :] >= 0)
    s_w = jnp.einsum('btkgd,bskd->bkgts', q, wkv[..., 0, :], preferred_element_type=f32) * scale + head_bias(w_dist)
    p_w = masked_softmax(s_w, w_mask)
    o_w = jnp.einsum('bkgts,bskd->btkgd', p_w, wkv[..., 1, :].astype(f32))

    g = jax.nn.sigmoid(gates.astype(f32)).reshape(b, t, N_KV_HEADS, GQA, N_BRANCH)
    o = g[..., 0:1] * o_c + g[..., 1:2] * o_s + g[..., 2:3] * o_w
    return o.reshape(b, t, ATT_WIDTH).astype(q.dtype)

def nsa_prompt(q, gates, cmp_kv, slc_kv, win_kv, cmp_pe, w_cmp, rel_table):
    b, s = q.shape[0], q.shape[1]
    nb = s // BLK
    ckv = compress_blocks(cmp_kv.reshape(b, nb, BLK, N_KV_HEADS, 2, ATT_HEAD_DIM), cmp_pe, w_cmp)
    kc, vc = ckv[..., 0, :], ckv[..., 1, :]
    slc_blocks = slc_kv.reshape(b, nb, BLK, N_KV_HEADS, 2, ATT_HEAD_DIM)
    b_ix = jnp.arange(b)[:, None, None, None]
    h_ix = jnp.arange(N_KV_HEADS)[None, None, :, None]

    def fetch(idx):
        rows = slc_blocks[b_ix, idx, :, h_ix]
        return rows[..., 0, :], rows[..., 1, :]

    win_pad = jnp.pad(win_kv, ((0, 0), (WINDOW, 0), (0, 0), (0, 0), (0, 0)))
    nq = s // Q_BLOCK
    qb = jnp.moveaxis(q.reshape(b, nq, Q_BLOCK, N_KV_HEADS, GQA, ATT_HEAD_DIM), 1, 0)
    gb = jnp.moveaxis(gates.reshape(b, nq, Q_BLOCK, N_BRANCH * N_ATT_HEADS), 1, 0)

    def one_block(args):
        i, q_i, g_i = args
        s0 = i * Q_BLOCK
        pos = s0 + jnp.arange(Q_BLOCK, dtype=jnp.int32)
        wkv = lax.dynamic_slice_in_dim(win_pad, s0, WINDOW + Q_BLOCK, axis=1)
        wpos = s0 - WINDOW + jnp.arange(WINDOW + Q_BLOCK, dtype=jnp.int32)
        return nsa_query_block(q_i, pos, g_i, kc, vc, fetch, wkv, wpos, rel_table)

    o = lax.map(one_block, (jnp.arange(nq, dtype=jnp.int32), qb, gb))
    return jnp.moveaxis(o, 0, 1).reshape(b, s, ATT_WIDTH)

def nsa_sample(q, gates, cmp_new, slc_new, win_new, cache_cmp, cache_slc, cache_win, page_table,
               cmp_pe, w_cmp, rel_table):
    b, t = q.shape[0], q.shape[1]
    npb = PAST_LEN // BLK
    nbn = -(-t // BLK)
    bpp = PAGE_SIZE // BLK
    pad = ((0, 0), (0, nbn * BLK - t), (0, 0), (0, 0), (0, 0))
    new_shape = (b, nbn, BLK, N_KV_HEADS, 2, ATT_HEAD_DIM)
    past_cmp = cache_cmp[page_table].reshape(b, npb, BLK, N_KV_HEADS, 2, ATT_HEAD_DIM)
    ckv = jnp.concatenate([compress_blocks(past_cmp, cmp_pe, w_cmp),
                           compress_blocks(jnp.pad(cmp_new, pad).reshape(new_shape), cmp_pe, w_cmp)], axis=1)
    kc, vc = ckv[..., 0, :], ckv[..., 1, :]
    pool = cache_slc.reshape((-1, bpp, BLK, N_KV_HEADS, 2, ATT_HEAD_DIM))
    new_blocks = jnp.pad(slc_new, pad).reshape(new_shape)
    b_ix = jnp.arange(b)[:, None, None, None]
    h_ix = jnp.arange(N_KV_HEADS)[None, None, :, None]

    def fetch(idx):
        in_past = (idx < npb)[..., None, None, None]
        pidx = jnp.minimum(idx, npb - 1)
        phys = page_table[b_ix, pidx // bpp]
        from_pool = pool[phys, pidx % bpp, :, h_ix]
        from_new = new_blocks[b_ix, jnp.clip(idx - npb, 0, nbn - 1), :, h_ix]
        rows = jnp.where(in_past, from_pool, from_new)
        return rows[..., 0, :], rows[..., 1, :]

    w_buf = cache_win.shape[1]
    wkv = jnp.concatenate([cache_win.astype(win_new.dtype), win_new], axis=1)
    wpos = PAST_LEN - w_buf + jnp.arange(w_buf + t, dtype=jnp.int32)
    pos = PAST_LEN + jnp.arange(t, dtype=jnp.int32)
    o = nsa_query_block(q, pos, gates, kc, vc, fetch, wkv, wpos, rel_table)
    return o, wkv[:, -min(WINDOW, w_buf + t):]

def causal_dwconv(xpad, w, bias):
    out = lax.conv_general_dilated(xpad, w[:, None, :].astype(xpad.dtype), window_strides=(1,), padding='VALID',
                                   dimension_numbers=('NWC', 'WIO', 'NWC'), feature_group_count=xpad.shape[-1])
    return out + bias

def ssd_scan(x, dt, a, b_in, c_in, h0):
    bsz, seq, nh, hp = x.shape
    r = nh // SSD_GROUPS
    cl = min(CHUNK, seq)
    nc = seq // cl
    f32 = jnp.float32
    xdt = (x.astype(f32) * dt[..., None]).reshape(bsz, nc, cl, SSD_GROUPS, r, hp)
    la = jnp.moveaxis((dt * a).reshape(bsz, nc, cl, SSD_GROUPS, r), 2, -1)
    bc = b_in.astype(f32).reshape(bsz, nc, cl, SSD_GROUPS, SSD_STATE)
    cc = c_in.astype(f32).reshape(bsz, nc, cl, SSD_GROUPS, SSD_STATE)
    cs = jnp.cumsum(la, axis=-1)
    causal = jnp.tril(jnp.ones((cl, cl), bool))
    decay = jnp.where(causal, jnp.exp(jnp.where(causal, cs[..., :, None] - cs[..., None, :], 0.0)), 0.0)
    cb = jnp.einsum('bclgn,bcsgn->bcgls', cc, bc)
    y_diag = jnp.einsum('bcgrls,bcsgrp->bclgrp', cb[:, :, :, None] * decay, xdt)
    to_end = jnp.exp(cs[..., -1:] - cs)
    chunk_states = jnp.einsum('bclgn,bcgrl,bclgrp->bcgrpn', bc, to_end, xdt)
    chunk_decay = jnp.exp(cs[..., -1])

    def step(h, inp):
        st, dc = inp
        return h * dc[..., None, None] + st, h

    h_last, h_start = lax.scan(step, h0.astype(f32).reshape(bsz, SSD_GROUPS, r, hp, SSD_STATE),
                               (jnp.moveaxis(chunk_states, 1, 0), jnp.moveaxis(chunk_decay, 1, 0)))
    h_start = jnp.moveaxis(h_start, 0, 1)
    y_off = jnp.einsum('bclgn,bcgrpn,bcgrl->bclgrp', cc, h_start, jnp.exp(cs))
    y = (y_diag + y_off).reshape(bsz, seq, nh, hp)
    return y, h_last.reshape(bsz, nh, hp, SSD_STATE)

def ssd_mixer(z, xbc, dt_raw, conv_prev, h0, conv_w, conv_b, dt_bias, a_log, d_skip, ssd_norm):
    bsz, seq = xbc.shape[0], xbc.shape[1]
    f32 = jnp.float32
    xpad = jnp.concatenate([conv_prev.astype(xbc.dtype), xbc], axis=1)
    new_conv = xpad[:, -(CONV_W - 1):]
    u = jax.nn.silu(causal_dwconv(xpad, conv_w, conv_b).astype(f32))
    xs = u[..., :SSD_INNER].reshape(bsz, seq, SSD_HEADS, SSD_HEAD_DIM)
    bm = u[..., SSD_INNER:SSD_INNER + SSD_GROUPS * SSD_STATE].reshape(bsz, seq, SSD_GROUPS, SSD_STATE)
    cm = u[..., SSD_INNER + SSD_GROUPS * SSD_STATE:].reshape(bsz, seq, SSD_GROUPS, SSD_STATE)
    dt = jax.nn.softplus(dt_raw.astype(f32) + dt_bias.astype(f32))
    a = -jnp.exp(a_log.astype(f32))
    y, h_last = ssd_scan(xs, dt, a, bm, cm, h0)
    y = (y + d_skip.astype(f32)[:, None] * xs).reshape(bsz, seq, SSD_INNER) * jax.nn.silu(z.astype(f32))
    yg = y.reshape(bsz, seq, SSD_GROUPS, SSD_INNER // SSD_GROUPS)
    yg = yg * lax.rsqrt(jnp.mean(yg * yg, axis=-1, keepdims=True) + EPS)
    y = yg.reshape(bsz, seq, SSD_INNER) * ssd_norm.astype(f32)
    return y.astype(z.dtype), h_last.astype(z.dtype), new_conv

def setup_inputs(seed: int = 0) -> dict:
    key = jax.random.key(seed)
    ks = list(jax.random.split(key, 32))

    def nrm(i, shape, scale):
        return jax.random.normal(ks[i], shape, jnp.float32) * scale

    n_pages = PAST_LEN // PAGE_SIZE
    n_used = DEC_BATCH * n_pages
    n_pool = n_used + max(1, n_used // 4)
    page_table = jax.random.permutation(ks[0], n_pool)[:n_used].reshape(DEC_BATCH, n_pages).astype(jnp.int32)
    w_buf = min(WINDOW, PAST_LEN)
    kv = (N_KV_HEADS, 2, ATT_HEAD_DIM)
    dt0 = jnp.exp(jax.random.uniform(ks[1], (DEPTH, SSD_HEADS), jnp.float32, math.log(1e-3), math.log(1e-1)))
    return {
        'x_prompt': nrm(2, (BATCH, SEQ, D_MODEL), 1.0),
        'x_sample': nrm(3, (DEC_BATCH, DEC_SEQ, D_MODEL), 1.0),
        'cache_cmp_kv': nrm(4, (DEPTH, n_pool, PAGE_SIZE) + kv, 1.0),
        'cache_slc_kv': nrm(5, (DEPTH, n_pool, PAGE_SIZE) + kv, 1.0),
        'cache_win_kv': nrm(6, (DEPTH, DEC_BATCH, w_buf) + kv, 1.0),
        'state_ssm': nrm(7, (DEPTH, DEC_BATCH, SSD_HEADS, SSD_HEAD_DIM, SSD_STATE), 0.3),
        'state_conv': nrm(8, (DEPTH, DEC_BATCH, CONV_W - 1, CONV_DIM), 1.0),
        'page_table': page_table,
        'rel_table': nrm(9, (N_BUCKETS, N_ATT_HEADS), 0.5),
        'ffn1_pre': 1.0 + nrm(10, (DEPTH, D_MODEL), 0.05),
        'ffn1_post': 1.0 + nrm(11, (DEPTH, D_MODEL), 0.05),
        'ffn1_w_in': nrm(12, (DEPTH, D_MODEL, 2 * D_FF), D_MODEL ** -0.5),
        'ffn1_w_out': nrm(13, (DEPTH, D_FF, D_MODEL), D_FF ** -0.5),
        'mix_pre': 1.0 + nrm(14, (DEPTH, D_MODEL), 0.05),
        'mix_post': 1.0 + nrm(15, (DEPTH, D_MODEL), 0.05),
        'w_in': nrm(16, (DEPTH, D_MODEL, D_IN), D_MODEL ** -0.5),
        'w_out': nrm(17, (DEPTH, D_MIX, D_MODEL), D_MIX ** -0.5),
        'att_out_norm': 1.0 + nrm(18, (DEPTH, ATT_WIDTH), 0.05),
        'cmp_pe': nrm(19, (DEPTH, BLK, 2, ATT_HEAD_DIM), 0.5),
        'w_cmp': nrm(20, (DEPTH, BLK, 2, ATT_HEAD_DIM, ATT_HEAD_DIM), (BLK * ATT_HEAD_DIM) ** -0.5),
        'conv_w': nrm(21, (DEPTH, CONV_W, CONV_DIM), CONV_W ** -0.5),
        'conv_b': nrm(22, (DEPTH, CONV_DIM), 0.02),
        'dt_bias': dt0 + jnp.log(-jnp.expm1(-dt0)),
        'a_log': jnp.log(jax.random.uniform(ks[23], (DEPTH, SSD_HEADS), jnp.float32, 1.0, 16.0)),
        'd_skip': 1.0 + nrm(24, (DEPTH, SSD_HEADS), 0.1),
        'ssd_norm': 1.0 + nrm(25, (DEPTH, SSD_INNER), 0.05),
        'ffn2_pre': 1.0 + nrm(26, (DEPTH, D_MODEL), 0.05),
        'ffn2_post': 1.0 + nrm(27, (DEPTH, D_MODEL), 0.05),
        'ffn2_w_in': nrm(28, (DEPTH, D_MODEL, 2 * D_FF), D_MODEL ** -0.5),
        'ffn2_w_out': nrm(29, (DEPTH, D_FF, D_MODEL), D_FF ** -0.5),
    }

def reference(x_prompt, x_sample, cache_cmp_kv, cache_slc_kv, cache_win_kv, state_ssm, state_conv, page_table,
              rel_table, ffn1_pre, ffn1_post, ffn1_w_in, ffn1_w_out, mix_pre, mix_post, w_in, w_out, att_out_norm,
              cmp_pe, w_cmp, conv_w, conv_b, dt_bias, a_log, d_skip, ssd_norm,
              ffn2_pre, ffn2_post, ffn2_w_in, ffn2_w_out):
    yp, ys = x_prompt, x_sample
    pc, psl, pw, pssm, pconv = [], [], [], [], []
    sc, ssl, sw, sssm, sconv = [], [], [], [], []
    for l in range(DEPTH):
        yp = ffn_sublayer(yp, ffn1_pre[l], ffn1_post[l], ffn1_w_in[l], ffn1_w_out[l])
        ys = ffn_sublayer(ys, ffn1_pre[l], ffn1_post[l], ffn1_w_in[l], ffn1_w_out[l])

        q, ckv, skv, wkv, gates, z, xbc, dt = mixer_inputs(yp, mix_pre[l], w_in[l])
        o_att = nsa_prompt(q, gates, ckv, skv, wkv, cmp_pe[l], w_cmp[l], rel_table)
        conv0 = jnp.zeros((yp.shape[0], CONV_W - 1, CONV_DIM), xbc.dtype)
        h0 = jnp.zeros((yp.shape[0], SSD_HEADS, SSD_HEAD_DIM, SSD_STATE), jnp.float32)
        o_ssd, h_new, conv_new = ssd_mixer(z, xbc, dt, conv0, h0, conv_w[l], conv_b[l], dt_bias[l], a_log[l],
                                           d_skip[l], ssd_norm[l])
        yp = mixer_output(yp, o_att, o_ssd, att_out_norm[l], mix_post[l], w_out[l])
        pc.append(ckv)
        psl.append(skv)
        pw.append(wkv[:, -min(WINDOW, wkv.shape[1]):])
        pssm.append(h_new)
        pconv.append(conv_new)

        q, ckv, skv, wkv, gates, z, xbc, dt = mixer_inputs(ys, mix_pre[l], w_in[l])
        o_att, win_state = nsa_sample(q, gates, ckv, skv, wkv, cache_cmp_kv[l], cache_slc_kv[l], cache_win_kv[l],
                                      page_table, cmp_pe[l], w_cmp[l], rel_table)
        o_ssd, h_new, conv_new = ssd_mixer(z, xbc, dt, state_conv[l], state_ssm[l], conv_w[l], conv_b[l],
                                           dt_bias[l], a_log[l], d_skip[l], ssd_norm[l])
        ys = mixer_output(ys, o_att, o_ssd, att_out_norm[l], mix_post[l], w_out[l])
        sc.append(ckv)
        ssl.append(skv)
        sw.append(win_state)
        sssm.append(h_new)
        sconv.append(conv_new)

        yp = ffn_sublayer(yp, ffn2_pre[l], ffn2_post[l], ffn2_w_in[l], ffn2_w_out[l])
        ys = ffn_sublayer(ys, ffn2_pre[l], ffn2_post[l], ffn2_w_in[l], ffn2_w_out[l])

    p_cmp_kv = jnp.stack(pc)
    p_slc_kv = jnp.stack(psl)
    p_win_kv = jnp.stack(pw)
    p_ssm = jnp.stack(pssm)
    p_conv = jnp.stack(pconv)
    s_cmp_kv = jnp.stack(sc)
    s_slc_kv = jnp.stack(ssl)
    s_win_kv = jnp.stack(sw)
    s_ssm = jnp.stack(sssm)
    s_conv = jnp.stack(sconv)
    return (yp, ys, p_cmp_kv, p_slc_kv, p_win_kv, p_ssm, p_conv, s_cmp_kv, s_slc_kv, s_win_kv, s_ssm, s_conv)


_drawn_inputs = setup_inputs


def setup_inputs(seed=0):
    import zlib

    import numpy as np

    out = dict(_drawn_inputs(seed))
    spreads = {}
    factors = {'ffn2_post': 3.942}
    for name, (base, spread) in spreads.items():
        noise = np.random.default_rng([zlib.crc32(name.encode()), seed]).standard_normal(out[name].shape)
        drawn = base * np.exp(spread * noise) if base else spread * noise
        out[name] = jnp.asarray(drawn.astype(out[name].dtype))
    for name, factor in factors.items():
        out[name] = (out[name] * factor).astype(out[name].dtype)
    return out
```

```python
from contextlib import ExitStack

import numpy as np

import concourse.bass as bass
from concourse import mybir

F32 = mybir.dt.float32
I32 = mybir.dt.int32
ALU = mybir.AluOpType
ACT = mybir.ActivationFunctionType
AXX = mybir.AxisListType.X

D_MODEL, SEQ, DEC_BATCH, DEC_SEQ, PAST_LEN, PAGE = 1024, 512, 8, 8, 1024, 128
N_HEADS, HD, N_KV, GQA = 16, 64, 4, 4
ATT_WIDTH, KV_WIDTH = 1024, 512
BLK, WINDOW, N_BUCKETS, MAX_DISTANCE = 64, 512, 32, 128
SSD_HEADS, SSD_GROUPS, SSD_STATE, CONV_W = 16, 2, 128, 4
SSD_INNER, CONV_DIM, D_MIX, D_FF, N_BRANCH = 1024, 1536, 2048, 2816, 3
N_POOL = 80
EPS = 1e-6
SCALE = HD ** -0.5
MASKED = -1e30

P = 128
NS = DEC_BATCH * DEC_SEQ
T = SEQ + NS
TILES = [(i * P, P) for i in range(SEQ // P)] + [(SEQ, NS)]
KD = D_MODEL // P
KF = D_FF // P
KC_XBC = CONV_DIM // P
PAGES = PAST_LEN // PAGE
ALL_PAGES = DEC_BATCH * PAGES
PAD = CONV_W - 1
XP_S = PAD + SEQ
XP_RUN = PAD + DEC_SEQ
XP = XP_S + DEC_BATCH * XP_RUN
CONV_N = XP - PAD

COL_KV = ATT_WIDTH
COL_GATES = ATT_WIDTH + 3 * KV_WIDTH
COL_Z = COL_GATES + N_BRANCH * N_HEADS
COL_DT = COL_Z + SSD_INNER + CONV_DIM
D_IN = COL_DT + SSD_HEADS

LEN_R, TOP_R = 1664, 1151
LEN_F, LOW_F = 1024, -512
LEN_T = SEQ + P
FIRST_T = TOP_R - (SEQ - P) - (P - 1)
LEN_W, TOP_W = 544, 527


def bucket_of(dist):
    exact = N_BUCKETS // 2
    n = np.maximum(dist, 0)
    f = np.maximum(n, 1).astype(np.float32)
    far = exact + (np.log(f / np.float32(exact)) / np.float32(np.log(MAX_DISTANCE / exact))
                   * np.float32(N_BUCKETS - exact)).astype(np.int32)
    return np.where(n < exact, n, np.minimum(far, N_BUCKETS - 1))


def one_hot(dist, limit):
    b = np.where((dist < 0) | (dist >= limit), N_BUCKETS, bucket_of(dist))
    return (np.arange(N_BUCKETS + 1)[:, None] == b[None, :]).astype(np.float32)


def constants():
    big = 10 ** 9
    hot = np.concatenate([
        one_hot(TOP_R - np.arange(LEN_R), big),
        one_hot(LOW_F + np.arange(LEN_F), big),
        one_hot(TOP_W - np.arange(LEN_W), WINDOW)], axis=1)
    r = np.arange(P)
    same = r[:, None] // DEC_SEQ == r[None, :] // DEC_SEQ
    tri = r[:, None] <= r[None, :]
    group = (r[:, None] // 32 == r[None, :] // 32) & (r[:, None] % DEC_SEQ == r[None, :] % DEC_SEQ)
    squares = np.stack([np.eye(P), tri, np.ones((P, P)), tri & same, same, group], axis=1).astype(np.float32)
    order = np.arange(16)
    block = (2 * (order % PAGES) + order // PAGES).astype(np.float32)
    forced = (block == 0) | (block == 15)
    rows = np.zeros((P, 3, 16), np.float32)
    rows[:, 0, :] = block
    rows[:, 1, :] = np.where(forced, 1e30, 0.0)
    rows[:NS, 2, :DEC_BATCH] = np.arange(NS)[:, None] // DEC_SEQ == np.arange(DEC_BATCH)[None, :]
    return {"c_hot": hot, "c_squares": squares, "c_rows": rows}


IDENT, TRI, ONES, BTRI, BONES, GROUP = range(6)


class Chain:

    def __init__(self, eng, sem):
        self.eng, self.sem, self.n, self.base, self.per = eng, sem, 0, None, 0

    def link(self, ins):
        self.n += 1
        ins.then_inc(self.sem, 1)
        self.eng.wait_ge(self.sem, self.n if self.base is None else self.base + self.n)

    def enter(self, i, per):
        self.start, self.per, self.base = self.n, per, i * per

    def leave(self, count):
        assert self.n - self.start == self.per, (self.n - self.start, self.per)
        self.n, self.base = self.start + self.per * count, None


def build(nc, io, out):
    with ExitStack() as ctx:
        def sb(name, shape, dt=F32):
            return ctx.enter_context(nc.sbuf_tensor(name, shape, dt))

        stage_sems = []

        def sem(name, lasting=False):
            s = nc.alloc_semaphore(name)
            if not lasting:
                stage_sems.append(s)
            return s

        def recycle_semaphores():
            nc.clear_and_free_semaphores(list(stage_sems))
            stage_sems.clear()
            nc.all_engine_barrier()

        xT = sb("xT", [P, KD, T])
        sq6 = sb("sq6", [P, 6, P])
        crow = sb("crow", [P, 3, 16])
        gT = sb("gT", [P, 64])
        convT = sb("convT", [P, 5 * KC_XBC])
        small = sb("small", [P, 6, SSD_HEADS])
        rstd = sb("rstd", [P, T])
        sqr = sb("sqr", [P, 2, T])
        bias_cmp = sb("bias_cmp", [P, 4, N_HEADS, 8])
        kc_all = sb("kc_all", [P, 2, 2, ALL_PAGES])
        vc_all = sb("vc_all", [ALL_PAGES, 2, 256])
        pe_c = sb("pe_c", [P, 2])
        eps_sb = sb("eps_sb", [P, 1])
        page_sb = sb("page_sb", [1, ALL_PAGES], I32)
        AW = 42400
        arena = sb("arena", [P, AW])
        PS = ctx.enter_context(nc.psum_tensor("PS", [P, 8, 512], F32))

        def at(o, *dims):
            n = int(np.prod(dims))
            assert o + n <= AW, (o, n)
            v = arena[:, o:o + n]
            if len(dims) == 1:
                return v
            names = "abcd"[:len(dims)]
            return v.rearrange("p (" + " ".join(names) + ") -> p " + " ".join(names),
                               **{c: d for c, d in zip(names[1:], dims[1:])})

        ident = sq6[:, IDENT, :]
        scr_r = nc.dram_tensor("scr_r", (N_HEADS, LEN_R), F32)
        scr_o = nc.dram_tensor("scr_o", (N_BRANCH, NS, ATT_WIDTH), F32)
        scr_t = nc.dram_tensor("scr_t", (N_HEADS, P, LEN_T), F32)
        scr_w = nc.dram_tensor("scr_w", (N_HEADS, LEN_W), F32)
        G1PRE, G1POST, GMPRE, GMPOST, GATT, GSSD, G2PRE, G2POST = range(8)

        def halves(v):
            return v[:, 0:SEQ], v[:, SEQ:T]

        def setup():
            xnat = at(0, 5, D_MODEL)
            hot = at(5120, LEN_R + LEN_F + LEN_W)
            gnat = at(8400, 2, P)
            tabl = at(8700, N_HEADS)
            fr = at(8800, LEN_R + LEN_W)
            ld, s_mm, s_ev, s_scr, s_tab, s_fr = (sem("su_" + n) for n in ("ld", "mm", "ev", "scr", "tab", "fr"))
            s_small, s_ch, s_dch = sem("su_small"), sem("su_ch"), sem("su_dch")
            LOADS = 4 + 5 + 8 + 3
            pieces = [(0, 512), (512, 512), (1024, 512), (1536, LEN_R - 1536)]
            with nc.Block() as block:
                @block.sync
                def _(sp):
                    n = [0]

                    def load(dst, src):
                        sp.dma_start(dst, src).then_inc(ld, 16)
                        n[0] += 1
                    sp.wait_ge(s_tab, 1)
                    load(tabl[0:N_BUCKETS, :], io["rel_table"])
                    load(sq6[:, :, :], io["c_squares"])
                    load(crow[:, :, :], io["c_rows"])
                    load(hot[0:N_BUCKETS + 1, :], io["c_hot"])
                    for i in range(4):
                        load(xnat[:, i, :], io["x_prompt"][0, i * P:(i + 1) * P, :])
                    load(xnat[0:NS, 4, :], io["x_sample"].rearrange("b t d -> (b t) d"))
                    for w, name in enumerate(["ffn1_pre", "ffn1_post", "mix_pre", "mix_post", "att_out_norm",
                                              "ssd_norm", "ffn2_pre", "ffn2_post"]):
                        load(gnat[8 * w:8 * w + 8, 0, :], io[name].rearrange("l (k p) -> (l k) p", p=P))
                    load(gnat[0:48, 1, :], io["conv_w"].rearrange("l w (k p) -> (l w k) p", p=P))
                    load(gnat[48:60, 1, :], io["conv_b"].rearrange("l (k p) -> (l k) p", p=P))
                    load(page_sb[0:1, :], io["page_table"].rearrange("b n -> (b n)").rearrange("(a n) -> a n", a=1))
                    assert n[0] == LOADS
                    sp.wait_ge(s_fr, 5)
                    sp.wait_ge(s_ev, 1)
                    sp.dma_start(scr_r.ap()[:, :], fr[0:N_HEADS, 0:LEN_R]).then_inc(s_scr, 16)
                    sp.dma_start(scr_w.ap()[:, :], fr[0:N_HEADS, LEN_R:LEN_R + LEN_W]).then_inc(s_scr, 16)
                    sp.dma_start(scr_t.ap()[:, :, :], fr[0:N_HEADS, FIRST_T:FIRST_T + LEN_T].unsqueeze(1)
                                 .to_broadcast([N_HEADS, P, LEN_T])).then_inc(s_scr, 16)
                    sp.wait_ge(s_scr, 48)

                @block.scalar
                def _(act):
                    with nc.allow_non_contiguous_dma(reason="small vectors spread over partitions"):
                        for k, name in enumerate(["dt_bias", "a_log"]):
                            h = io[name]
                            act.dma_start(small[:, k, :], bass.AP(h.tensor, 0, [[0, P], [1, SSD_HEADS]])).then_inc(s_small, 16)
                        for half in range(2):
                            act.dma_start(small[half * 64:half * 64 + 64, 3, 0:8],
                                          bass.AP(io["d_skip"].tensor, half, [[0, 64], [2, 8]])).then_inc(s_small, 16)
                    act.wait_ge(s_small, 64)
                    act.activation(small[:, 2, :], small[:, 1, :], ACT.Exp).then_inc(s_ch, 1)
                    act.wait_ge(s_ch, 1)
                    act.mul(small[:, 2, :], small[:, 2, :], -1.0).then_inc(s_ch, 1)
                    act.wait_ge(s_ch, 2)

                @block.tensor
                def _(pe):
                    pe.wait_ge(ld, 16 * LOADS)
                    for k, (a, n) in enumerate(pieces + [(LEN_R + LEN_F, 512), (LEN_R + LEN_F + 512, LEN_W - 512)]):
                        if k == 5:
                            mm = pe.matmul(PS[0:N_HEADS, 0, 0:n], tabl[0:33, :], hot[0:33, a:a + n], start=True, stop=True)
                            continue
                        b = [1, 2, 3, 4, 5][k]
                        mm = pe.matmul(PS[0:N_HEADS, b, 0:n], tabl[0:33, :], hot[0:33, a:a + n], start=True, stop=True)
                    mm.then_inc(s_mm, 1)
                    for i in range(4):
                        for o in range(8):
                            n = 2 * (o % 4) + o // 4
                            v = LEN_R + i * P - BLK * n - (BLK - 1) - LOW_F
                            mm = pe.matmul(PS[:, 6, (i * 8 + o) * 16:(i * 8 + o + 1) * 16], hot[0:33, v:v + P],
                                           tabl[0:33, :], start=True, stop=True)
                    mm.then_inc(s_mm, 1)
                    pe.transpose(PS[:, 7, 0:64], gnat[0:64, 0, :], ident[0:64, 0:64])
                    pe.transpose(PS[:, 7, 64:124], gnat[0:60, 1, :], ident[0:60, 0:60]).then_inc(s_mm, 1)
                    u = 0
                    for i, (t0, n) in enumerate(TILES):
                        for q in range(2):
                            if u < 2:
                                pe.wait_ge(s_ev, 1)
                            else:
                                pe.wait_ge(s_ev, u - 2 + 4)
                            for j in range(4):
                                mm = pe.transpose(PS[:, u % 2, j * P:j * P + n],
                                                  xnat[0:n, i, (4 * q + j) * P:(4 * q + j + 1) * P], ident[0:n, 0:n])
                            mm.then_inc(s_mm, 1)
                            u += 1

                @block.vector
                def _(dve):
                    dve.memset(tabl[0:33, :], MASKED).then_inc(s_tab, 1)
                    dve.memset(eps_sb[:, :], EPS).then_inc(s_dch, 1)
                    dve.wait_ge(s_mm, 1)
                    for k, (a, n) in enumerate(pieces + [(LEN_R, 512)]):
                        dve.tensor_copy(fr[0:N_HEADS, a:a + n], PS[0:N_HEADS, k + 1, 0:n]).then_inc(s_fr, 1)
                    dve.tensor_copy(fr[0:N_HEADS, LEN_R + 512:LEN_R + LEN_W], PS[0:N_HEADS, 0, 0:LEN_W - 512]).then_inc(s_ev, 1)
                    dve.wait_ge(s_mm, 2)
                    dve.tensor_copy(bias_cmp[:, :, :, :].rearrange("p i h o -> p i o h"),
                                    PS[:, 6, :].rearrange("p (i o h) -> p i o h", i=4, o=8)).then_inc(s_ev, 1)
                    dve.wait_ge(s_mm, 3)
                    dve.tensor_copy(gT[:, :], PS[:, 7, 0:64]).then_inc(s_dch, 1)
                    dve.tensor_copy(convT[:, :], PS[:, 7, 64:124]).then_inc(s_ev, 1)
                    u = 0
                    for i, (t0, n) in enumerate(TILES):
                        for q in range(2):
                            dve.wait_ge(s_mm, 4 + u)
                            dve.tensor_copy(xT[:, 4 * q:4 * q + 4, t0:t0 + n],
                                            PS[:, u % 2, :].rearrange("p (j n) -> p j n", j=4)[:, :, 0:n]).then_inc(s_ev, 1)
                            u += 1
                    dve.wait_ge(s_ev, 13)
                    for w in (G1POST, G2POST):
                        dve.wait_ge(s_dch, 2)
                        dve.tensor_scalar(gT[:, 8 * w:8 * w + 8], gT[:, 8 * w:8 * w + 8], 0.5, None, ALU.mult).then_inc(s_ev, 1)

        def compress_past():
            GP = 32
            wbd = at(0, P, 2, 64)
            pg = at(16384, GP + 1, 512)
            ck = at(16384 + (GP + 1) * 512, 2, N_KV, ALL_PAGES)
            ld_w, ld_p, s_z, mm, ev, s_t, s_k = (sem("cp_" + n) for n in ("w", "p", "z", "mm", "ev", "t", "k"))
            s_pe, s_added = sem("cp_pe"), sem("cp_added")
            kh = io["w_cmp"].rearrange("a l c d e -> (a l) (c d) e")
            with nc.Block() as block:
                @block.sync
                def _(sp):
                    with nc.allow_non_contiguous_dma(reason="rows of 256 bytes"):
                        sp.wait_ge(s_z, 2)
                        for q in range(4):
                            for half in range(2):
                                sp.dma_start(wbd[half * 64:half * 64 + 64, 32 * q:32 * q + 32, half, :],
                                             kh[:, 32 * q:32 * q + 32, :]).then_inc(ld_w, 16)
                    for half in range(2):
                        sp.dma_start(pg[half * 64:half * 64 + 64, GP, 0:P],
                                     io["cmp_pe"].rearrange("a l c d -> (a l) (c d)")).then_inc(s_pe, 16)
                    cache = io["cache_cmp_kv"].rearrange("a n p h c d -> (a n) p (h c d)")
                    for r in range(2):
                        if r:
                            sp.wait_ge(mm, 2 * r)
                        with sp.Fori(0, GP) as j:
                            page = sp.value_load(page_sb[0:1, bass.ds(r * GP + j, 1)], min_val=0, max_val=N_POOL - 1)
                            sp.dma_start(pg[:, bass.ds(j, 1), :].rearrange("p a n -> p (a n)"),
                                         cache[bass.ds(page, 1), :, :].rearrange("a p n -> (a p) n")).then_inc(ld_p, 16)
                    sp.wait_ge(ev, 4)
                    for half in range(2):
                        for odd in range(2):
                            sp.dma_start(kc_all[64 * odd:64 * odd + 64, :, half, :],
                                         ck[64 * half:64 * half + 64, 0, :, :].rearrange("p (a b) n -> p a b n", b=2)[:, :, odd, :]
                                         ).then_inc(s_k, 16)
                    sp.wait_ge(s_k, 64)

                @block.gpsimd
                def _(pool):
                    pool.memset(wbd[0:64, :, 1, :], 0.0).then_inc(s_z, 1)

                @block.tensor
                def _(pe):
                    pe.wait_ge(ld_w, 16 * 8)
                    pe.wait_ge(s_pe, 32)
                    with pe.Fori(0, 2) as r:
                        pe.wait_ge(ld_p, (r + 1) * (16 * GP))
                        pe.wait_ge(ev, r * 2)
                        for c in range(2):
                            for d in range(64):
                                rhs = bass.AP(pg.tensor, pg.offset + c * 64 + d, [pg.ap[0], [P, 4 * GP + 1]])
                                m = pe.matmul(PS[:, c, 0:4 * GP + 1], wbd[:, c * 64 + d, :, :].rearrange("p a b -> p (a b)"),
                                              rhs, start=(d == 0), stop=(d == 63))
                            m.then_inc(mm, 1)
                    pe.wait_ge(ev, 4)
                    for h in range(N_KV):
                        m = pe.transpose(PS[0:ALL_PAGES, 2, h * P:(h + 1) * P], ck[:, 1, h, :], ident)
                    m.then_inc(s_t, 1)

                @block.vector
                def _(dve):
                    dve.memset(wbd[64:P, :, 0, :], 0.0).then_inc(s_z, 1)
                    pe_done = s_added
                    with dve.Fori(0, 2) as r:
                        for c in range(2):
                            dve.wait_ge(mm, r * 2 + (c + 1))
                            dve.tensor_copy(pe_c[:, c:c + 1], PS[:, c, 4 * GP:4 * GP + 1]).then_inc(pe_done, 1)
                            dve.wait_ge(pe_done, r * 2 + (c + 1))
                            dst = ck[:, c, :, bass.ds(r * GP, GP)]
                            dve.tensor_scalar(dst, PS[:, c, 0:4 * GP].rearrange("p (n h) -> p h n", h=N_KV),
                                              pe_c[:, c:c + 1], None, ALU.add).then_inc(ev, 1)
                    dve.wait_ge(s_t, 1)
                    dve.tensor_copy(vc_all[:, :, :].rearrange("n a (h e) -> n h a e", h=N_KV),
                                    PS[0:ALL_PAGES, 2, :].rearrange("n (h a e) -> n h a e", h=N_KV, a=2)).then_inc(pe_done, 1)

        def norm_engines(tag, src, finish):
            s_sq, s_use, s_root, s_r = (sem(tag + n) for n in ("_sq", "_use", "_root", "_rstd"))

            def scalar(act):
                for k in range(KD):
                    if k >= 2:
                        act.wait_ge(s_use, k - 1)
                    act.activation(sqr[:, k % 2, :], src[:, k, :], ACT.Square, scale=D_MODEL ** -0.5).then_inc(s_sq, 1)
                act.wait_ge(s_use, KD)
                for a, b in ((rstd[:, 0:SEQ], PS[:, 6, :]), (rstd[:, SEQ:T], PS[:, 7, 0:NS])):
                    act.activation(a, b, ACT.Sqrt, bias=eps_sb[:, 0:1]).then_inc(s_root, 1)

            def tensor(pe):
                for k in range(KD):
                    pe.wait_ge(s_sq, k + 1)
                    pe.matmul(PS[:, 6, :], sq6[:, ONES, :], sqr[:, k % 2, 0:SEQ], start=(k == 0), stop=(k == KD - 1))
                    pe.matmul(PS[:, 7, 0:NS], sq6[:, ONES, :], sqr[:, k % 2, SEQ:T], start=(k == 0),
                              stop=(k == KD - 1)).then_inc(s_use, 1)

            def vector(dve):
                dve.wait_ge(s_root, 2)
                dve.reciprocal(rstd[:, :], rstd[:, :]).then_inc(s_r, 1)
                dve.wait_ge(s_r, 1)
                finish(dve)
            return scalar, tensor, vector

        def pre_norm(tag, gain, dst):
            def finish(dve):
                for k in range(KD):
                    dve.scalar_tensor_tensor(dst[:, k, :], xT[:, k, :], gT[:, 8 * gain + k:8 * gain + k + 1],
                                             rstd[:, :], ALU.mult, ALU.mult).then_inc(done, 1)
            done = sem(tag + "_xn")
            s, t, v = norm_engines(tag, xT, finish)
            with nc.Block() as block:
                block.scalar(s)
                block.tensor(t)
                block.vector(v)

        def post_norm(tag, gain, y):
            done, s_w = sem(tag + "_res"), sem(tag + "_w")

            def finish(dve):
                for k in range(KD):
                    dve.scalar_tensor_tensor(y[:, k, :], y[:, k, :], gT[:, 8 * gain + k:8 * gain + k + 1],
                                             rstd[:, :], ALU.mult, ALU.mult).then_inc(s_w, 1)
                for k in range(KD):
                    dve.wait_ge(s_w, k + 1)
                    dve.tensor_tensor(xT[:, k, :], xT[:, k, :], y[:, k, :], ALU.add).then_inc(done, 1)
            s, t, v = norm_engines(tag, y, finish)
            with nc.Block() as block:
                block.scalar(s)
                block.tensor(t)
                block.vector(v)

        def project_out(tag, w, kc, hT, y, off):
            slots = [at(off + s * kc * P, kc, P) for s in range(2)]
            land = [sem(f"{tag}_w{s}") for s in range(2)]
            mm = [sem(f"{tag}_mm{s}") for s in range(2)]
            ev = [sem(f"{tag}_ev{s}") for s in range(2)]
            wv = w.rearrange("(k p) n -> p k n", p=P)
            with nc.Block() as block:
                @block.sync
                def _(sp):
                    with sp.Fori(0, KD // 2) as i:
                        for s in range(2):
                            sp.wait_ge(mm[s], i)
                            sp.dma_start(slots[s], wv[:, :, bass.ds((2 * i + s) * P, P)]).then_inc(land[s], 16)

                @block.tensor
                def _(pe):
                    with pe.Fori(0, KD // 2) as i:
                        for s in range(2):
                            pe.wait_ge(land[s], (i + 1) * 16)
                            pe.wait_ge(ev[s], i)
                            for k in range(kc):
                                pe.matmul(PS[:, 2 * s, :], slots[s][:, k, :], hT[:, k, 0:SEQ], start=(k == 0), stop=(k == kc - 1))
                                m = pe.matmul(PS[:, 2 * s + 1, 0:NS], slots[s][:, k, :], hT[:, k, SEQ:T],
                                              start=(k == 0), stop=(k == kc - 1))
                            m.then_inc(mm[s], 1)

                @block.vector
                def _(dve):
                    with dve.Fori(0, KD // 2) as i:
                        for s in range(2):
                            dve.wait_ge(mm[s], i + 1)
                            row = y[:, bass.ds(2 * i + s, 1), :].rearrange("p a n -> p (a n)")
                            dve.tensor_copy(row[:, 0:SEQ], PS[:, 2 * s, :])
                            dve.tensor_copy(row[:, SEQ:T], PS[:, 2 * s + 1, 0:NS]).then_inc(ev[s], 1)

        def ffn(tag, w_in, w_out, pre, post):
            xn = at(0, KD, T)
            hT = at(KD * T, KF, T)
            o = KD * T + KF * T
            slots = [at(o + s * 2 * KD * P, 2, KD, P) for s in range(2)]
            silu = [at(o + 4 * KD * P + s * T, T) for s in range(2)]
            pre_norm(tag + "_pre", pre, xn)
            land = [sem(f"{tag}_w{s}") for s in range(2)]
            mm = [sem(f"{tag}_mm{s}") for s in range(2)]
            act_done = [sem(f"{tag}_silu{s}") for s in range(2)]
            ev = [sem(f"{tag}_h{s}") for s in range(2)]
            wv = w_in.rearrange("(k p) n -> p k n", p=P)
            with nc.Block() as block:
                @block.sync
                def _(sp):
                    with sp.Fori(0, KF // 2) as i:
                        for s in range(2):
                            sp.wait_ge(mm[s], i)
                            for side in range(2):
                                sp.dma_start(slots[s][:, side, :, :],
                                             wv[:, :, bass.ds((2 * i + s) * P + side * D_FF, P)]).then_inc(land[s], 16)

                @block.tensor
                def _(pe):
                    with pe.Fori(0, KF // 2) as i:
                        for s in range(2):
                            pe.wait_ge(land[s], (i + 1) * 32)
                            pe.wait_ge(ev[s], i)
                            for side in range(2):
                                for k in range(KD):
                                    w = slots[s][:, side, k, :]
                                    pe.matmul(PS[:, 4 * s + 2 * side, :], w, xn[:, k, 0:SEQ], start=(k == 0), stop=(k == KD - 1))
                                    m = pe.matmul(PS[:, 4 * s + 2 * side + 1, 0:NS], w, xn[:, k, SEQ:T],
                                                  start=(k == 0), stop=(k == KD - 1))
                            m.then_inc(mm[s], 1)

                @block.scalar
                def _(act):
                    with act.Fori(0, KF // 2) as i:
                        for s in range(2):
                            act.wait_ge(mm[s], i + 1)
                            act.wait_ge(ev[s], i)
                            act.activation(silu[s][:, 0:SEQ], PS[:, 4 * s, :], ACT.Silu)
                            act.activation(silu[s][:, SEQ:T], PS[:, 4 * s + 1, 0:NS], ACT.Silu).then_inc(act_done[s], 1)

                @block.vector
                def _(dve):
                    with dve.Fori(0, KF // 2) as i:
                        for s in range(2):
                            dve.wait_ge(act_done[s], i + 1)
                            row = hT[:, bass.ds(2 * i + s, 1), :].rearrange("p a n -> p (a n)")
                            dve.tensor_tensor(row[:, 0:SEQ], silu[s][:, 0:SEQ], PS[:, 4 * s + 2, :], ALU.mult)
                            dve.tensor_tensor(row[:, SEQ:T], silu[s][:, SEQ:T], PS[:, 4 * s + 3, 0:NS], ALU.mult).then_inc(ev[s], 1)
            project_out(tag + "_out", w_out, KF, hT, xn, o)
            post_norm(tag + "_post", post, xn)

        O_OT = 0
        O_Q = O_OT + 16 * T
        O_NAT = O_Q + 8 * T
        O_SM = O_NAT + 3 * 5 * 512
        O_Z = O_SM + 5 * 64
        O_U = O_Z + 8 * T
        O_XP = O_U + KC_XBC * T
        O_END = O_XP + KC_XBC * XP
        oT, qT, nat, gdt = at(O_OT, 16, T), at(O_Q, 8, T), at(O_NAT, 3, 5, 512), at(O_SM, 5, 64)
        zT, uT, xp = at(O_Z, 8, T), at(O_U, KC_XBC, T), at(O_XP, KC_XBC, XP)
        w_in = io["w_in"].rearrange("a k n -> (a k) n").rearrange("(k p) n -> p k n", p=P)

        def mixer_in():
            xn = at(O_OT, KD, T)
            pre_norm("mix_pre", GMPRE, xn)
            kvw = [at(O_U, KD, 512), at(O_Z, KD, 512)]
            smw = at(O_XP, KD, 64)
            land = [sem(f"mk_w{s}") for s in range(2)]
            s_sw, mm, ev, s_st, s_mm2, s_ev2 = (sem("mk_" + n) for n in ("sw", "mm", "ev", "st", "mm2", "ev2"))
            with nc.Block() as block:
                @block.sync
                def _(sp):
                    with nc.allow_non_contiguous_dma(reason="the narrow columns of gates and dt"):
                        sp.dma_start(smw[:, :, 0:48], w_in[:, :, COL_GATES:COL_GATES + 48]).then_inc(s_sw, 16)
                        sp.dma_start(smw[:, :, 48:64], w_in[:, :, COL_DT:COL_DT + 16]).then_inc(s_sw, 16)
                    for br in range(3):
                        if br == 2:
                            sp.wait_ge(mm, 5)
                        c0 = COL_KV + br * 512
                        sp.dma_start(kvw[br % 2], w_in[:, :, c0:c0 + 512]).then_inc(land[br % 2], 16)
                    for br in range(3):
                        sp.wait_ge(ev, 5 * br + 5)
                        pdst = [out["p_cmp_kv"], out["p_slc_kv"], out["p_win_kv"]][br]
                        sp.dma_start(pdst.rearrange("a b (i p) h c d -> p (a b i) (h c d)", p=P), nat[:, br, 0:4, :]).then_inc(s_out, 16)
                        if br < 2:
                            sdst = [out["s_cmp_kv"], out["s_slc_kv"]][br]
                            sp.dma_start(sdst.rearrange("a b t h c d -> (a b t) (h c d)"), nat[0:NS, br, 4, :]).then_inc(s_out, 16)
                        else:
                            for b in range(DEC_BATCH):
                                sp.dma_start(out["s_win_kv"][0, b, WINDOW - DEC_SEQ:WINDOW].rearrange("t h c d -> t (h c d)"),
                                               nat[b * 8:b * 8 + 8, 2, 4, :]).then_inc(s_out, 16)
                    sp.dma_start(out["s_win_kv"][0, :, 0:WINDOW - DEC_SEQ].rearrange("b t h c d -> b t (h c d)"),
                                   io["cache_win_kv"][0, :, DEC_SEQ:WINDOW].rearrange("b t h c d -> b t (h c d)")).then_inc(s_out, 16)
                    outs[0] += 3 + 2 + 8 + 1

                @block.tensor
                def _(pe):
                    pe.wait_ge(s_sw, 32)
                    for i, (t0, n) in enumerate(TILES):
                        for k in range(KD):
                            m = pe.matmul(PS[0:n, 6, i * 64:(i + 1) * 64], xn[:, k, t0:t0 + n], smw[:, k, :],
                                          start=(k == 0), stop=(k == KD - 1))
                    m.then_inc(s_mm2, 1)
                    u = 0
                    for br in range(3):
                        pe.wait_ge(land[br % 2], 16 * (br // 2 + 1))
                        for i, (t0, n) in enumerate(TILES):
                            if u >= 4:
                                pe.wait_ge(ev, u - 3)
                            for k in range(KD):
                                m = pe.matmul(PS[0:n, u % 4, :], xn[:, k, t0:t0 + n], kvw[br % 2][:, k, :],
                                              start=(k == 0), stop=(k == KD - 1))
                            m.then_inc(mm, 1)
                            u += 1

                @block.scalar
                def _(act):
                    u = 0
                    for br in range(3):
                        for i, (t0, n) in enumerate(TILES):
                            act.wait_ge(mm, u + 1)
                            act.copy(nat[0:n, br, i, :], PS[0:n, u % 4, :]).then_inc(ev, 1)
                            u += 1

                @block.vector
                def _(dve):
                    dve.wait_ge(s_mm2, 1)
                    dve.tensor_copy(gdt[:, 0:4, :], PS[:, 6, 0:256].rearrange("p (i n) -> p i n", i=4)).then_inc(s_ev2, 1)
                    dve.tensor_copy(gdt[0:NS, 4, :], PS[0:NS, 6, 256:320]).then_inc(s_ev2, 1)

            slots = [at(O_OT + KD * T + s * KD * P, KD, P) for s in range(4)]
            land = [sem(f"mq_w{s}") for s in range(4)]
            mm = [sem(f"mq_mm{s}") for s in range(4)]
            ev = [sem(f"mq_ev{s}") for s in range(4)]
            s_pad, s_in = sem("mq_pad"), sem("mq_in")
            stn = at(O_END, CONV_DIM)[0:24, :]
            s_tt, s_tc = sem("mq_tt"), sem("mq_tc")
            with nc.Block() as block:
                @block.sync
                def _(sp):
                    sp.dma_start(stn, io["state_conv"].rearrange("a b w n -> (a b w) n")).then_inc(s_in, 16)
                    with nc.allow_non_contiguous_dma(reason="rows of 256 bytes"):
                        with sp.Fori(0, GQA) as g:
                            for pair in range(2):
                                sp.wait_ge(mm[pair], g)
                                for e in range(2):
                                    sp.dma_start(slots[pair][:, :, 64 * e:64 * e + 64],
                                                 w_in[:, :, bass.ds((8 * pair + 4 * e + g) * 64, 64)]).then_inc(land[pair], 16)
                    with sp.Fori(0, 10) as i:
                        for s in range(2):
                            sp.wait_ge(mm[2 + s], i)
                            sp.dma_start(slots[2 + s], w_in[:, :, bass.ds(COL_Z + (2 * i + s) * P, P)]).then_inc(land[2 + s], 16)

                @block.tensor
                def _(pe):
                    pe.wait_ge(s_in, 16)
                    for k in range(KC_XBC):
                        m = pe.transpose(PS[:, 7, k * 24:(k + 1) * 24], stn[:, k * P:(k + 1) * P], ident[0:24, 0:24])
                    m.then_inc(s_tt, 1)

                    def chunk(s, i, per):
                        pe.wait_ge(land[s], (i + 1) * per)
                        pe.wait_ge(ev[s], i)
                        b = 2 * (s % 2)
                        for k in range(KD):
                            pe.matmul(PS[:, b, :], slots[s][:, k, :], xn[:, k, 0:SEQ], start=(k == 0), stop=(k == KD - 1))
                            m = pe.matmul(PS[:, b + 1, 0:NS], slots[s][:, k, :], xn[:, k, SEQ:T], start=(k == 0), stop=(k == KD - 1))
                        m.then_inc(mm[s], 1)
                    with pe.Fori(0, GQA) as g:
                        for s in range(2):
                            chunk(s, g, 32)
                    for s in range(2):
                        pe.wait_ge(ev[s], GQA)
                    with pe.Fori(0, 10) as i:
                        for s in range(2):
                            chunk(2 + s, i, 16)

                @block.vector
                def _(dve):
                    dve.memset(xp[:, :, 0:PAD], 0.0).then_inc(s_pad, 1)
                    dve.wait_ge(s_tt, 1)
                    runs = xp[:, :, XP_S:XP].rearrange("p k (b r) -> p k b r", r=XP_RUN)
                    for k in range(KC_XBC):
                        dve.tensor_copy(runs[:, k, :, 0:PAD],
                                        PS[:, 7, k * 24:(k + 1) * 24].rearrange("p (b w) -> p b w", w=PAD)).then_inc(s_tc, 1)
                    with dve.Fori(0, GQA) as g:
                        for s in range(2):
                            dve.wait_ge(mm[s], g + 1)
                            row = qT[:, bass.ds(4 * s + g, 1), :].rearrange("p a n -> p (a n)")
                            dve.tensor_scalar(row[:, 0:SEQ], PS[:, 2 * s, :], SCALE, None, ALU.mult)
                            dve.tensor_scalar(row[:, SEQ:T], PS[:, 2 * s + 1, 0:NS], SCALE, None, ALU.mult).then_inc(ev[s], 1)
                    with dve.Fori(0, 4) as i:
                        for s in range(2):
                            dve.wait_ge(mm[2 + s], i + 1)
                            row = zT[:, bass.ds(2 * i + s, 1), :].rearrange("p a n -> p (a n)")
                            dve.tensor_copy(row[:, 0:SEQ], PS[:, 2 * s, :])
                            dve.tensor_copy(row[:, SEQ:T], PS[:, 2 * s + 1, 0:NS]).then_inc(ev[2 + s], 1)
                    with dve.Fori(0, 6) as i:
                        for s in range(2):
                            dve.wait_ge(mm[2 + s], i + 5)
                            row = xp[:, bass.ds(2 * i + s, 1), :].rearrange("p a n -> p (a n)")
                            dve.tensor_copy(row[:, PAD:XP_S], PS[:, 2 * s, :])
                            dve.tensor_copy(row[:, XP_S:XP].rearrange("p (b r) -> p b r", r=XP_RUN)[:, :, PAD:XP_RUN],
                                            PS[:, 2 * s + 1, 0:NS].rearrange("p (b r) -> p b r", r=DEC_SEQ)).then_inc(ev[2 + s], 1)

        def finish_out():
            ynat = at(0, 5, D_MODEL)
            mm, ev = sem("fo_mm"), sem("fo_ev")
            with nc.Block() as block:
                @block.tensor
                def _(pe):
                    u = 0
                    for i, (t0, n) in enumerate(TILES):
                        for q in range(2):
                            if u >= 4:
                                pe.wait_ge(ev, u - 3)
                            for j in range(4):
                                m = pe.transpose(PS[0:n, u % 4, j * P:(j + 1) * P], xT[:, 4 * q + j, t0:t0 + n], ident)
                            m.then_inc(mm, 1)
                            u += 1

                @block.vector
                def _(dve):
                    u = 0
                    for i, (t0, n) in enumerate(TILES):
                        for q in range(2):
                            dve.wait_ge(mm, u + 1)
                            dve.tensor_copy(ynat[0:n, i, 512 * q:512 * q + 512], PS[0:n, u % 4, :]).then_inc(ev, 1)
                            u += 1

                @block.sync
                def _(sp):
                    for i in range(5):
                        sp.wait_ge(ev, 2 * i + 2)
                        if i < 4:
                            sp.dma_start(out["y_prompt"][0, i * P:(i + 1) * P, :], ynat[:, i, :]).then_inc(s_out, 16)
                        else:
                            sp.dma_start(out["y_sample"].rearrange("b t d -> (b t) d"), ynat[0:NS, 4, :]).then_inc(s_out, 16)
                        outs[0] += 1
                    sp.wait_ge(s_out, 16 * outs[0])

        s_out = sem("outputs", True)
        outs = [0]
        def conv():
            cv = [at(O_END, XP), at(O_END + XP, XP)]
            last = at(O_END + 2 * XP, KC_XBC, 27)
            rows = at(O_OT + 8 * T, CONV_DIM)[0:27, :]
            s_cv, s_u, s_last, s_t, s_row, s_z = (sem("cv_" + n) for n in ("taps", "silu", "last", "t", "row", "z"))
            with nc.Block() as block:
                @block.vector
                def _(dve):
                    n = 0
                    for k0 in range(0, KC_XBC, 2):
                        for w in range(CONV_W):
                            for j in range(2):
                                k = k0 + j
                                o = cv[j][:, 0:CONV_N]
                                tap = convT[:, w * KC_XBC + k:w * KC_XBC + k + 1]
                                if w == 0:
                                    if k >= 2:
                                        dve.wait_ge(s_u, k - 1)
                                    ins = dve.tensor_scalar(o, xp[:, k, 0:CONV_N], tap,
                                                            convT[:, 4 * KC_XBC + k:4 * KC_XBC + k + 1], ALU.mult, ALU.add)
                                else:
                                    dve.wait_ge(s_cv, n - 1)
                                    ins = dve.scalar_tensor_tensor(o, xp[:, k, w:w + CONV_N], tap, o, ALU.mult, ALU.add)
                                ins.then_inc(s_cv, 1)
                                n += 1
                    dve.wait_ge(s_t, 1)
                    for b in range(3):
                        dve.tensor_copy(rows[:, 512 * b:512 * b + 512], PS[0:27, b, :]).then_inc(s_row, 1)

                @block.scalar
                def _(act):
                    for k in range(KC_XBC):
                        act.wait_ge(s_cv, 8 * (k // 2) + 7 + k % 2)
                        c = cv[k % 2]
                        act.activation(uT[:, k, 0:SEQ], c[:, 0:SEQ], ACT.Silu)
                        act.activation(uT[:, k, SEQ:T].rearrange("p (b t) -> p b t", t=DEC_SEQ),
                                       c[:, XP_S:XP].rearrange("p (b r) -> p b r", r=XP_RUN)[:, :, 0:DEC_SEQ],
                                       ACT.Silu).then_inc(s_u, 1)
                    act.activation(zT[:, :, :], zT[:, :, :], ACT.Silu).then_inc(s_z, 1)

                @block.gpsimd
                def _(pool):
                    pool.tensor_copy(last[:, :, 0:PAD], xp[:, :, XP_S - PAD:XP_S]).then_inc(s_last, 1)
                    pool.tensor_copy(last[:, :, PAD:27].rearrange("p k (b w) -> p k b w", w=PAD),
                                     xp[:, :, XP_S:XP].rearrange("p k (b r) -> p k b r", r=XP_RUN)[:, :, :, DEC_SEQ:XP_RUN]
                                     ).then_inc(s_last, 1)

                @block.tensor
                def _(pe):
                    pe.wait_ge(s_last, 2)
                    for k in range(KC_XBC):
                        m = pe.transpose(PS[0:27, k // 4, (k % 4) * P:(k % 4 + 1) * P], last[:, k, :], ident)
                    m.then_inc(s_t, 1)

                @block.sync
                def _(sp):
                    sp.wait_ge(s_row, 3)
                    sp.dma_start(out["p_conv"].rearrange("a b w n -> (a b w) n"), rows[0:PAD, :]).then_inc(s_out, 16)
                    sp.dma_start(out["s_conv"].rearrange("a b w n -> (a b w) n"), rows[PAD:27, :]).then_inc(s_out, 16)
                    outs[0] += 2
                    sp.wait_ge(s_out, 16 * outs[0])

        def ssd():
            o = O_XP
            xdt = at(o, N_HEADS, HD)
            xe = at(o + 1024, N_HEADS, HD)
            larep = at(o + 2048, N_HEADS, HD)
            mb = [at(o + 3072, 4, P), at(o + 3584, 4, P)]
            ecs = at(o + 4096, 8, P)
            st = at(o + 5120, N_HEADS, HD)
            bnat = at(o + 6144, 2, P)
            cbm = at(o + 6400, 2, P)
            yt = at(o + 6656, 2, 512)
            bm = at(o + 7680, 2, 256)
            dtv = at(o + 8192, 7, 80)
            ted = at(o + 8752, 2, 16)
            nla = at(o + 8784, 80)
            h0 = [at(O_OT + 1024 * s, 8, P) for s in range(3)]
            h0t = at(O_OT + 3072, 8, P)
            names = ("dch", "ach", "la", "xs", "small", "cb", "cs", "diff", "yoff", "yd", "st", "lar", "xdt", "bn", "cbm",
                     "mn", "mm", "xe", "y", "sup", "te", "ecs", "ee", "h0t", "h0c", "new", "bmk", "hn",
                     "pst", "psc", "e", "l")
            S = {n: sem("ss_" + n) for n in names}
            s_h0 = [sem(f"ss_h0_{s}") for s in range(3)]
            s_ho = [sem(f"ss_ho_{s}") for s in range(3)]
            NC = len(TILES)
            states = io["state_ssm"].rearrange("a b (k e) p n -> (a b) (e p) k n", e=2)
            s_states = out["s_ssm"].rearrange("a b (k e) p n -> (a b) (e p) k n", e=2)

            with nc.Block() as block:
                @block.sync
                def _(sp):
                    for b in range(DEC_BATCH):
                        if b >= 3:
                            sp.wait_ge(s_ho[b % 3], 16 * (b // 3))
                        sp.dma_start(h0[b % 3], states[b]).then_inc(s_h0[b % 3], 16)
                        if b >= 1:
                            sp.wait_ge(S["hn"], b)
                            sp.dma_start(s_states[b - 1], h0[(b - 1) % 3]).then_inc(s_ho[(b - 1) % 3], 16)
                    sp.wait_ge(S["hn"], DEC_BATCH)
                    sp.dma_start(s_states[DEC_BATCH - 1], h0[(DEC_BATCH - 1) % 3]).then_inc(s_ho[(DEC_BATCH - 1) % 3], 16)
                    for s in range(3):
                        sp.wait_ge(s_ho[s], 16 * ((DEC_BATCH + 2 - s) // 3))
                    sp.wait_ge(S["psc"], 2)
                    sp.dma_start(out["p_ssm"][0, 0].rearrange("(k e) p n -> (e p) k n", e=2), h0[0]).then_inc(s_out, 16)
                    outs[0] += 1
                    sp.wait_ge(s_out, 16 * outs[0])

                @block.tensor
                def _(pe):
                    pe.wait_ge(S["la"], 2)
                    for c, (t0, n) in enumerate(TILES):
                        sample = c == NC - 1
                        tri = sq6[0:n, BTRI if sample else TRI, 0:n]
                        one = sq6[0:n, BONES if sample else ONES, 0:n]
                        la = dtv[0:n, 6, 16 * c:16 * c + 16]
                        if c:
                            pe.wait_ge(S["y"], 2 * c)
                            pe.wait_ge(S["sup"], 2 * c)
                        for k in range(8):
                            pe.transpose(PS[0:n, k // 4, (k % 4) * P:(k % 4 + 1) * P], uT[:, k, t0:t0 + n], ident)
                        for g in range(2):
                            m = pe.transpose(PS[0:n, 2, g * P:(g + 1) * P], uT[:, 8 + g, t0:t0 + n], ident)
                        m.then_inc(S["xs"], 1)
                        pe.matmul(PS[0:n, 2, 256:272], one, la, start=True, stop=True)
                        pe.matmul(PS[0:n, 2, 272:288], tri, la, start=True, stop=True).then_inc(S["small"], 1)
                        for g in range(2):
                            m = pe.matmul(PS[0:n, 3, g * P:g * P + n], uT[:, 8 + g, t0:t0 + n], uT[:, 10 + g, t0:t0 + n],
                                          start=True, stop=True)
                        m.then_inc(S["cb"], 1)
                        pe.wait_ge(S["lar"], c + 1)
                        for k in range(8):
                            if k % 4 == 0 and c:
                                pe.wait_ge(S["mn"], 4 * c - 1 + k // 4)
                            m = pe.matmul(PS[:, 4 + k // 4, (k % 4) * P:(k % 4) * P + n],
                                          larep[0:n, 2 * k:2 * k + 2, :].rearrange("p a b -> p (a b)"), tri, start=True, stop=True)
                            if k % 4 == 3:
                                m.then_inc(S["cs"], 1)
                        for q in range(4):
                            if q < 2:
                                pe.wait_ge(S["ecs"], 2 * c + q + 1)
                            else:
                                pe.wait_ge(S["mn"], 4 * c + q - 1)
                            bank = 4 + q % 2
                            for j in range(4):
                                pe.matmul(PS[0:n, bank, j * P:j * P + n], dtv[0:n, 6, 16 * c + 4 * q + j:16 * c + 4 * q + j + 1]
                                          .to_broadcast([n, n]), tri, start=True, stop=False)
                                m = pe.matmul(PS[0:n, bank, j * P:j * P + n], tri,
                                              nla[0:n, 16 * c + 4 * q + j:16 * c + 4 * q + j + 1].to_broadcast([n, n]),
                                              start=False, stop=True)
                            m.then_inc(S["diff"], 1)
                        if not sample:
                            pe.wait_ge(S["xdt"], c + 1)
                            if c == 0:
                                pe.wait_ge(S["e"], 1)
                            for k in range(8):
                                m = pe.matmul(PS[:, k // 4, (k % 4) * P:(k % 4) * P + n],
                                              st[:, 2 * k:2 * k + 2, :].rearrange("p a b -> p (a b)"),
                                              uT[:, 10 + k // 4, t0:t0 + n], start=True, stop=True)
                            m.then_inc(S["yoff"], 1)
                        pe.wait_ge(S["xdt"], c + 1)
                        for q in range(4):
                            pe.wait_ge(S["mm"], 4 * c + q + 1)
                            for j in range(4):
                                h = 4 * q + j
                                m = pe.matmul(PS[64 * (h % 2):64 * (h % 2) + 64, 6 + h // 8, (h // 2 % 4) * P:(h // 2 % 4) * P + n],
                                              xdt[0:n, h, :], mb[q % 2][0:n, j, 0:n], start=True, stop=True)
                            m.then_inc(S["yd"], 1)
                        pe.wait_ge(S["xe"], c + 1)
                        if not sample:
                            pe.wait_ge(S["bn"], c + 1)
                            pe.wait_ge(S["te"], c + 1)
                            pe.wait_ge(S["cbm"], c + 1)
                            for g in range(2):
                                m = pe.matmul(PS[:, 2 + g, :], bnat[0:n, g, :],
                                              xe[0:n, 8 * g:8 * g + 8, :].rearrange("p a b -> p (a b)"), start=True, stop=True)
                            m.then_inc(S["st"], 1)
                    n = NS
                    pe.wait_ge(S["cbm"], NC)
                    for b in range(DEC_BATCH):
                        pe.wait_ge(s_h0[b % 3], 16 * (b // 3 + 1))
                        if b == 0:
                            pe.wait_ge(S["mn"], 4 * NC)
                        else:
                            pe.wait_ge(S["h0c"], 2 * b)
                        for k in range(8):
                            m = pe.transpose(PS[:, 4 + k // 4, (k % 4) * P:(k % 4 + 1) * P], h0[b % 3][:, k, :], ident)
                        m.then_inc(S["h0t"], 1)
                        pe.wait_ge(S["bmk"], b + 1)
                        if b:
                            pe.wait_ge(S["hn"], b)
                        for k in range(8):
                            m = pe.matmul(PS[:, 2 + k // 4, (k % 4) * P:(k % 4 + 1) * P],
                                          xe[0:n, 2 * k:2 * k + 2, :].rearrange("p a b -> p (a b)"),
                                          bm[0:n, b % 2, (k // 4) * P:(k // 4 + 1) * P], start=True, stop=True)
                        m.then_inc(S["new"], 1)
                        pe.wait_ge(S["h0c"], 2 * b + 2)
                        for k in range(8):
                            m = pe.matmul(PS[:, k // 4, (k % 4) * P + 8 * b:(k % 4) * P + 8 * b + 8], h0t[:, k, :],
                                          uT[:, 10 + k // 4, SEQ + 8 * b:SEQ + 8 * b + 8], start=True, stop=True)
                        m.then_inc(S["yoff"], 1)
                    for k in range(8):
                        m = pe.transpose(PS[:, 4 + k // 4, (k % 4) * P:(k % 4 + 1) * P],
                                         st[:, 2 * k:2 * k + 2, :].rearrange("p a b -> p (a b)"), ident)
                    m.then_inc(S["pst"], 1)

                @block.scalar
                def _(act):
                    act.wait_ge(S["l"], 1)
                    act.activation(dtv[:, 2, :], dtv[:, 1, :], ACT.Exp, scale=-1.0).then_inc(S["ach"], 1)
                    act.wait_ge(S["l"], 2)
                    act.activation(dtv[:, 4, :], dtv[:, 3, :], ACT.Ln).then_inc(S["ach"], 1)
                    for c, (t0, n) in enumerate(TILES):
                        act.wait_ge(S["bn"], c + 1)
                        act.activation(ted[0:n, :, :], ted[0:n, :, :], ACT.Exp).then_inc(S["te"], 1)
                        for g in range(2):
                            act.wait_ge(S["cs"], 2 * c + g + 1)
                            act.activation(ecs[:, 4 * g:4 * g + 4, 0:n],
                                           PS[:, 4 + g, :].rearrange("p (a n) -> p a n", a=4)[:, :, 0:n], ACT.Exp).then_inc(S["ecs"], 1)
                        for q in range(4):
                            act.wait_ge(S["mn"], 4 * c + q + 1)
                            act.activation(mb[q % 2][0:n, :, 0:n], mb[q % 2][0:n, :, 0:n], ACT.Exp).then_inc(S["ee"], 1)
                    for b in range(DEC_BATCH):
                        act.wait_ge(S["h0t"], b + 1)
                        if b:
                            act.wait_ge(S["yoff"], NC - 1 + b)
                        for g in range(2):
                            act.copy(h0t[:, 4 * g:4 * g + 4, :].rearrange("p a b -> p (a b)"), PS[:, 4 + g, :]).then_inc(S["h0c"], 1)

                @block.vector
                def _(dve):
                    ch = Chain(dve, S["dch"])
                    sm = gdt[:, :, 48:64]
                    v = lambda k: dtv[:, k, :].rearrange("p (c h) -> p c h", c=NC)
                    ch.link(dve.memset(gdt[64:P, 4, :], 0.0))
                    dve.memset(st[:, :, :], 0.0).then_inc(S["e"], 1)
                    ch.link(dve.tensor_tensor(v(0), sm, small[:, 0:1, :].to_broadcast([P, NC, 16]), ALU.add))
                    dve.scalar_tensor_tensor(v(1), v(0), -1.0, v(0), ALU.mult, ALU.max).then_inc(S["l"], 1)
                    dve.wait_ge(S["ach"], 1)
                    dve.tensor_scalar(dtv[:, 3, :], dtv[:, 2, :], 1.0, None, ALU.add).then_inc(S["l"], 1)
                    dve.wait_ge(S["ach"], 2)
                    ch.link(dve.tensor_scalar(dtv[:, 1, :], dtv[:, 3, :], -1.0, None, ALU.add))
                    ch.link(dve.tensor_tensor(dtv[:, 4, :], dtv[:, 4, :], dtv[:, 2, :], ALU.mult))
                    ch.link(dve.scalar_tensor_tensor(dtv[:, 2, :], dtv[:, 1, :], 0.0, dtv[:, 2, :], ALU.is_equal, ALU.mult))
                    ch.link(dve.tensor_scalar(dtv[:, 1, :], dtv[:, 1, :], 1e-30, None, ALU.max))
                    ch.link(dve.reciprocal(dtv[:, 1, :], dtv[:, 1, :]))
                    ch.link(dve.tensor_tensor(dtv[:, 4, :], dtv[:, 4, :], dtv[:, 1, :], ALU.mult))
                    ch.link(dve.tensor_tensor(dtv[:, 4, :], dtv[:, 4, :], dtv[:, 2, :], ALU.add))
                    ch.link(dve.scalar_tensor_tensor(dtv[:, 5, :], dtv[:, 0, :], 0.0, dtv[:, 4, :], ALU.max, ALU.add))
                    dve.tensor_tensor(v(6), v(5), small[:, 2:3, :].to_broadcast([P, NC, 16]), ALU.mult).then_inc(S["la"], 1)
                    dve.wait_ge(S["la"], 1)
                    dve.tensor_scalar(nla[:, :], dtv[:, 6, :], -1.0, None, ALU.mult).then_inc(S["la"], 1)
                    for c, (t0, n) in enumerate(TILES):
                        sample = c == NC - 1
                        tri = sq6[0:n, BTRI if sample else TRI, 0:n]
                        dt = dtv[0:n, 5, 16 * c:16 * c + 16]
                        if c:
                            dve.wait_ge(S["cs"], 2 * c)
                        dve.tensor_copy(larep[0:n, :, :], dtv[0:n, 6, 16 * c:16 * c + 16].unsqueeze(2).to_broadcast([n, 16, 64])
                                        ).then_inc(S["lar"], 1)
                        dve.wait_ge(S["xs"], c + 1)
                        for g in range(2):
                            ins = dve.tensor_tensor(xdt[0:n, 8 * g:8 * g + 8, :], PS[0:n, g, :].rearrange("p (h d) -> p h d", d=HD),
                                                    dt[:, 8 * g:8 * g + 8].unsqueeze(2).to_broadcast([n, 8, 64]), ALU.mult)
                        ins.then_inc(S["xdt"], 1)
                        dve.wait_ge(S["small"], c + 1)
                        ch.link(dve.tensor_copy(bnat[0:n, :, :], PS[0:n, 2, 0:256].rearrange("p (g n) -> p g n", g=2)))
                        if c:
                            dve.wait_ge(S["sup"], 2 * c)
                        ch.link(dve.tensor_copy(ted[0:n, 0, :], PS[0:n, 2, 256:272]))
                        dve.tensor_tensor(ted[0:n, 1, :], ted[0:n, 0, :], PS[0:n, 2, 272:288], ALU.subtract).then_inc(S["bn"], 1)
                        dve.wait_ge(S["cb"], c + 1)
                        dve.tensor_tensor(cbm[0:n, :, 0:n], PS[0:n, 3, 0:256].rearrange("p (g n) -> p g n", g=2)[:, :, 0:n],
                                          tri.unsqueeze(1).to_broadcast([n, 2, n]), ALU.mult).then_inc(S["cbm"], 1)

                        def gate(q):
                            dve.wait_ge(S["ee"], 4 * c + q + 1)
                            dve.wait_ge(S["cbm"], c + 1)
                            dve.tensor_tensor(mb[q % 2][0:n, :, 0:n], mb[q % 2][0:n, :, 0:n],
                                              cbm[0:n, q // 2, 0:n].unsqueeze(1).to_broadcast([n, 4, n]), ALU.mult).then_inc(S["mm"], 1)
                        for q in range(4):
                            dve.wait_ge(S["diff"], 4 * c + q + 1)
                            if 4 * c + q >= 2:
                                dve.wait_ge(S["yd"], 4 * c + q - 1)
                            dve.tensor_scalar(mb[q % 2][0:n, :, 0:n],
                                              PS[0:n, 4 + q % 2, :].rearrange("p (a n) -> p a n", a=4)[:, :, 0:n],
                                              0.0, None, ALU.min).then_inc(S["mn"], 1)
                            if q:
                                gate(q - 1)
                        dve.wait_ge(S["te"], c + 1)
                        dve.wait_ge(S["xdt"], c + 1)
                        dve.tensor_tensor(xe[0:n, :, :], xdt[0:n, :, :], ted[0:n, 1, :].unsqueeze(2).to_broadcast([n, 16, 64]),
                                          ALU.mult).then_inc(S["xe"], 1)
                        gate(3)
                        if sample:
                            for b in range(DEC_BATCH):
                                if b >= 2:
                                    dve.wait_ge(S["new"], b - 1)
                                dve.tensor_scalar(bm[0:n, b % 2, :], bnat[0:n, :, :].rearrange("p a b -> p (a b)"),
                                                  crow[0:n, 2, b:b + 1], None, ALU.mult).then_inc(S["bmk"], 1)
                                dve.wait_ge(S["new"], b + 1)
                                dve.wait_ge(S["h0t"], b + 1)
                                dve.wait_ge(S["ecs"], 2 * NC)
                                for k in range(8):
                                    ins = dve.scalar_tensor_tensor(
                                        h0[b % 3][:, k, :], h0[b % 3][:, k, :], ecs[:, k, 8 * b + 7:8 * b + 8],
                                        PS[:, 2 + k // 4, (k % 4) * P:(k % 4 + 1) * P], ALU.mult, ALU.add)
                                ins.then_inc(S["hn"], 1)
                            dve.wait_ge(S["yoff"], NC - 1 + DEC_BATCH)
                        else:
                            dve.wait_ge(S["yoff"], c + 1)
                        for g in range(2):
                            dve.wait_ge(S["ecs"], 2 * c + g + 1)
                            yv = yt[:, g, :].rearrange("p (a n) -> p a n", a=4)[:, :, 0:n]
                            ch.link(dve.tensor_tensor(yv, PS[:, g, :].rearrange("p (a n) -> p a n", a=4)[:, :, 0:n],
                                                      ecs[:, 4 * g:4 * g + 4, 0:n], ALU.mult))
                            dve.wait_ge(S["yd"], 4 * c + 2 * g + 2)
                            ch.link(dve.tensor_tensor(yv, yv, PS[:, 6 + g, :].rearrange("p (a n) -> p a n", a=4)[:, :, 0:n], ALU.add))
                            for j in range(4):
                                k = 4 * g + j
                                ins = dve.scalar_tensor_tensor(oT[:, 8 + k, t0:t0 + n], uT[:, k, t0:t0 + n], small[:, 3, k:k + 1],
                                                               yv[:, j, :], ALU.mult, ALU.add)
                            ins.then_inc(S["y"], 1)
                        if not sample:
                            dve.wait_ge(S["te"], c + 1)
                            dve.wait_ge(S["e"], 1)
                            if c:
                                dve.wait_ge(S["sup"], 2 * c)
                            ch.link(dve.tensor_tensor(st[:, :, :], st[:, :, :], ted[:, 0, :].unsqueeze(2).to_broadcast([P, 16, 64]),
                                                      ALU.mult))
                            dve.wait_ge(S["st"], c + 1)
                            for g in range(2):
                                sv = st[:, 8 * g:8 * g + 8, :].rearrange("p a b -> p (a b)")
                                dve.tensor_tensor(sv, sv, PS[:, 2 + g, :], ALU.add).then_inc(S["sup"], 1)
                    dve.wait_ge(S["pst"], 1)
                    dve.wait_ge(s_ho[0], 16 * ((DEC_BATCH + 2) // 3))
                    for g in range(2):
                        dve.tensor_copy(h0[0][:, 4 * g:4 * g + 4, :].rearrange("p a b -> p (a b)"), PS[:, 4 + g, :]).then_inc(S["psc"], 1)

        def ssd_gate_norm():
            s_g, s_sq, s_use, s_root, s_r, s_f = (sem("sn_" + n) for n in ("g", "sq", "use", "root", "r", "f"))
            gs = [at(O_XP, T), at(O_XP + T, T)]
            with nc.Block() as block:
                @block.vector
                def _(dve):
                    for k in range(8):
                        dve.tensor_tensor(oT[:, 8 + k, :], oT[:, 8 + k, :], zT[:, k, :], ALU.mult).then_inc(s_g, 1)
                    for g in range(2):
                        dve.wait_ge(s_root, 2 * g + 2)
                        dve.reciprocal(gs[g], gs[g]).then_inc(s_r, 1)
                        dve.wait_ge(s_r, g + 1)
                        for k in range(4 * g, 4 * g + 4):
                            dve.scalar_tensor_tensor(oT[:, 8 + k, :], oT[:, 8 + k, :], gT[:, 8 * GSSD + k:8 * GSSD + k + 1],
                                                     gs[g], ALU.mult, ALU.mult).then_inc(s_f, 1)

                @block.scalar
                def _(act):
                    for k in range(8):
                        act.wait_ge(s_g, k + 1)
                        if k >= 2:
                            act.wait_ge(s_use, k - 1)
                        act.activation(sqr[:, k % 2, :], oT[:, 8 + k, :], ACT.Square,
                                       scale=(SSD_INNER // SSD_GROUPS) ** -0.5).then_inc(s_sq, 1)
                    for g in range(2):
                        act.wait_ge(s_use, 4 * g + 4)
                        act.activation(gs[g][:, 0:SEQ], PS[:, 2 * g, :], ACT.Sqrt, bias=eps_sb[:, 0:1]).then_inc(s_root, 1)
                        act.activation(gs[g][:, SEQ:T], PS[:, 2 * g + 1, 0:NS], ACT.Sqrt, bias=eps_sb[:, 0:1]).then_inc(s_root, 1)

                @block.tensor
                def _(pe):
                    for k in range(8):
                        pe.wait_ge(s_sq, k + 1)
                        g = k // 4
                        pe.matmul(PS[:, 2 * g, :], sq6[:, ONES, :], sqr[:, k % 2, 0:SEQ], start=(k % 4 == 0), stop=(k % 4 == 3))
                        pe.matmul(PS[:, 2 * g + 1, 0:NS], sq6[:, ONES, :], sqr[:, k % 2, SEQ:T], start=(k % 4 == 0),
                                  stop=(k % 4 == 3)).then_inc(s_use, 1)

        O_ON = O_Z
        O_SG = O_ON + 5 * ATT_WIDTH
        O_KTN = O_SG + 5 * 48
        O_FREE = O_KTN + 256
        onat, sg, ktn = at(O_ON, 5, ATT_WIDTH), at(O_SG, 5, 48), at(O_KTN, 2, 2, NS)

        def kt_transposes(pe, bank, rows, row0=0):
            for h in range(N_KV):
                c0 = h * P - (HD if h % 2 else 0)
                m = pe.transpose(PS[:, bank, h * P:h * P + rows.shape[0]], rows[:, c0:c0 + P], ident[0:rows.shape[0], 0:rows.shape[0]])
            return m

        def kt_halves(bank, n):
            v = PS[:, bank, :].rearrange("p (a e n) -> p a e n", a=2, e=2)
            return v[0:64, :, 0, 0:n], v[64:P, :, 1, 0:n]

        def compress_prompt():
            o = O_FREE
            ktp = at(o, 2, 2, SEQ)
            o += 2048
            wc = [at(o + 2048 * s, 32, HD) for s in range(2)]
            ckp = at(o + 4096, 2, N_KV, 4)
            kcp = at(o + 5600, 2, 2, 8)
            vtmp = at(o + 4160, P)
            vbd = at(o + 4288, 16 * HD)
            sc = at(o + 5312, N_HEADS, 8)
            mx = at(o + 5440, 2, 16)
            pT = at(o + 5472, P)
            wl = [sem(f"pc_w{s}") for s in range(2)]
            names = ("mm", "ck", "kc", "t", "vt", "z", "vb", "kt", "ktc", "s", "x", "e", "p", "pt", "ptc", "o", "oc", "dch", "sg")
            S = {n: sem("pc_" + n) for n in names}
            w = io["w_cmp"].rearrange("a l c d e -> (a l) (c d) e")
            with nc.Block() as block:
                @block.sync
                def _(sp):
                    for q in range(4):
                        if q >= 2:
                            sp.wait_ge(S["mm"], q - 1)
                        for half in range(2):
                            sp.dma_start(wc[q % 2][64 * half:64 * half + 64, :, :], w[:, 32 * q:32 * q + 32, :]).then_inc(wl[q % 2], 16)
                    sp.wait_ge(S["ck"], 2)
                    sp.wait_ge(S["z"], 2)
                    for half in range(2):
                        for odd in range(2):
                            sp.dma_start(kcp[64 * odd:64 * odd + 64, :, odd, 4 * half:4 * half + 4],
                                         ckp[64 * half:64 * half + 64, 0, :, :].rearrange("p (a b) n -> p a b n", b=2)[:, :, odd, :]
                                         ).then_inc(S["kc"], 16)
                    sp.wait_ge(S["vt"], 1)
                    for h in range(N_HEADS):
                        for half in range(2):
                            sp.dma_start(vbd[8 * h + 4 * half:8 * h + 4 * half + 4, HD * h:HD * h + HD],
                                         vtmp[4 * (h // GQA):4 * (h // GQA) + 4, 64 * half:64 * half + 64]).then_inc(S["vb"], 16)

                @block.gpsimd
                def _(pool):
                    pool.memset(kcp[:, :, :, :], 0.0).then_inc(S["z"], 1)
                    pool.memset(vbd, 0.0).then_inc(S["z"], 1)

                @block.tensor
                def _(pe):
                    u = 0
                    for br in range(2):
                        for i, (t0, n) in enumerate(TILES):
                            if u >= 2:
                                pe.wait_ge(S["ktc"], 2 * (u - 1))
                            kt_transposes(pe, 4 + u % 2, nat[0:n, 1 + br, i, :]).then_inc(S["kt"], 1)
                            u += 1
                    for q in range(4):
                        pe.wait_ge(wl[q % 2], 32 * (q // 2 + 1))
                        for j in range(32):
                            c, d = (32 * q + j) // 64, (32 * q + j) % 64
                            for half in range(2):
                                base = nat[64 * half:64 * half + 64, 0, 0:4, :]
                                rhs = bass.AP(base.tensor, base.offset + c * 64 + d, [base.ap[0], [P, 16]])
                                m = pe.matmul(PS[64 * half:64 * half + 64, c, 0:16], wc[q % 2][64 * half:64 * half + 64, j, :], rhs,
                                              start=(d == 0), stop=(d == 63))
                        m.then_inc(S["mm"], 1)
                    pe.wait_ge(S["ck"], 2)
                    pe.transpose(PS[0:16, 2, 0:P], ckp[:, 1, :, :].rearrange("p a b -> p (a b)"), ident).then_inc(S["t"], 1)
                    pe.wait_ge(S["kc"], 64)
                    for i in range(4):
                        if i:
                            pe.wait_ge(S["x"], i)
                        sv = PS[:, 3, 0:P].rearrange("p (a e g n) -> p a e g n", a=2, e=2, g=GQA)
                        for c in range(8):
                            m = pe.matmul(sv[:, c // GQA, :, c % GQA, :], qT[:, c, i * P:(i + 1) * P], kcp[:, c // GQA, :, :],
                                          start=True, stop=True)
                        m.then_inc(S["s"], 1)
                        pe.wait_ge(S["p"], i + 1)
                        pe.transpose(PS[:, 2, 0:P], sc[:, :, :].rearrange("p a b -> p (a b)"), ident).then_inc(S["pt"], 1)
                        pe.wait_ge(S["ptc"], i + 1)
                        pe.wait_ge(S["vb"], 16 * 32)
                        if i == 0:
                            pe.wait_ge(S["ck"], 2)
                        else:
                            pe.wait_ge(S["oc"], 2 * i)
                        for g in range(2):
                            m = pe.matmul(PS[:, g, :], pT, vbd[:, 512 * g:512 * g + 512], start=True, stop=True)
                        m.then_inc(S["o"], 1)

                @block.scalar
                def _(act):
                    act.activation(sg[:, :, :], gdt[:, :, 0:48], ACT.Sigmoid).then_inc(S["sg"], 1)
                    u = 0
                    for br in range(2):
                        for i, (t0, n) in enumerate(TILES):
                            act.wait_ge(S["kt"], u + 1)
                            lo, hi = kt_halves(4 + u % 2, n)
                            dst = ktp[:, br, :, t0:t0 + n] if i < 4 else ktn[:, br, :, :]
                            act.copy(dst[0:64], lo).then_inc(S["ktc"], 1)
                            act.copy(dst[64:P], hi).then_inc(S["ktc"], 1)
                            u += 1
                    for i in range(4):
                        act.wait_ge(S["x"], i + 1)
                        act.activation(sc[:, :, :], sc[:, :, :], ACT.Exp).then_inc(S["e"], 1)
                        act.wait_ge(S["pt"], i + 1)
                        if i:
                            act.wait_ge(S["o"], i)
                        act.copy(pT, PS[:, 2, 0:P]).then_inc(S["ptc"], 1)
                        act.wait_ge(S["o"], i + 1)
                        for g in range(2):
                            act.copy(onat[:, i, 512 * g:512 * g + 512], PS[:, g, :]).then_inc(S["oc"], 1)

                @block.vector
                def _(dve):
                    ch = Chain(dve, S["dch"])
                    dve.wait_ge(S["mm"], 4)
                    for c in range(2):
                        dve.tensor_scalar(ckp[:, c, :, :], PS[:, c, 0:16].rearrange("p (n h) -> p h n", h=N_KV),
                                          pe_c[:, c:c + 1], None, ALU.add).then_inc(S["ck"], 1)
                    dve.wait_ge(S["t"], 1)
                    dve.tensor_copy(vtmp[0:16, :], PS[0:16, 2, 0:P]).then_inc(S["vt"], 1)
                    for i in range(4):
                        dve.wait_ge(S["s"], i + 1)
                        if i:
                            dve.wait_ge(S["pt"], i)
                        ch.link(dve.tensor_tensor(sc[:, :, :], PS[:, 3, 0:P].rearrange("p (h n) -> p h n", h=16), bias_cmp[:, i, :, :], ALU.add))
                        ch.link(dve.tensor_reduce(mx[:, 0, :], sc[:, :, :], AXX, ALU.max))
                        ch.link(dve.tensor_scalar(mx[:, 0, :], mx[:, 0, :], 0.1 * MASKED, None, ALU.max))
                        dve.tensor_tensor(sc[:, :, :], sc[:, :, :], mx[:, 0, :].unsqueeze(2).to_broadcast([P, 16, 8]),
                                          ALU.subtract).then_inc(S["x"], 1)
                        dve.wait_ge(S["e"], i + 1)
                        ch.link(dve.tensor_reduce(mx[:, 1, :], sc[:, :, :], AXX, ALU.add))
                        ch.link(dve.tensor_scalar(mx[:, 1, :], mx[:, 1, :], 1e-30, None, ALU.max))
                        ch.link(dve.reciprocal(mx[:, 1, :], mx[:, 1, :]))
                        dve.wait_ge(S["sg"], 1)
                        ch.link(dve.tensor_tensor(mx[:, 1, :], mx[:, 1, :], sg[:, i, :].rearrange("p (h r) -> p h r", r=3)[:, :, 0], ALU.mult))
                        dve.tensor_tensor(sc[:, :, :], sc[:, :, :], mx[:, 1, :].unsqueeze(2).to_broadcast([P, 16, 8]),
                                          ALU.mult).then_inc(S["p"], 1)

        def attend_prompt():
            o = O_FREE
            ktp = at(o, 2, 2, SEQ)
            o += 2048
            mh = at(o, N_KV, SEQ)
            qg = at(o + 2048, 2, SEQ)
            Sx = [at(o + 3072 + 512 * s, SEQ) for s in range(3)]
            PT = [at(o + 4608 + 512 * s, SEQ) for s in range(2)]
            st = at(o + 5632, 4, 4)
            spare = at(o + 5648, 1)
            units = [(kv, br, i) for kv in range(N_KV) for br in range(2) for i in range(4)]
            NU = len(units)
            names = ("qg", "s", "x", "nm", "e", "t", "pt", "o", "b", "d1", "d2", "d3")
            S = {n: sem("pa_" + n) for n in names}
            s_mh = [sem(f"pa_mh{kv}") for kv in range(N_KV)]
            with nc.Block() as block:
                @block.sync
                def _(sp):
                    for g in range(GQA):
                        for kv in range(N_KV):
                            if g:
                                sp.wait_ge(S["x"], NU * (g - 1) + 8 * (kv + 1))
                            sp.dma_start(mh[:, kv, :], bass.AP(scr_t, (4 * kv + g) * P * LEN_T + P - 1, [[LEN_T - 1, P], [1, SEQ]])
                                         ).then_inc(s_mh[kv], 16)

                @block.tensor
                def _(pe):
                    with pe.Fori(0, GQA) as g:
                        base = g * NU

                        def scores(u):
                            kv, br, i = units[u]
                            r, n = 64 * (kv % 2), (i + 1) * P
                            if u >= 2:
                                pe.wait_ge(S["x"], base + u - 1)
                            pe.matmul(PS[:, u % 2, 0:n], qg[r:r + 64, kv // 2, i * P:(i + 1) * P], ktp[r:r + 64, br, kv // 2, 0:n],
                                      start=True, stop=True).then_inc(S["s"], 1)

                        def values(u):
                            kv, br, i = units[u]
                            pe.wait_ge(S["pt"], base + u + 1)
                            if u >= 2:
                                pe.wait_ge(S["b"], base + u - 1)
                            for j in range(i + 1):
                                m = pe.matmul(PS[:, 4 + u % 2, 0:HD], PT[u % 2][:, j * P:(j + 1) * P],
                                              nat[:, 1 + br, j, kv * P + HD:(kv + 1) * P], start=(j == 0), stop=(j == i))
                            m.then_inc(S["o"], 1)
                        pe.wait_ge(S["qg"], g + 1)
                        scores(0)
                        for u in range(NU):
                            if u + 1 < NU:
                                scores(u + 1)
                            pe.wait_ge(S["e"], base + u + 1)
                            if u >= 2:
                                pe.wait_ge(S["pt"], base + u - 1)
                            for j in range(units[u][2] + 1):
                                m = pe.transpose(PS[:, 2 + u % 2, j * P:(j + 1) * P], Sx[u % 3][:, j * P:(j + 1) * P], ident)
                            m.then_inc(S["t"], 1)
                            if u:
                                values(u - 1)
                        values(NU - 1)

                @block.scalar
                def _(act):
                    with act.Fori(0, GQA) as g:
                        base = g * NU

                        def to_sbuf(u):
                            n = (units[u][2] + 1) * P
                            act.wait_ge(S["t"], base + u + 1)
                            if u >= 2:
                                act.wait_ge(S["o"], base + u - 1)
                            act.copy(PT[u % 2][:, 0:n], PS[:, 2 + u % 2, 0:n]).then_inc(S["pt"], 1)
                        for u in range(NU):
                            n = (units[u][2] + 1) * P
                            act.wait_ge(S["nm"], base + u + 1)
                            act.activation(Sx[u % 3][:, 0:n], Sx[u % 3][:, 0:n], ACT.Exp, bias=st[:, u % 4, 1:2],
                                           accum_out=st[:, u % 4, 2:3]).then_inc(S["e"], 1)
                            if u:
                                to_sbuf(u - 1)
                        to_sbuf(NU - 1)

                @block.vector
                def _(dve):
                    with dve.Fori(0, GQA) as g:
                        base = g * NU
                        dve.wait_ge(S["b"], base)
                        for pair in range(2):
                            ins = dve.tensor_copy(qg[:, pair, :], qT[:, bass.ds(4 * pair + g, 1), 0:SEQ].rearrange("p a n -> p (a n)"))
                        ins.then_inc(S["qg"], 1)

                        def invert(u):
                            dve.wait_ge(S["e"], base + u + 1)
                            dve.reciprocal(st[:, u % 4, 3:4], st[:, u % 4, 2:3]).then_inc(S["d1"], 1)

                        def finish(u):
                            kv, br, i = units[u]
                            dve.wait_ge(S["d1"], base + u + 1)
                            dve.tensor_tensor(st[:, u % 4, 3:4], st[:, u % 4, 3:4],
                                              sg[:, i, bass.ds((4 * kv + g) * 3 + 1 + br, 1)], ALU.mult).then_inc(S["d2"], 1)
                            dve.wait_ge(S["d2"], base + u + 1)
                            dve.wait_ge(S["o"], base + u + 1)
                            dst = onat[:, i, bass.ds((4 * kv + g) * HD, HD)]
                            dve.scalar_tensor_tensor(dst, PS[:, 4 + u % 2, 0:HD], st[:, u % 4, 3:4], dst, ALU.mult, ALU.add
                                                     ).then_inc(S["b"], 1)
                        for u in range(NU):
                            kv, br, i = units[u]
                            n = (i + 1) * P
                            dve.wait_ge(s_mh[kv], (g + 1) * 16)
                            dve.wait_ge(S["s"], base + u + 1)
                            if u >= 2:
                                invert(u - 2)
                            else:
                                dve.memset(spare, 0.0)
                            dve.tensor_tensor_reduce(Sx[u % 3][:, 0:n], PS[:, u % 2, 0:n], mh[:, kv, SEQ - n:SEQ], 1.0, 3.0 * MASKED,
                                                     ALU.add, ALU.max, st[:, u % 4, 0:1]).then_inc(S["x"], 1)
                            if u >= 2:
                                finish(u - 2)
                            dve.wait_ge(S["x"], base + u + 1)
                            dve.tensor_scalar(st[:, u % 4, 1:2], st[:, u % 4, 0:1], -1.0, None, ALU.mult).then_inc(S["nm"], 1)
                        for u in (NU - 2, NU - 1):
                            invert(u)
                            finish(u)

        def attend_sample():
            o = O_FREE
            qbd = at(o, DEC_BATCH, 2, P)
            kt = at(o + 2048, 2, PAST_LEN)
            ktw = at(o + 4096, 2, WINDOW)
            Ss = at(o + 5120, PAST_LEN + NS)
            Sw = at(o + 6208, WINDOW + NS)
            bs = at(o + 6784, PAST_LEN)
            bw = at(o + 7808, WINDOW)
            bn = at(o + 8320, 120)
            cb = at(o + 8440, 2, 120)
            pc = at(o + 8680, 2, ALL_PAGES)
            pcT = at(o + 8808, 2, P)
            PTs = at(o + 9064, 9, P)
            PTw = at(o + 10216, 5, P)
            osb = at(o + 10856, 3, HD)
            qb = at(o + 11048, 2, P)
            pgw0 = at(o + 11304, 4, 512)
            st = at(o + 13352, 24)
            sel = at(o + 13376, 4, 16)
            pgs = [at(O_OT, PAGES, 512), at(O_NAT, PAGES, 512)]
            pgw = [pgw0, at(O_NAT + 2 * 5 * 512, 4, 512)]
            names = ("bias", "z", "fill", "qbd", "cbz", "qb", "cs", "nmc", "ec", "pn", "pct", "pctc", "kt", "ktc", "ss", "sw",
                     "nms", "nmw", "es", "ew", "tp", "tpc", "ov", "osc", "og", "dch")
            S = {n: sem("sa_" + n) for n in names}
            lp = [sem(f"sa_pg{s}") for s in range(2)]
            lw = [sem(f"sa_pw{s}") for s in range(2)]
            cache = io["cache_slc_kv"].rearrange("a n p h c d -> (a n) p (h c d)")
            win = io["cache_win_kv"].rearrange("a b (i p) h c d -> (a b) p i (h c d)", p=P)

            with nc.Block() as block:
                @block.sync
                def _(sp):
                    with nc.allow_non_contiguous_dma(reason="strided biases of the compressed blocks"):
                        sp.dma_start(bs, bass.AP(scr_r, TOP_R - PAST_LEN, [[LEN_R, N_HEADS], [-1, DEC_SEQ], [1, PAST_LEN]])).then_inc(S["bias"], 16)
                        sp.dma_start(bw, bass.AP(scr_w, TOP_W - WINDOW, [[LEN_W, N_HEADS], [-1, DEC_SEQ], [1, WINDOW]])).then_inc(S["bias"], 16)
                        sp.wait_ge(S["fill"], 2)
                        sp.dma_start(bn[:, 56:64], bass.AP(scr_r, TOP_R, [[LEN_R, N_HEADS], [-1, DEC_SEQ], [1, DEC_SEQ]])).then_inc(S["bias"], 16)
                    def load(s, b):
                        for j in range(PAGES):
                            page = sp.value_load(page_sb[0:1, bass.ds(b * PAGES + j, 1)], min_val=0, max_val=N_POOL - 1)
                            sp.dma_start(pgs[s][:, j, :], cache[bass.ds(page, 1), :, :].rearrange("a p n -> (a p) n")).then_inc(lp[s], 16)
                        sp.dma_start(pgw[s], win[bass.ds(b, 1), :, :, :].rearrange("a p i n -> (a p) i n")).then_inc(lw[s], 16)
                    for s in range(2):
                        load(s, s)
                    with sp.Fori(0, DEC_BATCH // 2 - 1) as i:
                        for s in range(2):
                            sp.wait_ge(S["ov"], i * 2 + (s + 1))
                            load(s, i * 2 + (s + 2))

                @block.gpsimd
                def _(pool):
                    pool.memset(qbd[:, :, :, :], 0.0).then_inc(S["z"], 1)
                    for b in range(DEC_BATCH):
                        pool.wait_ge(S["osc"], b + 1)
                        for br in range(3):
                            pool.dma_start(bass.AP(scr_o, (br * NS + b * DEC_SEQ) * ATT_WIDTH,
                                                   [[HD, N_HEADS], [ATT_WIDTH, DEC_SEQ], [1, HD]]), osb[:, br, :]).then_inc(S["og"], 16)
                    pool.wait_ge(S["og"], 16 * 3 * DEC_BATCH)


                @block.tensor
                def _(pe):
                    pe.wait_ge(S["z"], 1)
                    with pe.Fori(0, DEC_BATCH // 2) as i:
                        for s in range(2):
                            b2 = i * 2
                            pe.wait_ge(S["qb"], b2 + (s + 1))
                            for p in range(2):
                                m = pe.matmul(PS[:, 0, 0:P], qb[:, p, :], kc_all[:, p, :, :].rearrange("p a b -> p (a b)"),
                                              start=(p == 0), stop=(p == 1))
                            m.then_inc(S["cs"], 1)
                            for j in range(12):
                                if j == 0:
                                    pe.wait_ge(lp[s], (i + 1) * (16 * PAGES))
                                if j == 8:
                                    pe.wait_ge(lw[s], (i + 1) * 16)
                                if j < 2:
                                    if j == 0:
                                        pe.wait_ge(S["tpc"], i * 8 + 4 * s)
                                else:
                                    pe.wait_ge(S["ktc"], b2 * 24 + (24 * s + 2 * (j - 1)))
                                src = pgs[s][:, j, :] if j < 8 else pgw[s][:, j - 8, :]
                                kt_transposes(pe, 2 + j % 2, src).then_inc(S["kt"], 1)
                            pe.wait_ge(S["ktc"], b2 * 24 + (24 * s + 16))
                            for half in range(2):
                                for p in range(2):
                                    pe.matmul(PS[:, 4 + half, :], qb[:, p, :], kt[:, p, 512 * half:512 * half + 512], start=(p == 0), stop=(p == 1))
                            pe.wait_ge(S["nmc"], b2 + (s + 1))
                            for p in range(2):
                                m = pe.matmul(PS[:, 0, P:P + NS], qb[:, p, :], ktn[:, 0, p, :], start=(p == 0), stop=(p == 1))
                            m.then_inc(S["ss"], 1)
                            pe.wait_ge(S["ktc"], b2 * 24 + (24 * s + 24))
                            pe.wait_ge(S["osc"], b2 + s)
                            for p in range(2):
                                pe.matmul(PS[:, 6, :], qb[:, p, :], ktw[:, p, :], start=(p == 0), stop=(p == 1))
                            for p in range(2):
                                m = pe.matmul(PS[:, 0, P + NS:P + 2 * NS], qb[:, p, :], ktn[:, 1, p, :], start=(p == 0), stop=(p == 1))
                            m.then_inc(S["sw"], 1)
                            pe.wait_ge(S["pn"], b2 + (s + 1))
                            pe.matmul(PS[:, 1, 0:16], sq6[:, GROUP, :], pc[:, :, bass.ds(b2 * 8 + 8 * s, 8)], start=True, stop=True)
                            for half in range(2):
                                m = pe.transpose(PS[0:64, 1, P + half * P:2 * P + half * P], pc[:, half, :], ident)
                            m.then_inc(S["pct"], 1)
                            pe.wait_ge(S["pctc"], b2 + (s + 1))
                            for half in range(2):
                                m = pe.matmul(PS[:, 7, 0:256], pcT[0:64, half, :], vc_all[:, half, :], start=(half == 0), stop=(half == 1))
                            pe.wait_ge(S["ew"], b2 + (s + 1))
                            pe.wait_ge(S["es"], b2 + (s + 1))
                            for j in range(4):
                                m = pe.transpose(PS[:, 2, j * P:(j + 1) * P], Sw[:, j * P:(j + 1) * P], ident)
                            m.then_inc(S["tp"], 1)
                            pe.transpose(PS[0:64, 3, 0:P], Sw[:, 512:576], ident)
                            pe.transpose(PS[0:64, 3, P:2 * P], Ss[:, 1024:1088], ident).then_inc(S["tp"], 1)
                            for half in range(2):
                                pe.wait_ge(S["tpc"], i * 8 + (4 * s + half + 1))
                                for j in range(4):
                                    c0 = 512 * half + j * P
                                    m = pe.transpose(PS[:, 2 + half, j * P:(j + 1) * P], Ss[:, c0:c0 + P], ident)
                                m.then_inc(S["tp"], 1)
                            vcols = lambda rows: rows.rearrange("p (h c d) -> p h c d", h=N_KV, c=2)[:, :, 1, :]
                            for j in range(5):
                                v = vcols(pgw[s][:, j, :]) if j < 4 else vcols(nat[0:NS, 2, 4, :])
                                pr = PTw[:, j, :] if j < 4 else PTw[0:NS, 4, :]
                                pe.matmul(PS[:, 6, 0:256], pr, v, start=(j == 0), stop=(j == 4))
                            pe.wait_ge(S["tpc"], i * 8 + (4 * s + 4))
                            for j in range(9):
                                v = vcols(pgs[s][:, j, :]) if j < 8 else vcols(nat[0:NS, 1, 4, :])
                                pr = PTs[:, j, :] if j < 8 else PTs[0:NS, 8, :]
                                m = pe.matmul(PS[:, 7, 256:512], pr, v, start=(j == 0), stop=(j == 8))
                            m.then_inc(S["ov"], 1)

                @block.scalar
                def _(act):
                    act.wait_ge(S["z"], 1)
                    with act.Fori(0, DEC_BATCH // 2) as i:
                        for s in range(2):
                            b2 = i * 2
                            act.wait_ge(S["nmc"], b2 + (s + 1))
                            act.activation(pc[:, :, :], pc[:, :, :], ACT.Exp, bias=st[:, 1:2], accum_out=st[:, 2:3]).then_inc(S["ec"], 1)
                            for j in range(12):
                                act.wait_ge(S["kt"], i * 24 + (12 * s + j + 1))
                                lo, hi = kt_halves(2 + j % 2, P)
                                dst = kt[:, :, j * P:(j + 1) * P] if j < 8 else ktw[:, :, (j - 8) * P:(j - 7) * P]
                                act.copy(dst[0:64], lo).then_inc(S["ktc"], 1)
                                act.copy(dst[64:P], hi).then_inc(S["ktc"], 1)
                            act.wait_ge(S["nmw"], b2 + (s + 1))
                            act.activation(Sw, Sw, ACT.Exp, bias=st[:, 5:6], accum_out=st[:, 6:7]).then_inc(S["ew"], 1)
                            act.wait_ge(S["nms"], b2 + (s + 1))
                            act.activation(Ss, Ss, ACT.Exp, bias=st[:, 9:10], accum_out=st[:, 10:11]).then_inc(S["es"], 1)
                            act.wait_ge(S["tp"], i * 8 + (4 * s + 1))
                            act.copy(PTw[:, 0:4, :].rearrange("p a n -> p (a n)"), PS[:, 2, :]).then_inc(S["tpc"], 1)
                            act.wait_ge(S["tp"], i * 8 + (4 * s + 2))
                            act.copy(PTw[0:NS, 4, :], PS[0:NS, 3, 0:P])
                            act.copy(PTs[0:NS, 8, :], PS[0:NS, 3, P:2 * P]).then_inc(S["tpc"], 1)
                            for half in range(2):
                                act.wait_ge(S["tp"], i * 8 + (4 * s + 3 + half))
                                act.copy(PTs[:, 4 * half:4 * half + 4, :].rearrange("p a n -> p (a n)"), PS[:, 2 + half, :]).then_inc(S["tpc"], 1)

                @block.vector
                def _(dve):
                    ch = Chain(dve, S["dch"])
                    dve.memset(bn, MASKED).then_inc(S["fill"], 1)
                    dve.memset(cb[:, :, :], MASKED).then_inc(S["fill"], 1)
                    dve.wait_ge(S["z"], 1)
                    for p in range(2):
                        for e in range(2):
                            src = qT[64 * e:64 * e + 64, 4 * p:4 * p + 4, SEQ:T].rearrange("p g (b t) -> p g b t", t=DEC_SEQ)
                            c0 = (2 * p + e) * 32
                            dst = qbd[64 * e:64 * e + 64, :, p, c0:c0 + 32].rearrange("p b (g t) -> p g b t", t=DEC_SEQ)
                            for g in range(GQA):
                                ins = dve.tensor_copy(dst[:, g], src[:, g])
                    ins.then_inc(S["qbd"], 1)
                    dve.wait_ge(S["qbd"], 1)
                    dve.wait_ge(S["bias"], 16 * 3)
                    ends = bs.rearrange("p (g a l) -> p a g l", a=2, l=BLK)[:, :, :, BLK - 1]
                    dve.tensor_copy(cb[:, :, 56:64], ends).then_inc(S["cbz"], 1)
                    dve.wait_ge(S["cbz"], 1)
                    PER = 40
                    with dve.Fori(0, DEC_BATCH // 2) as i:
                        ch.enter(i, PER)
                        for s in range(2):
                            b2 = i * 2
                            off = 56 - (b2 * 8 + 8 * s)
                            dve.tensor_copy(qb[:, :, :], qbd[:, bass.ds(b2 + s, 1), :, :].rearrange("p a b n -> p (a b) n")).then_inc(S["qb"], 1)
                            dve.wait_ge(S["cs"], b2 + (s + 1))
                            ch.link(dve.tensor_tensor(pc[:, :, :], PS[:, 0, 0:P].rearrange("p (a n) -> p a n", a=2),
                                                      cb[:, :, bass.ds(off, 64)], ALU.add))
                            ch.link(dve.tensor_reduce(st[:, 0:1], pc[:, :, :].rearrange("p a n -> p (a n)"), AXX, ALU.max))
                            dve.tensor_scalar(st[:, 1:2], st[:, 0:1], 0.1 * MASKED, -1.0, ALU.max, ALU.mult).then_inc(S["nmc"], 1)
                            dve.wait_ge(S["ec"], b2 + (s + 1))
                            ch.link(dve.tensor_scalar(st[:, 2:3], st[:, 2:3], 1e-30, None, ALU.max))
                            ch.link(dve.reciprocal(st[:, 3:4], st[:, 2:3]))
                            dve.tensor_scalar(pc[:, :, :], pc[:, :, :], st[:, 3:4], None, ALU.mult).then_inc(S["pn"], 1)
                            dve.wait_ge(S["sw"], b2 + (s + 1))
                            ch.link(dve.tensor_tensor(Sw[:, 0:512], PS[:, 6, :], bw, ALU.add))
                            ch.link(dve.tensor_tensor(Sw[:, 512:576], PS[:, 0, P + NS:P + 2 * NS], bn[:, bass.ds(off, 64)], ALU.add))
                            ch.link(dve.tensor_reduce(st[:, 4:5], Sw, AXX, ALU.max))
                            dve.tensor_scalar(st[:, 5:6], st[:, 4:5], -1.0, None, ALU.mult).then_inc(S["nmw"], 1)
                            dve.wait_ge(S["pct"], b2 + (s + 1))
                            dve.tensor_copy(pcT[0:64, :, :], PS[0:64, 1, P:3 * P].rearrange("p (a n) -> p a n", a=2)).then_inc(S["pctc"], 1)
                            ch.link(dve.tensor_tensor(sel[:, 0, :], PS[:, 1, 0:16], crow[:, 1, :], ALU.add))
                            ch.link(dve.tensor_reduce(st[:, 12:13], sel[:, 0, :], AXX, ALU.min))
                            ch.link(dve.scalar_tensor_tensor(sel[:, 1, :], sel[:, 0, :], st[:, 12:13], crow[:, 0, :], ALU.is_equal, ALU.mult))
                            ch.link(dve.tensor_reduce(st[:, 13:14], sel[:, 1, :], AXX, ALU.max))
                            ch.link(dve.tensor_scalar(sel[:, 2, :], crow[:, 0, :], st[:, 13:14], MASKED, ALU.is_equal, ALU.mult))
                            dve.wait_ge(S["ss"], b2 + (s + 1))
                            for half in range(2):
                                ch.link(dve.tensor_tensor(Ss[:, 512 * half:512 * half + 512], PS[:, 4 + half, :],
                                                          bs[:, 512 * half:512 * half + 512], ALU.add))
                            ch.link(dve.tensor_tensor(Ss[:, 1024:1088], PS[:, 0, P:P + NS], bn[:, bass.ds(off, 64)], ALU.add))
                            for half in range(2):
                                v = Ss[:, 0:1024].rearrange("p (g a l) -> p g a l", a=2, l=BLK)[:, :, half, :]
                                ch.link(dve.tensor_tensor(v, v, sel[:, 2, 8 * half:8 * half + 8].unsqueeze(2).to_broadcast([P, 8, BLK]), ALU.add))
                            ch.link(dve.tensor_reduce(st[:, 8:9], Ss, AXX, ALU.max))
                            dve.tensor_scalar(st[:, 9:10], st[:, 8:9], -1.0, None, ALU.mult).then_inc(S["nms"], 1)
                            dve.wait_ge(S["es"], b2 + (s + 1))
                            dve.wait_ge(S["ew"], b2 + (s + 1))
                            ch.link(dve.reciprocal(st[:, 7:8], st[:, 6:7]))
                            ch.link(dve.reciprocal(st[:, 11:12], st[:, 10:11]))
                            dve.wait_ge(S["og"], i * (2 * 48) + 48 * s)
                            dve.wait_ge(S["ov"], b2 + (s + 1))
                            for h in range(N_KV):
                                r = slice(32 * h, 32 * h + 32)
                                dve.tensor_copy(osb[r, 0, :], PS[r, 7, HD * h:HD * h + HD])
                                dve.tensor_scalar(osb[r, 1, :], PS[r, 7, 256 + HD * h:256 + HD * h + HD], st[r, 11:12], None, ALU.mult)
                                ins = dve.tensor_scalar(osb[r, 2, :], PS[r, 6, HD * h:HD * h + HD], st[r, 7:8], None, ALU.mult)
                            ins.then_inc(S["osc"], 1)
                        ch.leave(DEC_BATCH // 2)

        def attention_out():
            og = at(O_Q, 3, N_HEADS, HD)
            junk = at(O_FREE, ATT_WIDTH)
            st = at(O_FREE + 1024, 5, 2)
            S = {n: sem("ao_" + n) for n in ("dch", "sq", "rt", "n", "t", "c", "z", "ld")}
            with nc.Block() as block:
                @block.sync
                def _(sp):
                    sp.dma_start(og[0:NS, :, :, :].rearrange("p r h d -> p r (h d)"),
                                 scr_o.ap().rearrange("r t n -> t r n")).then_inc(S["ld"], 16)

                @block.vector
                def _(dve):
                    ch = Chain(dve, S["dch"])
                    dve.wait_ge(S["ld"], 16)
                    g3 = sg[0:NS, 4, :].rearrange("p (h r) -> p h r", r=3)
                    for br in range(3):
                        ch.link(dve.tensor_tensor(og[0:NS, br, :, :], og[0:NS, br, :, :],
                                                  g3[:, :, br:br + 1].to_broadcast([NS, 16, HD]), ALU.mult))
                    flat = [og[0:NS, br, :, :].rearrange("p h d -> p (h d)") for br in range(3)]
                    ch.link(dve.tensor_tensor(flat[0], flat[0], flat[1], ALU.add))
                    dve.tensor_tensor(onat[0:NS, 4, :], flat[0], flat[2], ALU.add).then_inc(S["z"], 1)
                    for i, (t0, n) in enumerate(TILES):
                        dve.wait_ge(S["rt"], i + 1)
                        ch.link(dve.reciprocal(st[0:n, i, 1:2], st[0:n, i, 1:2]))
                        dve.tensor_scalar(onat[0:n, i, :], onat[0:n, i, :], st[0:n, i, 1:2], None, ALU.mult).then_inc(S["n"], 1)
                    u = 0
                    for i, (t0, n) in enumerate(TILES):
                        for q in range(2):
                            dve.wait_ge(S["t"], u + 1)
                            for j in range(4):
                                k = 4 * q + j
                                ins = dve.tensor_scalar(oT[:, k, t0:t0 + n], PS[:, u % 4, j * P:j * P + n],
                                                        gT[:, 8 * GATT + k:8 * GATT + k + 1], None, ALU.mult)
                            ins.then_inc(S["c"], 1)
                            u += 1

                @block.scalar
                def _(act):
                    for i, (t0, n) in enumerate(TILES):
                        if i == 4:
                            act.wait_ge(S["z"], 1)
                        act.activation(junk[0:n, :], onat[0:n, i, :], ACT.Square, scale=ATT_WIDTH ** -0.5,
                                       accum_out=st[0:n, i, 0:1]).then_inc(S["sq"], 1)
                        act.wait_ge(S["sq"], i + 1)
                        act.activation(st[0:n, i, 1:2], st[0:n, i, 0:1], ACT.Sqrt, bias=eps_sb[0:n, 0:1]).then_inc(S["rt"], 1)

                @block.tensor
                def _(pe):
                    u = 0
                    for i, (t0, n) in enumerate(TILES):
                        pe.wait_ge(S["n"], i + 1)
                        for q in range(2):
                            if u >= 4:
                                pe.wait_ge(S["c"], u - 3)
                            for j in range(4):
                                m = pe.transpose(PS[:, u % 4, j * P:j * P + n], onat[0:n, i, (4 * q + j) * P:(4 * q + j + 1) * P], ident[0:n, 0:n])
                            m.then_inc(S["t"], 1)
                            u += 1

        def mixer_out():
            y = at(O_Z, KD, T)
            project_out("mo", io["w_out"].rearrange("a k n -> (a k) n"), D_MIX // P, oT, y, O_Z + KD * T)
            post_norm("mpost", GMPOST, y)


        setup()
        compress_past()
        ffn("f1", io["ffn1_w_in"].rearrange("a k n -> (a k) n"), io["ffn1_w_out"].rearrange("a k n -> (a k) n"), G1PRE, G1POST)
        mixer_in()
        conv()
        ssd()
        ssd_gate_norm()
        recycle_semaphores()
        compress_prompt()
        attend_prompt()
        attend_sample()
        attention_out()
        mixer_out()
        ffn("f2", io["ffn2_w_in"].rearrange("a k n -> (a k) n"), io["ffn2_w_out"].rearrange("a k n -> (a k) n"), G2PRE, G2POST)
        finish_out()


_INS = ['x_prompt', 'x_sample', 'cache_cmp_kv', 'cache_slc_kv', 'cache_win_kv', 'state_ssm', 'state_conv',
        'page_table', 'rel_table', 'ffn1_pre', 'ffn1_post', 'ffn1_w_in', 'ffn1_w_out', 'mix_pre', 'mix_post',
        'w_in', 'w_out', 'att_out_norm', 'cmp_pe', 'w_cmp', 'conv_w', 'conv_b', 'dt_bias', 'a_log', 'd_skip',
        'ssd_norm', 'ffn2_pre', 'ffn2_post', 'ffn2_w_in', 'ffn2_w_out']
_OUTS = [("y_prompt", (1, 512, 1024)), ("y_sample", (8, 8, 1024)),
         ("p_cmp_kv", (1, 1, 512, 4, 2, 64)), ("p_slc_kv", (1, 1, 512, 4, 2, 64)), ("p_win_kv", (1, 1, 512, 4, 2, 64)),
         ("p_ssm", (1, 1, 16, 64, 128)), ("p_conv", (1, 1, 3, 1536)),
         ("s_cmp_kv", (1, 8, 8, 4, 2, 64)), ("s_slc_kv", (1, 8, 8, 4, 2, 64)), ("s_win_kv", (1, 8, 512, 4, 2, 64)),
         ("s_ssm", (1, 8, 16, 64, 128)), ("s_conv", (1, 8, 3, 1536))]


def kernel(**inputs):
    import numpy as _np
    import concourse.bacc as _bacc
    from concourse import mybir as _mybir
    from concourse.bass_utils import run_bass_kernel_spmd as _run

    nc = _bacc.Bacc("TRN2", target_bir_lowering=False, num_devices=1)
    arrays, io = {}, {}
    for name in _INS:
        arrays[f"in_{name}"] = _np.ascontiguousarray(inputs[name])
    for name, value in constants().items():
        arrays[f"in_{name}"] = value
    for name, a in arrays.items():
        io[name[3:]] = nc.dram_tensor(name, a.shape, _mybir.dt.from_np(a.dtype), kind="ExternalInput").ap()
    out = {name: nc.dram_tensor(f"out_{name}", shape, F32, kind="ExternalOutput").ap() for name, shape in _OUTS}
    build(nc, io, out)
    r = _run(nc, [arrays], core_ids=[0])
    return tuple(r.results[0][f"out_{name}"] for name, _ in _OUTS)
```

```python
from contextlib import ExitStack

import numpy as np

import concourse.bass as bass
from concourse import mybir

F32 = mybir.dt.float32
I32 = mybir.dt.int32
F32R = mybir.dt.float32r
ALU = mybir.AluOpType
ACT = mybir.ActivationFunctionType
AXX = mybir.AxisListType.X

D_MODEL, SEQ, DEC_BATCH, DEC_SEQ, PAST_LEN, PAGE = 1024, 512, 8, 8, 1024, 128
N_HEADS, HD, N_KV, GQA = 16, 64, 4, 4
ATT_WIDTH, KV_WIDTH = 1024, 512
BLK, WINDOW, N_BUCKETS, MAX_DISTANCE = 64, 512, 32, 128
SSD_HEADS, SSD_GROUPS, SSD_STATE, CONV_W = 16, 2, 128, 4
SSD_INNER, CONV_DIM, D_MIX, D_FF, N_BRANCH = 1024, 1536, 2048, 2816, 3
N_POOL = 80
EPS = 1e-6
SCALE = HD ** -0.5
MASKED = -1e30

P = 128
NS = DEC_BATCH * DEC_SEQ
T = SEQ + NS
TILES = [(i * P, P) for i in range(SEQ // P)] + [(SEQ, NS)]
KD = D_MODEL // P
KF = D_FF // P
KC_XBC = CONV_DIM // P
PAGES = PAST_LEN // PAGE
ALL_PAGES = DEC_BATCH * PAGES
PAD = CONV_W - 1
XP_S = PAD + SEQ
XP_RUN = PAD + DEC_SEQ
XP = XP_S + DEC_BATCH * XP_RUN
CONV_N = XP - PAD

COL_KV = ATT_WIDTH
COL_GATES = ATT_WIDTH + 3 * KV_WIDTH
COL_Z = COL_GATES + N_BRANCH * N_HEADS
COL_DT = COL_Z + SSD_INNER + CONV_DIM
D_IN = COL_DT + SSD_HEADS

LEN_R, TOP_R = 1664, 1151
LEN_F, LOW_F = 1024, -512
LEN_T = SEQ + P
FIRST_T = TOP_R - (SEQ - P) - (P - 1)
LEN_W, TOP_W = 544, 527


def bucket_of(dist):
    exact = N_BUCKETS // 2
    n = np.maximum(dist, 0)
    f = np.maximum(n, 1).astype(np.float32)
    far = exact + (np.log(f / np.float32(exact)) / np.float32(np.log(MAX_DISTANCE / exact))
                   * np.float32(N_BUCKETS - exact)).astype(np.int32)
    return np.where(n < exact, n, np.minimum(far, N_BUCKETS - 1))


def one_hot(dist, limit):
    b = np.where((dist < 0) | (dist >= limit), N_BUCKETS, bucket_of(dist))
    return (np.arange(N_BUCKETS + 1)[:, None] == b[None, :]).astype(np.float32)


def constants():
    big = 10 ** 9
    hot = np.concatenate([
        one_hot(TOP_R - np.arange(LEN_R), big),
        one_hot(LOW_F + np.arange(LEN_F), big),
        one_hot(TOP_W - np.arange(LEN_W), WINDOW)], axis=1)
    r = np.arange(P)
    same = r[:, None] // DEC_SEQ == r[None, :] // DEC_SEQ
    tri = r[:, None] <= r[None, :]
    group = (r[:, None] // 32 == r[None, :] // 32) & (r[:, None] % DEC_SEQ == r[None, :] % DEC_SEQ)
    squares = np.stack([np.eye(P), tri, np.ones((P, P)), tri & same, same, group], axis=1).astype(np.float32)
    order = np.arange(16)
    block = (2 * (order % PAGES) + order // PAGES).astype(np.float32)
    forced = (block == 0) | (block == 15)
    rows = np.zeros((P, 3, 16), np.float32)
    rows[:, 0, :] = block
    rows[:, 1, :] = np.where(forced, 1e30, 0.0)
    rows[:NS, 2, :DEC_BATCH] = np.arange(NS)[:, None] // DEC_SEQ == np.arange(DEC_BATCH)[None, :]
    return {"c_hot": hot, "c_squares": squares, "c_rows": rows}


IDENT, TRI, ONES, BTRI, BONES, GROUP = range(6)


def turns(eng, first, count):
    yield 0
    with eng.Fori(1, count if first else count - 1) as i:
        yield i
    if not first:
        yield count - 1


def known(i):
    return isinstance(i, int)


class Chain:

    def __init__(self, eng, sem):
        self.eng, self.sem, self.n, self.base, self.per = eng, sem, 0, None, 0

    def link(self, ins):
        self.n += 1
        ins.then_inc(self.sem, 1)
        self.eng.wait_ge(self.sem, self.n if self.base is None else self.base + self.n)

    def enter(self, i, per):
        if self.base is None:
            self.start, self.per = self.n, per
        assert self.n in (self.start, self.start + per), (self.n, self.start, per)
        self.n, self.base = self.start, i * per

    def leave(self, count):
        assert self.n - self.start == self.per, (self.n - self.start, self.per)
        self.n, self.base = self.start + self.per * count, None


def build(nc, io, out):
    with ExitStack() as ctx:
        def sb(name, shape, dt=F32):
            return ctx.enter_context(nc.sbuf_tensor(name, shape, dt))

        stage_sems = []

        def sem(name, lasting=False):
            s = nc.alloc_semaphore(name)
            if not lasting:
                stage_sems.append(s)
            return s

        def recycle_semaphores():
            nc.clear_and_free_semaphores(list(stage_sems))
            stage_sems.clear()
            nc.all_engine_barrier()

        xT = sb("xT", [P, KD, T])
        sq6 = sb("sq6", [P, 6, P])
        crow = sb("crow", [P, 3, 16])
        gT = sb("gT", [P, 64])
        convT = sb("convT", [P, 5 * KC_XBC])
        small = sb("small", [P, 6, SSD_HEADS])
        rstd = sb("rstd", [P, T])
        sqr = sb("sqr", [P, 2, T])
        sacc = sb("sacc", [P, T])
        bias_cmp = sb("bias_cmp", [P, 4, N_HEADS, 8])
        kc_all = sb("kc_all", [P, 2, 2, ALL_PAGES])
        vc_all = sb("vc_all", [ALL_PAGES, 2, 256])
        pe_c = sb("pe_c", [P, 2])
        eps_sb = sb("eps_sb", [P, 1])
        page_sb = sb("page_sb", [1, ALL_PAGES], I32)
        AW = 43600
        arena_at = nc.sbuf_base
        arena = sb("arena", [P, AW])

        def part(name, o, *dims, dt=F32):
            v = nc.alloc_sbuf_tensor_at(name, [P] + list(dims), dt, offset=arena_at + 4 * o)
            return v[tuple([slice(None)] * (len(dims) + 1))]
        PS = ctx.enter_context(nc.psum_tensor("PS", [P, 8, 512], F32))

        def at(o, *dims):
            n = int(np.prod(dims))
            assert o + n <= AW, (o, n)
            v = arena[:, o:o + n]
            if len(dims) == 1:
                return v
            names = "abcd"[:len(dims)]
            return v.rearrange("p (" + " ".join(names) + ") -> p " + " ".join(names),
                               **{c: d for c, d in zip(names[1:], dims[1:])})

        ident = sq6[:, IDENT, :]
        scr_r = nc.dram_tensor("scr_r", (N_HEADS, LEN_R), F32)
        scr_o = nc.dram_tensor("scr_o", (N_BRANCH, NS, ATT_WIDTH), F32)
        scr_t = nc.dram_tensor("scr_t", (N_HEADS, P, LEN_T), F32)
        scr_w = nc.dram_tensor("scr_w", (N_HEADS, LEN_W), F32)
        G1PRE, G1POST, GMPRE, GMPOST, GATT, GSSD, G2PRE, G2POST = range(8)

        def halves(v):
            return v[:, 0:SEQ], v[:, SEQ:T]

        def setup():
            xnat = at(0, 5, D_MODEL)
            hot = at(5120, LEN_R + LEN_F + LEN_W)
            gnat = at(8400, 2, P)
            tabl = at(8700, N_HEADS)
            fr = at(8800, LEN_R + LEN_W)
            ld, s_mm, s_ev, s_scr, s_tab, s_fr = (sem("su_" + n) for n in ("ld", "mm", "ev", "scr", "tab", "fr"))
            s_small, s_ch, s_dch = sem("su_small"), sem("su_ch"), sem("su_dch")
            LOADS = 4 + 5 + 8 + 3
            pieces = [(0, 512), (512, 512), (1024, 512), (1536, LEN_R - 1536)]
            with nc.Block() as block:
                @block.sync
                def _(sp):
                    n = [0]

                    def load(dst, src):
                        sp.dma_start(dst, src).then_inc(ld, 16)
                        n[0] += 1
                    sp.wait_ge(s_tab, 1)
                    load(tabl[0:N_BUCKETS, :], io["rel_table"])
                    load(sq6[:, :, :], io["c_squares"])
                    load(crow[:, :, :], io["c_rows"])
                    load(hot[0:N_BUCKETS + 1, :], io["c_hot"])
                    for i in range(4):
                        load(xnat[:, i, :], io["x_prompt"][0, i * P:(i + 1) * P, :])
                    load(xnat[0:NS, 4, :], io["x_sample"].rearrange("b t d -> (b t) d"))
                    for w, name in enumerate(["ffn1_pre", "ffn1_post", "mix_pre", "mix_post", "att_out_norm",
                                              "ssd_norm", "ffn2_pre", "ffn2_post"]):
                        load(gnat[8 * w:8 * w + 8, 0, :], io[name].rearrange("l (k p) -> (l k) p", p=P))
                    load(gnat[0:48, 1, :], io["conv_w"].rearrange("l w (k p) -> (l w k) p", p=P))
                    load(gnat[48:60, 1, :], io["conv_b"].rearrange("l (k p) -> (l k) p", p=P))
                    load(page_sb[0:1, :], io["page_table"].rearrange("b n -> (b n)").rearrange("(a n) -> a n", a=1))
                    assert n[0] == LOADS
                    sp.wait_ge(s_fr, 5)
                    sp.wait_ge(s_ev, 1)
                    sp.dma_start(scr_r.ap()[:, :], fr[0:N_HEADS, 0:LEN_R]).then_inc(s_scr, 16)
                    sp.dma_start(scr_w.ap()[:, :], fr[0:N_HEADS, LEN_R:LEN_R + LEN_W]).then_inc(s_scr, 16)
                    sp.dma_start(scr_t.ap()[:, :, :], fr[0:N_HEADS, FIRST_T:FIRST_T + LEN_T].unsqueeze(1)
                                 .to_broadcast([N_HEADS, P, LEN_T])).then_inc(s_scr, 16)
                    sp.wait_ge(s_scr, 48)

                @block.scalar
                def _(act):
                    with nc.allow_non_contiguous_dma(reason="small vectors spread over partitions"):
                        for k, name in enumerate(["dt_bias", "a_log"]):
                            h = io[name]
                            act.dma_start(small[:, k, :], bass.AP(h.tensor, 0, [[0, P], [1, SSD_HEADS]])).then_inc(s_small, 16)
                        for half in range(2):
                            act.dma_start(small[half * 64:half * 64 + 64, 3, 0:8],
                                          bass.AP(io["d_skip"].tensor, half, [[0, 64], [2, 8]])).then_inc(s_small, 16)
                    act.wait_ge(s_small, 64)
                    act.activation(small[:, 2, :], small[:, 1, :], ACT.Exp).then_inc(s_ch, 1)
                    act.wait_ge(s_ch, 1)
                    act.mul(small[:, 2, :], small[:, 2, :], -1.0).then_inc(s_ch, 1)
                    act.wait_ge(s_ch, 2)

                @block.tensor
                def _(pe):
                    pe.wait_ge(ld, 16 * LOADS)
                    for k, (a, n) in enumerate(pieces + [(LEN_R + LEN_F, 512), (LEN_R + LEN_F + 512, LEN_W - 512)]):
                        if k == 5:
                            mm = pe.matmul(PS[0:N_HEADS, 0, 0:n], tabl[0:33, :], hot[0:33, a:a + n], start=True, stop=True)
                            continue
                        b = [1, 2, 3, 4, 5][k]
                        mm = pe.matmul(PS[0:N_HEADS, b, 0:n], tabl[0:33, :], hot[0:33, a:a + n], start=True, stop=True)
                    mm.then_inc(s_mm, 1)
                    for i in range(4):
                        for o in range(8):
                            n = 2 * (o % 4) + o // 4
                            v = LEN_R + i * P - BLK * n - (BLK - 1) - LOW_F
                            mm = pe.matmul(PS[:, 6, (i * 8 + o) * 16:(i * 8 + o + 1) * 16], hot[0:33, v:v + P],
                                           tabl[0:33, :], start=True, stop=True)
                    mm.then_inc(s_mm, 1)
                    pe.transpose(PS[:, 7, 0:64], gnat[0:64, 0, :], ident[0:64, 0:64])
                    pe.transpose(PS[:, 7, 64:124], gnat[0:60, 1, :], ident[0:60, 0:60]).then_inc(s_mm, 1)
                    u = 0
                    for i, (t0, n) in enumerate(TILES):
                        for q in range(2):
                            if u < 2:
                                pe.wait_ge(s_ev, 1)
                            else:
                                pe.wait_ge(s_ev, u - 2 + 4)
                            for j in range(4):
                                mm = pe.transpose(PS[:, u % 2, j * P:j * P + n],
                                                  xnat[0:n, i, (4 * q + j) * P:(4 * q + j + 1) * P], ident[0:n, 0:n])
                            mm.then_inc(s_mm, 1)
                            u += 1

                @block.vector
                def _(dve):
                    dve.memset(tabl[0:33, :], MASKED).then_inc(s_tab, 1)
                    dve.memset(eps_sb[:, :], EPS).then_inc(s_dch, 1)
                    dve.wait_ge(s_mm, 1)
                    for k, (a, n) in enumerate(pieces + [(LEN_R, 512)]):
                        dve.tensor_copy(fr[0:N_HEADS, a:a + n], PS[0:N_HEADS, k + 1, 0:n]).then_inc(s_fr, 1)
                    dve.tensor_copy(fr[0:N_HEADS, LEN_R + 512:LEN_R + LEN_W], PS[0:N_HEADS, 0, 0:LEN_W - 512]).then_inc(s_ev, 1)
                    dve.wait_ge(s_mm, 2)
                    dve.tensor_copy(bias_cmp[:, :, :, :].rearrange("p i h o -> p i o h"),
                                    PS[:, 6, :].rearrange("p (i o h) -> p i o h", i=4, o=8)).then_inc(s_ev, 1)
                    dve.wait_ge(s_mm, 3)
                    dve.tensor_copy(gT[:, :], PS[:, 7, 0:64]).then_inc(s_dch, 1)
                    dve.tensor_copy(convT[:, :], PS[:, 7, 64:124]).then_inc(s_ev, 1)
                    u = 0
                    for i, (t0, n) in enumerate(TILES):
                        for q in range(2):
                            dve.wait_ge(s_mm, 4 + u)
                            dve.tensor_copy(xT[:, 4 * q:4 * q + 4, t0:t0 + n],
                                            PS[:, u % 2, :].rearrange("p (j n) -> p j n", j=4)[:, :, 0:n]).then_inc(s_ev, 1)
                            u += 1
                    dve.wait_ge(s_ev, 13)
                    for w in (G1POST, G2POST):
                        dve.wait_ge(s_dch, 2)
                        dve.tensor_scalar(gT[:, 8 * w:8 * w + 8], gT[:, 8 * w:8 * w + 8], 0.5, None, ALU.mult).then_inc(s_ev, 1)

        def compress_past():
            GP = 32
            wbd = at(0, P, 2, 64)
            pg = at(16384, GP + 1, 512)
            ck = at(16384 + (GP + 1) * 512, 2, N_KV, ALL_PAGES)
            ld_w, ld_p, s_z, mm, ev, s_t, s_k = (sem("cp_" + n) for n in ("w", "p", "z", "mm", "ev", "t", "k"))
            s_pe, s_added = sem("cp_pe"), sem("cp_added")
            kh = io["w_cmp"].rearrange("a l c d e -> (a l) (c d) e")
            with nc.Block() as block:
                @block.sync
                def _(sp):
                    with nc.allow_non_contiguous_dma(reason="rows of 256 bytes"):
                        sp.wait_ge(s_z, 2)
                        for q in range(4):
                            for half in range(2):
                                sp.dma_start(wbd[half * 64:half * 64 + 64, 32 * q:32 * q + 32, half, :],
                                             kh[:, 32 * q:32 * q + 32, :]).then_inc(ld_w, 16)
                    for half in range(2):
                        sp.dma_start(pg[half * 64:half * 64 + 64, GP, 0:P],
                                     io["cmp_pe"].rearrange("a l c d -> (a l) (c d)")).then_inc(s_pe, 16)
                    cache = io["cache_cmp_kv"].rearrange("a n p h c d -> (a n) p (h c d)")
                    for r in range(2):
                        if r:
                            sp.wait_ge(mm, 2 * r)
                        with sp.Fori(0, GP) as j:
                            page = sp.value_load(page_sb[0:1, bass.ds(r * GP + j, 1)], min_val=0, max_val=N_POOL - 1)
                            sp.dma_start(pg[:, bass.ds(j, 1), :].rearrange("p a n -> p (a n)"),
                                         cache[bass.ds(page, 1), :, :].rearrange("a p n -> (a p) n")).then_inc(ld_p, 16)
                    sp.wait_ge(ev, 4)
                    for half in range(2):
                        for odd in range(2):
                            sp.dma_start(kc_all[64 * odd:64 * odd + 64, :, half, :],
                                         ck[64 * half:64 * half + 64, 0, :, :].rearrange("p (a b) n -> p a b n", b=2)[:, :, odd, :]
                                         ).then_inc(s_k, 16)
                    sp.wait_ge(s_k, 64)

                @block.gpsimd
                def _(pool):
                    pool.memset(wbd[0:64, :, 1, :], 0.0).then_inc(s_z, 1)

                @block.tensor
                def _(pe):
                    pe.wait_ge(ld_w, 16 * 8)
                    pe.wait_ge(s_pe, 32)
                    for r in range(2):
                        pe.wait_ge(ld_p, (r + 1) * (16 * GP))
                        if r:
                            pe.wait_ge(ev, r * 2)
                        for c in range(2):
                            for d in range(64):
                                rhs = bass.AP(pg.tensor, pg.offset + c * 64 + d, [pg.ap[0], [P, 4 * GP + 1]])
                                m = pe.matmul(PS[:, c, 0:4 * GP + 1], wbd[:, c * 64 + d, :, :].rearrange("p a b -> p (a b)"),
                                              rhs, start=(d == 0), stop=(d == 63))
                            m.then_inc(mm, 1)
                    pe.wait_ge(ev, 4)
                    for h in range(N_KV):
                        m = pe.transpose(PS[0:ALL_PAGES, 2, h * P:(h + 1) * P], ck[:, 1, h, :], ident)
                    m.then_inc(s_t, 1)

                @block.vector
                def _(dve):
                    dve.memset(wbd[64:P, :, 0, :], 0.0).then_inc(s_z, 1)
                    pe_done = s_added
                    with dve.Fori(0, 2) as r:
                        for c in range(2):
                            dve.wait_ge(mm, r * 2 + (c + 1))
                            dve.tensor_copy(pe_c[:, c:c + 1], PS[:, c, 4 * GP:4 * GP + 1]).then_inc(pe_done, 1)
                            dve.wait_ge(pe_done, r * 2 + (c + 1))
                            dst = ck[:, c, :, bass.ds(r * GP, GP)]
                            dve.tensor_scalar(dst, PS[:, c, 0:4 * GP].rearrange("p (n h) -> p h n", h=N_KV),
                                              pe_c[:, c:c + 1], None, ALU.add).then_inc(ev, 1)
                    dve.wait_ge(s_t, 1)
                    dve.tensor_copy(vc_all[:, :, :].rearrange("n a (h e) -> n h a e", h=N_KV),
                                    PS[0:ALL_PAGES, 2, :].rearrange("n (h a e) -> n h a e", h=N_KV, a=2)).then_inc(pe_done, 1)

        class Split:

            def __init__(self, name, o, *dims):
                n = int(np.prod(dims))
                self.h, self.l = part(name + "_h", o, *dims, dt=F32R), part(name + "_l", o + n, *dims, dt=F32R)
                self.h_f32 = self.h.bitcast(F32)

        HALF = T // 2

        def both(bank):
            return PS[:, bank:bank + 2, 0:HALF]

        def cut(row):
            return row.rearrange("p (a n) -> p a n", a=2)

        def product(pe, bank, w, wk, x, xk, start, stop):
            passes = [(w.h, x.h), (w.h, x.l), (w.l, x.h)]
            for j, (a, b) in enumerate(passes):
                for half in range(2):
                    m = pe.matmul(PS[:, bank + half, 0:HALF], a[:, wk, :], b[:, xk, half * HALF:(half + 1) * HALF],
                                  start=start and j == 0, stop=stop and j == 2)
            return m

        class Norm:

            def __init__(self, tag, src):
                self.src = src
                self.sq, self.acc, self.tot, self.root, self.r = (sem(tag + n) for n in ("_sq", "_acc", "_tot", "_root", "_rstd"))

            def square(self, act, k):
                if k >= 3:
                    act.wait_ge(self.acc, k - 2)
                act.activation(sqr[:, k % 2, :] if k else sacc[:, :], self.src[:, k, :], ACT.Square,
                               scale=D_MODEL ** -0.5).then_inc(self.sq, 1)

            def add(self, dve, k):
                dve.wait_ge(self.sq, k + 1)
                if k > 1:
                    dve.wait_ge(self.acc, k - 1)
                dve.tensor_tensor(sacc[:, :], sacc[:, :], sqr[:, k % 2, :], ALU.add).then_inc(self.acc, 1)

            def total(self, pe):
                pe.wait_ge(self.acc, KD - 1)
                for half in range(2):
                    m = pe.matmul(PS[:, 6 + half, 0:HALF], sq6[:, ONES, :], sacc[:, half * HALF:(half + 1) * HALF], start=True, stop=True)
                m.then_inc(self.tot, 1)

            def take_root(self, act):
                act.wait_ge(self.tot, 1)
                act.activation(cut(rstd[:, :]), both(6), ACT.Sqrt, bias=eps_sb[:, 0:1]).then_inc(self.root, 1)

            def invert(self, dve):
                dve.wait_ge(self.root, 1)
                dve.reciprocal(rstd[:, :], rstd[:, :]).then_inc(self.r, 1)
                dve.wait_ge(self.r, 1)

        def project_out(tag, w, kc, x, y, o_round, o_raw, gain, source=None):
            kp = kc // 2
            raw = [part(f"{tag}_raw{s}", o_raw + s * kp * P, kp, P) for s in range(2)]
            ws = [Split(f"{tag}_w{s}", o_round + 2 * s * kp * P, kp, P) for s in range(2)]
            land, s_h, s_l, mm = ([sem(f"{tag}_{n}{s}") for s in range(2)] for n in ("land", "wh", "wl", "mm"))
            done, ev, s_src_h, s_src, s_w, s_res = (sem(f"{tag}_{n}") for n in ("done", "ev", "xh", "xl", "scaled", "res"))
            nrm = Norm(tag + "_post", y)
            wv = w.rearrange("(k p) n -> p k n", p=P)
            with nc.Block() as block:
                @block.sync
                def _(sp):
                    for m in turns(sp, True, KD):
                        for s in range(2):
                            if not known(m):
                                sp.wait_ge(s_l[s], m)
                            sp.dma_start(raw[s], wv[:, s * kp:(s + 1) * kp, bass.ds(m * P, P)]).then_inc(land[s], 16)

                @block.tensor
                def _(pe):
                    for i in turns(pe, True, KD // 2):
                        for c in range(2):
                            m = 2 * i + c
                            for s in range(2):
                                pe.wait_ge(s_l[s], m + 1)
                                if s == 0 and not (known(m) and m < 2):
                                    pe.wait_ge(ev, m - 1)
                                for k in range(kp):
                                    if source is not None and known(m) and m == 0:
                                        pe.wait_ge(s_src, s * kp + k + 1)
                                    last = product(pe, 2 * c, ws[s], k, x, s * kp + k, s == 0 and k == 0, s == 1 and k == kp - 1)
                                last.then_inc(mm[s], 1)
                    nrm.total(pe)

                @block.scalar
                def _(act):
                    def round_piece(s, m):
                        act.wait_ge(land[s], (m + 1) * 16)
                        if not (known(m) and m == 0):
                            act.wait_ge(mm[s], m)
                        act.copy(ws[s].h, raw[s]).then_inc(s_h[s], 1)
                    for s in range(2):
                        round_piece(s, 0)
                    if source is not None:
                        for k in range(kc):
                            act.copy(x.h[:, k, :], source[:, k, :]).then_inc(s_src_h, 1)
                    for m in range(KD):
                        if m + 1 < KD:
                            for s in range(2):
                                round_piece(s, m + 1)
                        act.wait_ge(ev, m + 1)
                        nrm.square(act, m)
                    nrm.take_root(act)

                @block.vector
                def _(dve):
                    def rest_of_piece(s, m):
                        dve.wait_ge(s_h[s], m + 1)
                        dve.tensor_tensor(ws[s].l, raw[s], ws[s].h_f32, ALU.subtract).then_inc(s_l[s], 1)
                    for s in range(2):
                        rest_of_piece(s, 0)
                    if source is not None:
                        for k in range(kc):
                            dve.wait_ge(s_src_h, k + 1)
                            dve.tensor_tensor(x.l[:, k, :], source[:, k, :], x.h_f32[:, k, :], ALU.subtract).then_inc(s_src, 1)
                    for m in range(KD):
                        if m + 1 < KD:
                            for s in range(2):
                                rest_of_piece(s, m + 1)
                        dve.wait_ge(mm[1], m + 1)
                        dve.tensor_copy(cut(y[:, m, :]), both(2 * (m % 2))).then_inc(ev, 1)
                        if m > 1:
                            nrm.add(dve, m - 1)
                    nrm.add(dve, KD - 1)
                    nrm.invert(dve)
                    for k in range(KD):
                        dve.scalar_tensor_tensor(y[:, k, :], y[:, k, :], gT[:, 8 * gain + k:8 * gain + k + 1],
                                                 rstd[:, :], ALU.mult, ALU.mult).then_inc(s_w, 1)
                        if k:
                            dve.wait_ge(s_w, k)
                            dve.tensor_tensor(xT[:, k - 1, :], xT[:, k - 1, :], y[:, k - 1, :], ALU.add).then_inc(s_res, 1)
                    dve.wait_ge(s_w, KD)
                    dve.tensor_tensor(xT[:, KD - 1, :], xT[:, KD - 1, :], y[:, KD - 1, :], ALU.add).then_inc(s_res, 1)

        def ffn(tag, w_in, w_out, pre, post):
            x = Split(tag + "_x", 0, KD, T)
            h = Split(tag + "_h", 2 * KD * T, KF, T)
            o = 2 * KD * T + 2 * KF * T
            ws = [Split(f"{tag}_w{side}", o + side * 2 * KD * P, KD, P) for side in range(2)]
            raw = [part(f"{tag}_raw{side}", o + (4 + side) * KD * P, KD, P) for side in range(2)]
            o += 6 * KD * P
            silu = [part(f"{tag}_silu{c}", o + c * T, T) for c in range(2)]
            tmp = [part(f"{tag}_prod{c}", o + (2 + c) * T, T) for c in range(2)]
            land, s_h, s_l, mm = ([sem(f"{tag}_{n}{s}") for s in range(2)] for n in ("land", "wh", "wl", "mm"))
            s_silu, s_prod, s_hh, s_hl, s_x, s_xh, s_xl = (sem(f"{tag}_{n}") for n in ("silu", "prod", "hh", "hl", "x", "xh", "xl"))
            nrm = Norm(tag + "_pre", xT)
            wv = w_in.rearrange("(k p) n -> p k n", p=P)
            xt = silu + [tmp[0]]
            with nc.Block() as block:
                @block.sync
                def _(sp):
                    for c in turns(sp, True, KF):
                        for side in range(2):
                            if not known(c):
                                sp.wait_ge(s_l[side], c)
                            sp.dma_start(raw[side], wv[:, :, bass.ds(c * P + side * D_FF, P)]).then_inc(land[side], 16)

                @block.tensor
                def _(pe):
                    nrm.total(pe)
                    for i in turns(pe, True, KF // 2):
                        for j in range(2):
                            c = 2 * i + j
                            for side in range(2):
                                pe.wait_ge(s_l[side], c + 1)
                                if side == 0 and not (known(c) and c < 2):
                                    pe.wait_ge(s_prod, c - 1)
                                for k in range(KD):
                                    if known(c) and c == 0 and side == 0:
                                        pe.wait_ge(s_xl, k + 1)
                                    m = product(pe, 4 * j + 2 * side, ws[side], k, x, k, k == 0, k == KD - 1)
                                m.then_inc(mm[side], 1)

                @block.scalar
                def _(act):
                    def round_piece(side, c):
                        act.wait_ge(land[side], (c + 1) * 16)
                        if not (known(c) and c == 0):
                            act.wait_ge(mm[side], c)
                        act.copy(ws[side].h, raw[side]).then_inc(s_h[side], 1)
                    for k in range(KD):
                        nrm.square(act, k)
                    nrm.take_root(act)
                    for side in range(2):
                        round_piece(side, 0)
                    for k in range(KD):
                        act.wait_ge(s_x, k + 1)
                        act.copy(x.h[:, k, :], xt[k % 3]).then_inc(s_xh, 1)
                    for i in turns(act, False, KF // 2):
                        for j in range(2):
                            c = 2 * i + j
                            last = known(c) and c == KF - 1
                            if not last:
                                round_piece(0, c + 1)
                            act.wait_ge(mm[0], c + 1)
                            act.activation(cut(silu[j]), both(4 * j), ACT.Silu).then_inc(s_silu, 1)
                            if not last:
                                round_piece(1, c + 1)
                            act.wait_ge(s_prod, c + 1)
                            act.copy(h.h[:, bass.ds(c, 1), :].rearrange("p a n -> p (a n)"), tmp[j]).then_inc(s_hh, 1)

                @block.vector
                def _(dve):
                    def rest_of_piece(side, c):
                        dve.wait_ge(s_h[side], c + 1)
                        dve.tensor_tensor(ws[side].l, raw[side], ws[side].h_f32, ALU.subtract).then_inc(s_l[side], 1)

                    def rest_of_x(k):
                        dve.wait_ge(s_xh, k + 1)
                        dve.tensor_tensor(x.l[:, k, :], xt[k % 3], x.h_f32[:, k, :], ALU.subtract).then_inc(s_xl, 1)
                    for k in range(1, KD):
                        nrm.add(dve, k)
                    nrm.invert(dve)
                    for k in range(KD):
                        if k >= 3:
                            dve.wait_ge(s_xl, k - 2)
                        dve.scalar_tensor_tensor(xt[k % 3], xT[:, k, :], gT[:, 8 * pre + k:8 * pre + k + 1],
                                                 rstd[:, :], ALU.mult, ALU.mult).then_inc(s_x, 1)
                        if k == 0:
                            rest_of_piece(0, 0)
                        else:
                            rest_of_x(k - 1)
                    rest_of_x(KD - 1)
                    rest_of_piece(1, 0)
                    for i in turns(dve, False, KF // 2):
                        for j in range(2):
                            c = 2 * i + j
                            last = known(c) and c == KF - 1
                            if not last:
                                rest_of_piece(0, c + 1)
                            dve.wait_ge(s_silu, c + 1)
                            dve.wait_ge(mm[1], c + 1)
                            if not known(c) or c >= 2:
                                dve.wait_ge(s_hl, c - 1)
                            dve.tensor_tensor(cut(tmp[j]), cut(silu[j]), both(4 * j + 2), ALU.mult).then_inc(s_prod, 1)
                            if not last:
                                rest_of_piece(1, c + 1)
                            dve.wait_ge(s_hh, c + 1)
                            row = bass.ds(c, 1)
                            dve.tensor_tensor(h.l[:, row, :].rearrange("p a n -> p (a n)"), tmp[j],
                                              h.h_f32[:, row, :].rearrange("p a n -> p (a n)"), ALU.subtract).then_inc(s_hl, 1)
            kp = KF // 2
            project_out(tag + "_out", w_out, KF, h, at(o - 6 * KD * P, KD, T), 0, o - 6 * KD * P + KD * T, post)
            assert 4 * kp * P <= 2 * KD * T

        O_OT = 0
        O_Q = O_OT + 16 * T
        O_NAT = O_Q + 8 * T
        O_SM = O_NAT + 3 * 5 * 512
        O_Z = O_SM + 5 * 64
        O_U = O_Z + 8 * T
        O_XP = O_U + KC_XBC * T
        O_END = O_XP + KC_XBC * XP
        oT, qT, nat, gdt = part("mixed", O_OT, 16, T), at(O_Q, 8, T), at(O_NAT, 3, 5, 512), at(O_SM, 5, 64)
        zT, uT, xp = at(O_Z, 8, T), at(O_U, KC_XBC, T), at(O_XP, KC_XBC, XP)
        w_in = io["w_in"].rearrange("a k n -> (a k) n").rearrange("(k p) n -> p k n", p=P)

        def mixer_in():
            xn = part("mk_xn_rows", O_U, KD, T)
            kvw = [at(O_XP, KD, 512), at(O_Z, KD, 512)]
            smw = at(O_U + KD * T, KD, 64)
            nrm = Norm("mix_pre", xT)
            xh = Split("mk_x", O_OT, KD, T)
            s_xn, s_h, s_xl = sem("mk_xn"), sem("mk_xh"), sem("mk_xl")
            land = [sem(f"mk_w{s}") for s in range(2)]
            s_sw, mm, ev, s_st, s_mm2, s_ev2 = (sem("mk_" + n) for n in ("sw", "mm", "ev", "st", "mm2", "ev2"))
            with nc.Block() as block:
                @block.sync
                def _(sp):
                    with nc.allow_non_contiguous_dma(reason="the narrow columns of gates and dt"):
                        sp.dma_start(smw[:, :, 0:48], w_in[:, :, COL_GATES:COL_GATES + 48]).then_inc(s_sw, 16)
                        sp.dma_start(smw[:, :, 48:64], w_in[:, :, COL_DT:COL_DT + 16]).then_inc(s_sw, 16)
                    for br in range(3):
                        if br == 2:
                            sp.wait_ge(mm, 5)
                        c0 = COL_KV + br * 512
                        sp.dma_start(kvw[br % 2], w_in[:, :, c0:c0 + 512]).then_inc(land[br % 2], 16)
                    for br in range(3):
                        sp.wait_ge(ev, 5 * br + 5)
                        pdst = [out["p_cmp_kv"], out["p_slc_kv"], out["p_win_kv"]][br]
                        sp.dma_start(pdst.rearrange("a b (i p) h c d -> p (a b i) (h c d)", p=P), nat[:, br, 0:4, :]).then_inc(s_out, 16)
                        if br < 2:
                            sdst = [out["s_cmp_kv"], out["s_slc_kv"]][br]
                            sp.dma_start(sdst.rearrange("a b t h c d -> (a b t) (h c d)"), nat[0:NS, br, 4, :]).then_inc(s_out, 16)
                        else:
                            for b in range(DEC_BATCH):
                                sp.dma_start(out["s_win_kv"][0, b, WINDOW - DEC_SEQ:WINDOW].rearrange("t h c d -> t (h c d)"),
                                               nat[b * 8:b * 8 + 8, 2, 4, :]).then_inc(s_out, 16)
                    sp.dma_start(out["s_win_kv"][0, :, 0:WINDOW - DEC_SEQ].rearrange("b t h c d -> b t (h c d)"),
                                   io["cache_win_kv"][0, :, DEC_SEQ:WINDOW].rearrange("b t h c d -> b t (h c d)")).then_inc(s_out, 16)
                    outs[0] += 3 + 2 + 8 + 1

                @block.tensor
                def _(pe):
                    nrm.total(pe)
                    pe.wait_ge(s_xn, KD)
                    pe.wait_ge(s_sw, 32)
                    for i, (t0, n) in enumerate(TILES):
                        for k in range(KD):
                            m = pe.matmul(PS[0:n, 6, i * 64:(i + 1) * 64], xn[:, k, t0:t0 + n], smw[:, k, :],
                                          start=(k == 0), stop=(k == KD - 1))
                    m.then_inc(s_mm2, 1)
                    u = 0
                    for br in range(3):
                        pe.wait_ge(land[br % 2], 16 * (br // 2 + 1))
                        for i, (t0, n) in enumerate(TILES):
                            if u >= 4:
                                pe.wait_ge(ev, u - 3)
                            for k in range(KD):
                                m = pe.matmul(PS[0:n, u % 4, :], xn[:, k, t0:t0 + n], kvw[br % 2][:, k, :],
                                              start=(k == 0), stop=(k == KD - 1))
                            m.then_inc(mm, 1)
                            u += 1

                @block.scalar
                def _(act):
                    for k in range(KD):
                        nrm.square(act, k)
                    nrm.take_root(act)
                    for k in range(KD):
                        act.wait_ge(s_xn, k + 1)
                        act.copy(xh.h[:, k, :], xn[:, k, :]).then_inc(s_h, 1)
                    u = 0
                    for br in range(3):
                        for i, (t0, n) in enumerate(TILES):
                            act.wait_ge(mm, u + 1)
                            act.copy(nat[0:n, br, i, :], PS[0:n, u % 4, :]).then_inc(ev, 1)
                            u += 1

                @block.vector
                def _(dve):
                    for k in range(1, KD):
                        nrm.add(dve, k)
                    nrm.invert(dve)
                    for k in range(KD):
                        dve.scalar_tensor_tensor(xn[:, k, :], xT[:, k, :], gT[:, 8 * GMPRE + k:8 * GMPRE + k + 1],
                                                 rstd[:, :], ALU.mult, ALU.mult).then_inc(s_xn, 1)
                    for k in range(KD):
                        dve.wait_ge(s_h, k + 1)
                        dve.tensor_tensor(xh.l[:, k, :], xn[:, k, :], xh.h_f32[:, k, :], ALU.subtract).then_inc(s_xl, 1)
                    dve.wait_ge(s_mm2, 1)
                    dve.tensor_copy(gdt[:, 0:4, :], PS[:, 6, 0:256].rearrange("p (i n) -> p i n", i=4)).then_inc(s_ev2, 1)
                    dve.tensor_copy(gdt[0:NS, 4, :], PS[0:NS, 6, 256:320]).then_inc(s_ev2, 1)

            ws = [Split(f"mq_w{s}", O_U + 2 * s * KD * P, KD, P) for s in range(2)]
            raw = [part(f"mq_raw{s}", O_U + (4 + s) * KD * P, KD, P) for s in range(2)]
            land_q, land, s_h, s_l, mm, ev = ([sem(f"mq_{n}{s}") for s in range(2)] for n in ("land_q", "land", "wh", "wl", "mm", "ev"))
            s_pad, s_in = sem("mq_pad"), sem("mq_in")
            stn = at(O_END, CONV_DIM)[0:24, :]
            s_tt, s_tc = sem("mq_tt"), sem("mq_tc")
            NC = 10
            with nc.Block() as block:
                @block.sync
                def _(sp):
                    with nc.allow_non_contiguous_dma(reason="rows of 256 bytes"):
                        for g in turns(sp, True, GQA):
                            for pair in range(2):
                                if not known(g):
                                    sp.wait_ge(s_l[pair], g)
                                for e in range(2):
                                    sp.dma_start(raw[pair][:, :, 64 * e:64 * e + 64],
                                                 w_in[:, :, bass.ds((8 * pair + 4 * e + g) * 64, 64)]).then_inc(land_q[pair], 16)
                    with sp.Fori(0, NC) as i:
                        for s in range(2):
                            sp.wait_ge(s_l[s], i + GQA)
                            sp.dma_start(raw[s], w_in[:, :, bass.ds(COL_Z + (2 * i + s) * P, P)]).then_inc(land[s], 16)

                @block.tensor
                def _(pe):
                    def chunk(s, n):
                        pe.wait_ge(s_l[s], n + 1)
                        if not (known(n) and n == 0):
                            pe.wait_ge(ev[s], n)
                        for k in range(KD):
                            m = product(pe, 2 * s, ws[s], k, xh, k, k == 0, k == KD - 1)
                        m.then_inc(mm[s], 1)
                    for g in turns(pe, True, GQA):
                        for s in range(2):
                            chunk(s, g)
                    pe.wait_ge(s_in, 16)
                    for k in range(KC_XBC):
                        m = pe.transpose(PS[:, 7, k * 24:(k + 1) * 24], stn[:, k * P:(k + 1) * P], ident[0:24, 0:24])
                    m.then_inc(s_tt, 1)
                    with pe.Fori(0, NC) as i:
                        for s in range(2):
                            chunk(s, i + GQA)

                @block.scalar
                def _(act):
                    act.dma_start(stn, io["state_conv"].rearrange("a b w n -> (a b w) n")).then_inc(s_in, 16)

                    def round_piece(s, n, land_sem, value):
                        act.wait_ge(land_sem, value)
                        if not (known(n) and n == 0):
                            act.wait_ge(mm[s], n)
                        act.copy(ws[s].h, raw[s]).then_inc(s_h[s], 1)
                    for g in turns(act, True, GQA):
                        for s in range(2):
                            round_piece(s, g, land_q[s], (g + 1) * 32)
                    with act.Fori(0, NC) as i:
                        for s in range(2):
                            round_piece(s, i + GQA, land[s], (i + 1) * 16)

                @block.vector
                def _(dve):
                    def rest_of_piece(s, n):
                        dve.wait_ge(s_h[s], n + 1)
                        dve.tensor_tensor(ws[s].l, raw[s], ws[s].h_f32, ALU.subtract).then_inc(s_l[s], 1)
                    for s in range(2):
                        rest_of_piece(s, 0)
                    dve.memset(xp[:, :, 0:PAD], 0.0).then_inc(s_pad, 1)
                    with dve.Fori(0, GQA) as g:
                        for s in range(2):
                            rest_of_piece(s, g + 1)
                            dve.wait_ge(mm[s], g + 1)
                            row = qT[:, bass.ds(4 * s + g, 1), :].rearrange("p a n -> p (a n)")
                            dve.tensor_scalar(cut(row), both(2 * s), SCALE, None, ALU.mult).then_inc(ev[s], 1)
                    dve.wait_ge(s_tt, 1)
                    runs = xp[:, :, XP_S:XP].rearrange("p k (b r) -> p k b r", r=XP_RUN)
                    for k in range(KC_XBC):
                        dve.tensor_copy(runs[:, k, :, 0:PAD],
                                        PS[:, 7, k * 24:(k + 1) * 24].rearrange("p (b w) -> p b w", w=PAD)).then_inc(s_tc, 1)
                    with dve.Fori(0, 4) as i:
                        for s in range(2):
                            rest_of_piece(s, i + (GQA + 1))
                            dve.wait_ge(mm[s], i + (GQA + 1))
                            row = zT[:, bass.ds(2 * i + s, 1), :].rearrange("p a n -> p (a n)")
                            dve.tensor_copy(cut(row), both(2 * s)).then_inc(ev[s], 1)

                    def xbc(i, s):
                        dve.wait_ge(mm[s], i + (GQA + 5))
                        row = xp[:, bass.ds(2 * i + s, 1), :].rearrange("p a n -> p (a n)")
                        rest = SEQ - HALF
                        dve.tensor_copy(row[:, PAD:PAD + HALF], PS[:, 2 * s, 0:HALF])
                        dve.tensor_copy(row[:, PAD + HALF:XP_S], PS[:, 2 * s + 1, 0:rest])
                        dve.tensor_copy(row[:, XP_S:XP].rearrange("p (b r) -> p b r", r=XP_RUN)[:, :, PAD:XP_RUN],
                                        PS[:, 2 * s + 1, rest:HALF].rearrange("p (b r) -> p b r", r=DEC_SEQ)).then_inc(ev[s], 1)
                    with dve.Fori(0, 5) as i:
                        for s in range(2):
                            rest_of_piece(s, i + (GQA + 5))
                            xbc(i, s)
                    for s in range(2):
                        xbc(5, s)

        def finish_out():
            ynat = at(0, 5, D_MODEL)
            mm, ev = sem("fo_mm"), sem("fo_ev")
            with nc.Block() as block:
                @block.tensor
                def _(pe):
                    u = 0
                    for i, (t0, n) in enumerate(TILES):
                        for q in range(2):
                            if u >= 4:
                                pe.wait_ge(ev, u - 3)
                            for j in range(4):
                                m = pe.transpose(PS[0:n, u % 4, j * P:(j + 1) * P], xT[:, 4 * q + j, t0:t0 + n], ident)
                            m.then_inc(mm, 1)
                            u += 1

                @block.vector
                def _(dve):
                    u = 0
                    for i, (t0, n) in enumerate(TILES):
                        for q in range(2):
                            dve.wait_ge(mm, u + 1)
                            dve.tensor_copy(ynat[0:n, i, 512 * q:512 * q + 512], PS[0:n, u % 4, :]).then_inc(ev, 1)
                            u += 1

                @block.sync
                def _(sp):
                    for i in range(5):
                        sp.wait_ge(ev, 2 * i + 2)
                        if i < 4:
                            sp.dma_start(out["y_prompt"][0, i * P:(i + 1) * P, :], ynat[:, i, :]).then_inc(s_out, 16)
                        else:
                            sp.dma_start(out["y_sample"].rearrange("b t d -> (b t) d"), ynat[0:NS, 4, :]).then_inc(s_out, 16)
                        outs[0] += 1
                    sp.wait_ge(s_out, 16 * outs[0])

        s_out = sem("outputs", True)
        outs = [0]
        def conv():
            cv = [at(O_END, XP), at(O_END + XP, XP)]
            last = at(O_END + 2 * XP, KC_XBC, 27)
            rows = at(O_OT + 8 * T, CONV_DIM)[0:27, :]
            s_cv, s_u, s_last, s_t, s_row, s_z = (sem("cv_" + n) for n in ("taps", "silu", "last", "t", "row", "z"))
            with nc.Block() as block:
                @block.vector
                def _(dve):
                    n = 0
                    for k0 in range(0, KC_XBC, 2):
                        for w in range(CONV_W):
                            for j in range(2):
                                k = k0 + j
                                o = cv[j][:, 0:CONV_N]
                                tap = convT[:, w * KC_XBC + k:w * KC_XBC + k + 1]
                                if w == 0:
                                    if k >= 2:
                                        dve.wait_ge(s_u, k - 1)
                                    ins = dve.tensor_scalar(o, xp[:, k, 0:CONV_N], tap,
                                                            convT[:, 4 * KC_XBC + k:4 * KC_XBC + k + 1], ALU.mult, ALU.add)
                                else:
                                    dve.wait_ge(s_cv, n - 1)
                                    ins = dve.scalar_tensor_tensor(o, xp[:, k, w:w + CONV_N], tap, o, ALU.mult, ALU.add)
                                ins.then_inc(s_cv, 1)
                                n += 1
                    dve.wait_ge(s_t, 1)
                    for b in range(3):
                        dve.tensor_copy(rows[:, 512 * b:512 * b + 512], PS[0:27, b, :]).then_inc(s_row, 1)

                @block.scalar
                def _(act):
                    for k in range(KC_XBC):
                        act.wait_ge(s_cv, 8 * (k // 2) + 7 + k % 2)
                        c = cv[k % 2]
                        act.activation(uT[:, k, 0:SEQ], c[:, 0:SEQ], ACT.Silu)
                        act.activation(uT[:, k, SEQ:T].rearrange("p (b t) -> p b t", t=DEC_SEQ),
                                       c[:, XP_S:XP].rearrange("p (b r) -> p b r", r=XP_RUN)[:, :, 0:DEC_SEQ],
                                       ACT.Silu).then_inc(s_u, 1)
                    act.activation(zT[:, :, :], zT[:, :, :], ACT.Silu).then_inc(s_z, 1)

                @block.gpsimd
                def _(pool):
                    pool.tensor_copy(last[:, :, 0:PAD], xp[:, :, XP_S - PAD:XP_S]).then_inc(s_last, 1)
                    pool.tensor_copy(last[:, :, PAD:27].rearrange("p k (b w) -> p k b w", w=PAD),
                                     xp[:, :, XP_S:XP].rearrange("p k (b r) -> p k b r", r=XP_RUN)[:, :, :, DEC_SEQ:XP_RUN]
                                     ).then_inc(s_last, 1)

                @block.tensor
                def _(pe):
                    pe.wait_ge(s_last, 2)
                    for k in range(KC_XBC):
                        m = pe.transpose(PS[0:27, k // 4, (k % 4) * P:(k % 4 + 1) * P], last[:, k, :], ident)
                    m.then_inc(s_t, 1)

                @block.sync
                def _(sp):
                    sp.wait_ge(s_row, 3)
                    sp.dma_start(out["p_conv"].rearrange("a b w n -> (a b w) n"), rows[0:PAD, :]).then_inc(s_out, 16)
                    sp.dma_start(out["s_conv"].rearrange("a b w n -> (a b w) n"), rows[PAD:27, :]).then_inc(s_out, 16)
                    outs[0] += 2
                    sp.wait_ge(s_out, 16 * outs[0])

        def ssd():
            o = O_XP
            xdt = at(o, N_HEADS, HD)
            xe = at(o + 1024, N_HEADS, HD)
            larep = at(o + 2048, N_HEADS, HD)
            mb = [at(o + 3072, 4, P), at(o + 3584, 4, P)]
            ecs = at(o + 4096, 8, P)
            st = at(o + 5120, N_HEADS, HD)
            bnat = at(o + 6144, 2, P)
            cbm = at(o + 6400, 2, P)
            yt = at(o + 6656, 2, 512)
            bm = at(o + 7680, 2, 256)
            dtv = at(o + 8192, 7, 80)
            ted = at(o + 8752, 2, 16)
            nla = at(o + 8784, 80)
            h0 = [at(O_OT + 1024 * s, 8, P) for s in range(3)]
            h0t = at(O_OT + 3072, 8, P)
            names = ("dch", "ach", "la", "xs", "small", "cb", "cs", "diff", "yoff", "yd", "st", "lar", "xdt", "bn", "cbm",
                     "mn", "mm", "xe", "y", "sup", "te", "ecs", "ee", "h0t", "h0c", "new", "bmk", "hn",
                     "pst", "psc", "e", "l")
            S = {n: sem("ss_" + n) for n in names}
            s_h0 = [sem(f"ss_h0_{s}") for s in range(3)]
            s_ho = [sem(f"ss_ho_{s}") for s in range(3)]
            NC = len(TILES)
            states = io["state_ssm"].rearrange("a b (k e) p n -> (a b) (e p) k n", e=2)
            s_states = out["s_ssm"].rearrange("a b (k e) p n -> (a b) (e p) k n", e=2)

            with nc.Block() as block:
                @block.sync
                def _(sp):
                    for b in range(DEC_BATCH):
                        if b >= 3:
                            sp.wait_ge(s_ho[b % 3], 16 * (b // 3))
                        sp.dma_start(h0[b % 3], states[b]).then_inc(s_h0[b % 3], 16)
                        if b >= 1:
                            sp.wait_ge(S["hn"], b)
                            sp.dma_start(s_states[b - 1], h0[(b - 1) % 3]).then_inc(s_ho[(b - 1) % 3], 16)
                    sp.wait_ge(S["hn"], DEC_BATCH)
                    sp.dma_start(s_states[DEC_BATCH - 1], h0[(DEC_BATCH - 1) % 3]).then_inc(s_ho[(DEC_BATCH - 1) % 3], 16)
                    for s in range(3):
                        sp.wait_ge(s_ho[s], 16 * ((DEC_BATCH + 2 - s) // 3))
                    sp.wait_ge(S["psc"], 2)
                    sp.dma_start(out["p_ssm"][0, 0].rearrange("(k e) p n -> (e p) k n", e=2), h0[0]).then_inc(s_out, 16)
                    outs[0] += 1
                    sp.wait_ge(s_out, 16 * outs[0])

                @block.tensor
                def _(pe):
                    pe.wait_ge(S["la"], 2)
                    for c, (t0, n) in enumerate(TILES):
                        sample = c == NC - 1
                        tri = sq6[0:n, BTRI if sample else TRI, 0:n]
                        one = sq6[0:n, BONES if sample else ONES, 0:n]
                        la = dtv[0:n, 6, 16 * c:16 * c + 16]
                        if c:
                            pe.wait_ge(S["y"], 2 * c)
                            pe.wait_ge(S["sup"], 2 * c)
                        for k in range(8):
                            pe.transpose(PS[0:n, k // 4, (k % 4) * P:(k % 4 + 1) * P], uT[:, k, t0:t0 + n], ident)
                        for g in range(2):
                            m = pe.transpose(PS[0:n, 2, g * P:(g + 1) * P], uT[:, 8 + g, t0:t0 + n], ident)
                        m.then_inc(S["xs"], 1)
                        pe.matmul(PS[0:n, 2, 256:272], one, la, start=True, stop=True)
                        pe.matmul(PS[0:n, 2, 272:288], tri, la, start=True, stop=True).then_inc(S["small"], 1)
                        for g in range(2):
                            m = pe.matmul(PS[0:n, 3, g * P:g * P + n], uT[:, 8 + g, t0:t0 + n], uT[:, 10 + g, t0:t0 + n],
                                          start=True, stop=True)
                        m.then_inc(S["cb"], 1)
                        pe.wait_ge(S["lar"], c + 1)
                        for k in range(8):
                            if k % 4 == 0 and c:
                                pe.wait_ge(S["mn"], 4 * c - 1 + k // 4)
                            m = pe.matmul(PS[:, 4 + k // 4, (k % 4) * P:(k % 4) * P + n],
                                          larep[0:n, 2 * k:2 * k + 2, :].rearrange("p a b -> p (a b)"), tri, start=True, stop=True)
                            if k % 4 == 3:
                                m.then_inc(S["cs"], 1)
                        for q in range(4):
                            if q < 2:
                                pe.wait_ge(S["ecs"], 2 * c + q + 1)
                            else:
                                pe.wait_ge(S["mn"], 4 * c + q - 1)
                            bank = 4 + q % 2
                            for j in range(4):
                                pe.matmul(PS[0:n, bank, j * P:j * P + n], dtv[0:n, 6, 16 * c + 4 * q + j:16 * c + 4 * q + j + 1]
                                          .to_broadcast([n, n]), tri, start=True, stop=False)
                                m = pe.matmul(PS[0:n, bank, j * P:j * P + n], tri,
                                              nla[0:n, 16 * c + 4 * q + j:16 * c + 4 * q + j + 1].to_broadcast([n, n]),
                                              start=False, stop=True)
                            m.then_inc(S["diff"], 1)
                        if not sample:
                            pe.wait_ge(S["xdt"], c + 1)
                            if c == 0:
                                pe.wait_ge(S["e"], 1)
                            for k in range(8):
                                m = pe.matmul(PS[:, k // 4, (k % 4) * P:(k % 4) * P + n],
                                              st[:, 2 * k:2 * k + 2, :].rearrange("p a b -> p (a b)"),
                                              uT[:, 10 + k // 4, t0:t0 + n], start=True, stop=True)
                            m.then_inc(S["yoff"], 1)
                        pe.wait_ge(S["xdt"], c + 1)
                        for q in range(4):
                            pe.wait_ge(S["mm"], 4 * c + q + 1)
                            for j in range(4):
                                h = 4 * q + j
                                m = pe.matmul(PS[64 * (h % 2):64 * (h % 2) + 64, 6 + h // 8, (h // 2 % 4) * P:(h // 2 % 4) * P + n],
                                              xdt[0:n, h, :], mb[q % 2][0:n, j, 0:n], start=True, stop=True)
                            m.then_inc(S["yd"], 1)
                        pe.wait_ge(S["xe"], c + 1)
                        if not sample:
                            pe.wait_ge(S["bn"], c + 1)
                            pe.wait_ge(S["te"], c + 1)
                            pe.wait_ge(S["cbm"], c + 1)
                            for g in range(2):
                                m = pe.matmul(PS[:, 2 + g, :], bnat[0:n, g, :],
                                              xe[0:n, 8 * g:8 * g + 8, :].rearrange("p a b -> p (a b)"), start=True, stop=True)
                            m.then_inc(S["st"], 1)
                    n = NS
                    pe.wait_ge(S["cbm"], NC)
                    for b in range(DEC_BATCH):
                        pe.wait_ge(s_h0[b % 3], 16 * (b // 3 + 1))
                        if b == 0:
                            pe.wait_ge(S["mn"], 4 * NC)
                        else:
                            pe.wait_ge(S["h0c"], 2 * b)
                        for k in range(8):
                            m = pe.transpose(PS[:, 4 + k // 4, (k % 4) * P:(k % 4 + 1) * P], h0[b % 3][:, k, :], ident)
                        m.then_inc(S["h0t"], 1)
                        pe.wait_ge(S["bmk"], b + 1)
                        if b:
                            pe.wait_ge(S["hn"], b)
                        for k in range(8):
                            m = pe.matmul(PS[:, 2 + k // 4, (k % 4) * P:(k % 4 + 1) * P],
                                          xe[0:n, 2 * k:2 * k + 2, :].rearrange("p a b -> p (a b)"),
                                          bm[0:n, b % 2, (k // 4) * P:(k // 4 + 1) * P], start=True, stop=True)
                        m.then_inc(S["new"], 1)
                        pe.wait_ge(S["h0c"], 2 * b + 2)
                        for k in range(8):
                            m = pe.matmul(PS[:, k // 4, (k % 4) * P + 8 * b:(k % 4) * P + 8 * b + 8], h0t[:, k, :],
                                          uT[:, 10 + k // 4, SEQ + 8 * b:SEQ + 8 * b + 8], start=True, stop=True)
                        m.then_inc(S["yoff"], 1)
                    for k in range(8):
                        m = pe.transpose(PS[:, 4 + k // 4, (k % 4) * P:(k % 4 + 1) * P],
                                         st[:, 2 * k:2 * k + 2, :].rearrange("p a b -> p (a b)"), ident)
                    m.then_inc(S["pst"], 1)

                @block.scalar
                def _(act):
                    act.wait_ge(S["l"], 1)
                    act.activation(dtv[:, 2, :], dtv[:, 1, :], ACT.Exp, scale=-1.0).then_inc(S["ach"], 1)
                    act.wait_ge(S["l"], 2)
                    act.activation(dtv[:, 4, :], dtv[:, 3, :], ACT.Ln).then_inc(S["ach"], 1)
                    for c, (t0, n) in enumerate(TILES):
                        act.wait_ge(S["bn"], c + 1)
                        act.activation(ted[0:n, :, :], ted[0:n, :, :], ACT.Exp).then_inc(S["te"], 1)
                        for g in range(2):
                            act.wait_ge(S["cs"], 2 * c + g + 1)
                            act.activation(ecs[:, 4 * g:4 * g + 4, 0:n],
                                           PS[:, 4 + g, :].rearrange("p (a n) -> p a n", a=4)[:, :, 0:n], ACT.Exp).then_inc(S["ecs"], 1)
                        for q in range(4):
                            act.wait_ge(S["mn"], 4 * c + q + 1)
                            act.activation(mb[q % 2][0:n, :, 0:n], mb[q % 2][0:n, :, 0:n], ACT.Exp).then_inc(S["ee"], 1)
                    for b in range(DEC_BATCH):
                        act.wait_ge(S["h0t"], b + 1)
                        if b:
                            act.wait_ge(S["yoff"], NC - 1 + b)
                        for g in range(2):
                            act.copy(h0t[:, 4 * g:4 * g + 4, :].rearrange("p a b -> p (a b)"), PS[:, 4 + g, :]).then_inc(S["h0c"], 1)

                @block.vector
                def _(dve):
                    ch = Chain(dve, S["dch"])
                    sm = gdt[:, :, 48:64]
                    v = lambda k: dtv[:, k, :].rearrange("p (c h) -> p c h", c=NC)
                    ch.link(dve.memset(gdt[64:P, 4, :], 0.0))
                    dve.memset(st[:, :, :], 0.0).then_inc(S["e"], 1)
                    ch.link(dve.tensor_tensor(v(0), sm, small[:, 0:1, :].to_broadcast([P, NC, 16]), ALU.add))
                    dve.scalar_tensor_tensor(v(1), v(0), -1.0, v(0), ALU.mult, ALU.max).then_inc(S["l"], 1)
                    dve.wait_ge(S["ach"], 1)
                    dve.tensor_scalar(dtv[:, 3, :], dtv[:, 2, :], 1.0, None, ALU.add).then_inc(S["l"], 1)
                    dve.wait_ge(S["ach"], 2)
                    ch.link(dve.tensor_scalar(dtv[:, 1, :], dtv[:, 3, :], -1.0, None, ALU.add))
                    ch.link(dve.tensor_tensor(dtv[:, 4, :], dtv[:, 4, :], dtv[:, 2, :], ALU.mult))
                    ch.link(dve.scalar_tensor_tensor(dtv[:, 2, :], dtv[:, 1, :], 0.0, dtv[:, 2, :], ALU.is_equal, ALU.mult))
                    ch.link(dve.tensor_scalar(dtv[:, 1, :], dtv[:, 1, :], 1e-30, None, ALU.max))
                    ch.link(dve.reciprocal(dtv[:, 1, :], dtv[:, 1, :]))
                    ch.link(dve.tensor_tensor(dtv[:, 4, :], dtv[:, 4, :], dtv[:, 1, :], ALU.mult))
                    ch.link(dve.tensor_tensor(dtv[:, 4, :], dtv[:, 4, :], dtv[:, 2, :], ALU.add))
                    ch.link(dve.scalar_tensor_tensor(dtv[:, 5, :], dtv[:, 0, :], 0.0, dtv[:, 4, :], ALU.max, ALU.add))
                    dve.tensor_tensor(v(6), v(5), small[:, 2:3, :].to_broadcast([P, NC, 16]), ALU.mult).then_inc(S["la"], 1)
                    dve.wait_ge(S["la"], 1)
                    dve.tensor_scalar(nla[:, :], dtv[:, 6, :], -1.0, None, ALU.mult).then_inc(S["la"], 1)
                    for c, (t0, n) in enumerate(TILES):
                        sample = c == NC - 1
                        tri = sq6[0:n, BTRI if sample else TRI, 0:n]
                        dt = dtv[0:n, 5, 16 * c:16 * c + 16]
                        if c:
                            dve.wait_ge(S["cs"], 2 * c)
                        dve.tensor_copy(larep[0:n, :, :], dtv[0:n, 6, 16 * c:16 * c + 16].unsqueeze(2).to_broadcast([n, 16, 64])
                                        ).then_inc(S["lar"], 1)
                        dve.wait_ge(S["xs"], c + 1)
                        for g in range(2):
                            ins = dve.tensor_tensor(xdt[0:n, 8 * g:8 * g + 8, :], PS[0:n, g, :].rearrange("p (h d) -> p h d", d=HD),
                                                    dt[:, 8 * g:8 * g + 8].unsqueeze(2).to_broadcast([n, 8, 64]), ALU.mult)
                        ins.then_inc(S["xdt"], 1)
                        dve.wait_ge(S["small"], c + 1)
                        ch.link(dve.tensor_copy(bnat[0:n, :, :], PS[0:n, 2, 0:256].rearrange("p (g n) -> p g n", g=2)))
                        if c:
                            dve.wait_ge(S["sup"], 2 * c)
                        ch.link(dve.tensor_copy(ted[0:n, 0, :], PS[0:n, 2, 256:272]))
                        dve.tensor_tensor(ted[0:n, 1, :], ted[0:n, 0, :], PS[0:n, 2, 272:288], ALU.subtract).then_inc(S["bn"], 1)
                        dve.wait_ge(S["cb"], c + 1)
                        dve.tensor_tensor(cbm[0:n, :, 0:n], PS[0:n, 3, 0:256].rearrange("p (g n) -> p g n", g=2)[:, :, 0:n],
                                          tri.unsqueeze(1).to_broadcast([n, 2, n]), ALU.mult).then_inc(S["cbm"], 1)

                        def gate(q):
                            dve.wait_ge(S["ee"], 4 * c + q + 1)
                            dve.wait_ge(S["cbm"], c + 1)
                            dve.tensor_tensor(mb[q % 2][0:n, :, 0:n], mb[q % 2][0:n, :, 0:n],
                                              cbm[0:n, q // 2, 0:n].unsqueeze(1).to_broadcast([n, 4, n]), ALU.mult).then_inc(S["mm"], 1)
                        for q in range(4):
                            dve.wait_ge(S["diff"], 4 * c + q + 1)
                            if 4 * c + q >= 2:
                                dve.wait_ge(S["yd"], 4 * c + q - 1)
                            dve.tensor_scalar(mb[q % 2][0:n, :, 0:n],
                                              PS[0:n, 4 + q % 2, :].rearrange("p (a n) -> p a n", a=4)[:, :, 0:n],
                                              0.0, None, ALU.min).then_inc(S["mn"], 1)
                            if q:
                                gate(q - 1)
                        dve.wait_ge(S["te"], c + 1)
                        dve.wait_ge(S["xdt"], c + 1)
                        dve.tensor_tensor(xe[0:n, :, :], xdt[0:n, :, :], ted[0:n, 1, :].unsqueeze(2).to_broadcast([n, 16, 64]),
                                          ALU.mult).then_inc(S["xe"], 1)
                        gate(3)
                        if sample:
                            for b in range(DEC_BATCH):
                                if b >= 2:
                                    dve.wait_ge(S["new"], b - 1)
                                dve.tensor_scalar(bm[0:n, b % 2, :], bnat[0:n, :, :].rearrange("p a b -> p (a b)"),
                                                  crow[0:n, 2, b:b + 1], None, ALU.mult).then_inc(S["bmk"], 1)
                                dve.wait_ge(S["new"], b + 1)
                                dve.wait_ge(S["h0t"], b + 1)
                                dve.wait_ge(S["ecs"], 2 * NC)
                                for k in range(8):
                                    ins = dve.scalar_tensor_tensor(
                                        h0[b % 3][:, k, :], h0[b % 3][:, k, :], ecs[:, k, 8 * b + 7:8 * b + 8],
                                        PS[:, 2 + k // 4, (k % 4) * P:(k % 4 + 1) * P], ALU.mult, ALU.add)
                                ins.then_inc(S["hn"], 1)
                            dve.wait_ge(S["yoff"], NC - 1 + DEC_BATCH)
                        else:
                            dve.wait_ge(S["yoff"], c + 1)
                        for g in range(2):
                            dve.wait_ge(S["ecs"], 2 * c + g + 1)
                            yv = yt[:, g, :].rearrange("p (a n) -> p a n", a=4)[:, :, 0:n]
                            ch.link(dve.tensor_tensor(yv, PS[:, g, :].rearrange("p (a n) -> p a n", a=4)[:, :, 0:n],
                                                      ecs[:, 4 * g:4 * g + 4, 0:n], ALU.mult))
                            dve.wait_ge(S["yd"], 4 * c + 2 * g + 2)
                            ch.link(dve.tensor_tensor(yv, yv, PS[:, 6 + g, :].rearrange("p (a n) -> p a n", a=4)[:, :, 0:n], ALU.add))
                            for j in range(4):
                                k = 4 * g + j
                                ins = dve.scalar_tensor_tensor(oT[:, 8 + k, t0:t0 + n], uT[:, k, t0:t0 + n], small[:, 3, k:k + 1],
                                                               yv[:, j, :], ALU.mult, ALU.add)
                            ins.then_inc(S["y"], 1)
                        if not sample:
                            dve.wait_ge(S["te"], c + 1)
                            dve.wait_ge(S["e"], 1)
                            if c:
                                dve.wait_ge(S["sup"], 2 * c)
                            ch.link(dve.tensor_tensor(st[:, :, :], st[:, :, :], ted[:, 0, :].unsqueeze(2).to_broadcast([P, 16, 64]),
                                                      ALU.mult))
                            dve.wait_ge(S["st"], c + 1)
                            for g in range(2):
                                sv = st[:, 8 * g:8 * g + 8, :].rearrange("p a b -> p (a b)")
                                dve.tensor_tensor(sv, sv, PS[:, 2 + g, :], ALU.add).then_inc(S["sup"], 1)
                    dve.wait_ge(S["pst"], 1)
                    dve.wait_ge(s_ho[0], 16 * ((DEC_BATCH + 2) // 3))
                    for g in range(2):
                        dve.tensor_copy(h0[0][:, 4 * g:4 * g + 4, :].rearrange("p a b -> p (a b)"), PS[:, 4 + g, :]).then_inc(S["psc"], 1)

        def ssd_gate_norm():
            s_g, s_sq, s_use, s_root, s_r, s_f = (sem("sn_" + n) for n in ("g", "sq", "use", "root", "r", "f"))
            gs = [at(O_XP, T), at(O_XP + T, T)]
            with nc.Block() as block:
                @block.vector
                def _(dve):
                    for k in range(8):
                        dve.tensor_tensor(oT[:, 8 + k, :], oT[:, 8 + k, :], zT[:, k, :], ALU.mult).then_inc(s_g, 1)
                    for g in range(2):
                        dve.wait_ge(s_root, 2 * g + 2)
                        dve.reciprocal(gs[g], gs[g]).then_inc(s_r, 1)
                        dve.wait_ge(s_r, g + 1)
                        for k in range(4 * g, 4 * g + 4):
                            dve.scalar_tensor_tensor(oT[:, 8 + k, :], oT[:, 8 + k, :], gT[:, 8 * GSSD + k:8 * GSSD + k + 1],
                                                     gs[g], ALU.mult, ALU.mult).then_inc(s_f, 1)

                @block.scalar
                def _(act):
                    for k in range(8):
                        act.wait_ge(s_g, k + 1)
                        if k >= 2:
                            act.wait_ge(s_use, k - 1)
                        act.activation(sqr[:, k % 2, :], oT[:, 8 + k, :], ACT.Square,
                                       scale=(SSD_INNER // SSD_GROUPS) ** -0.5).then_inc(s_sq, 1)
                    for g in range(2):
                        act.wait_ge(s_use, 4 * g + 4)
                        act.activation(gs[g][:, 0:SEQ], PS[:, 2 * g, :], ACT.Sqrt, bias=eps_sb[:, 0:1]).then_inc(s_root, 1)
                        act.activation(gs[g][:, SEQ:T], PS[:, 2 * g + 1, 0:NS], ACT.Sqrt, bias=eps_sb[:, 0:1]).then_inc(s_root, 1)

                @block.tensor
                def _(pe):
                    for k in range(8):
                        pe.wait_ge(s_sq, k + 1)
                        g = k // 4
                        pe.matmul(PS[:, 2 * g, :], sq6[:, ONES, :], sqr[:, k % 2, 0:SEQ], start=(k % 4 == 0), stop=(k % 4 == 3))
                        pe.matmul(PS[:, 2 * g + 1, 0:NS], sq6[:, ONES, :], sqr[:, k % 2, SEQ:T], start=(k % 4 == 0),
                                  stop=(k % 4 == 3)).then_inc(s_use, 1)

        O_ON = O_Z
        O_SG = O_ON + 5 * ATT_WIDTH
        O_KTN = O_SG + 5 * 48
        O_FREE = O_KTN + 256
        onat, sg, ktn = at(O_ON, 5, ATT_WIDTH), at(O_SG, 5, 48), at(O_KTN, 2, 2, NS)

        def kt_transposes(pe, bank, rows, row0=0):
            for h in range(N_KV):
                c0 = h * P - (HD if h % 2 else 0)
                m = pe.transpose(PS[:, bank, h * P:h * P + rows.shape[0]], rows[:, c0:c0 + P], ident[0:rows.shape[0], 0:rows.shape[0]])
            return m

        def kt_halves(bank, n):
            v = PS[:, bank, :].rearrange("p (a e n) -> p a e n", a=2, e=2)
            return v[0:64, :, 0, 0:n], v[64:P, :, 1, 0:n]

        def compress_prompt():
            o = O_FREE
            ktp = at(o, 2, 2, SEQ)
            o += 2048
            wc = [at(o + 2048 * s, 32, HD) for s in range(2)]
            ckp = at(o + 4096, 2, N_KV, 4)
            kcp = at(o + 5600, 2, 2, 8)
            vtmp = at(o + 4160, P)
            vbd = at(o + 4288, 16 * HD)
            sc = at(o + 5312, N_HEADS, 8)
            mx = at(o + 5440, 2, 16)
            pT = at(o + 5472, P)
            wl = [sem(f"pc_w{s}") for s in range(2)]
            names = ("mm", "ck", "kc", "t", "vt", "z", "vb", "kt", "ktc", "s", "x", "e", "p", "pt", "ptc", "o", "oc", "dch", "sg")
            S = {n: sem("pc_" + n) for n in names}
            w = io["w_cmp"].rearrange("a l c d e -> (a l) (c d) e")
            with nc.Block() as block:
                @block.sync
                def _(sp):
                    for q in range(4):
                        if q >= 2:
                            sp.wait_ge(S["mm"], q - 1)
                        for half in range(2):
                            sp.dma_start(wc[q % 2][64 * half:64 * half + 64, :, :], w[:, 32 * q:32 * q + 32, :]).then_inc(wl[q % 2], 16)
                    sp.wait_ge(S["ck"], 2)
                    sp.wait_ge(S["z"], 2)
                    for half in range(2):
                        for odd in range(2):
                            sp.dma_start(kcp[64 * odd:64 * odd + 64, :, odd, 4 * half:4 * half + 4],
                                         ckp[64 * half:64 * half + 64, 0, :, :].rearrange("p (a b) n -> p a b n", b=2)[:, :, odd, :]
                                         ).then_inc(S["kc"], 16)
                    sp.wait_ge(S["vt"], 1)
                    for h in range(N_HEADS):
                        for half in range(2):
                            sp.dma_start(vbd[8 * h + 4 * half:8 * h + 4 * half + 4, HD * h:HD * h + HD],
                                         vtmp[4 * (h // GQA):4 * (h // GQA) + 4, 64 * half:64 * half + 64]).then_inc(S["vb"], 16)

                @block.gpsimd
                def _(pool):
                    pool.memset(kcp[:, :, :, :], 0.0).then_inc(S["z"], 1)
                    pool.memset(vbd, 0.0).then_inc(S["z"], 1)

                @block.tensor
                def _(pe):
                    u = 0
                    for br in range(2):
                        for i, (t0, n) in enumerate(TILES):
                            if u >= 2:
                                pe.wait_ge(S["ktc"], 2 * (u - 1))
                            kt_transposes(pe, 4 + u % 2, nat[0:n, 1 + br, i, :]).then_inc(S["kt"], 1)
                            u += 1
                    for q in range(4):
                        pe.wait_ge(wl[q % 2], 32 * (q // 2 + 1))
                        for j in range(32):
                            c, d = (32 * q + j) // 64, (32 * q + j) % 64
                            for half in range(2):
                                base = nat[64 * half:64 * half + 64, 0, 0:4, :]
                                rhs = bass.AP(base.tensor, base.offset + c * 64 + d, [base.ap[0], [P, 16]])
                                m = pe.matmul(PS[64 * half:64 * half + 64, c, 0:16], wc[q % 2][64 * half:64 * half + 64, j, :], rhs,
                                              start=(d == 0), stop=(d == 63))
                        m.then_inc(S["mm"], 1)
                    pe.wait_ge(S["ck"], 2)
                    pe.transpose(PS[0:16, 2, 0:P], ckp[:, 1, :, :].rearrange("p a b -> p (a b)"), ident).then_inc(S["t"], 1)
                    pe.wait_ge(S["kc"], 64)
                    for i in range(4):
                        if i:
                            pe.wait_ge(S["x"], i)
                        sv = PS[:, 3, 0:P].rearrange("p (a e g n) -> p a e g n", a=2, e=2, g=GQA)
                        for c in range(8):
                            m = pe.matmul(sv[:, c // GQA, :, c % GQA, :], qT[:, c, i * P:(i + 1) * P], kcp[:, c // GQA, :, :],
                                          start=True, stop=True)
                        m.then_inc(S["s"], 1)
                        pe.wait_ge(S["p"], i + 1)
                        pe.transpose(PS[:, 2, 0:P], sc[:, :, :].rearrange("p a b -> p (a b)"), ident).then_inc(S["pt"], 1)
                        pe.wait_ge(S["ptc"], i + 1)
                        pe.wait_ge(S["vb"], 16 * 32)
                        if i == 0:
                            pe.wait_ge(S["ck"], 2)
                        else:
                            pe.wait_ge(S["oc"], 2 * i)
                        for g in range(2):
                            m = pe.matmul(PS[:, g, :], pT, vbd[:, 512 * g:512 * g + 512], start=True, stop=True)
                        m.then_inc(S["o"], 1)

                @block.scalar
                def _(act):
                    act.activation(sg[:, :, :], gdt[:, :, 0:48], ACT.Sigmoid).then_inc(S["sg"], 1)
                    u = 0
                    for br in range(2):
                        for i, (t0, n) in enumerate(TILES):
                            act.wait_ge(S["kt"], u + 1)
                            lo, hi = kt_halves(4 + u % 2, n)
                            dst = ktp[:, br, :, t0:t0 + n] if i < 4 else ktn[:, br, :, :]
                            act.copy(dst[0:64], lo).then_inc(S["ktc"], 1)
                            act.copy(dst[64:P], hi).then_inc(S["ktc"], 1)
                            u += 1
                    for i in range(4):
                        act.wait_ge(S["x"], i + 1)
                        act.activation(sc[:, :, :], sc[:, :, :], ACT.Exp).then_inc(S["e"], 1)
                        act.wait_ge(S["pt"], i + 1)
                        if i:
                            act.wait_ge(S["o"], i)
                        act.copy(pT, PS[:, 2, 0:P]).then_inc(S["ptc"], 1)
                        act.wait_ge(S["o"], i + 1)
                        for g in range(2):
                            act.copy(onat[:, i, 512 * g:512 * g + 512], PS[:, g, :]).then_inc(S["oc"], 1)

                @block.vector
                def _(dve):
                    ch = Chain(dve, S["dch"])
                    dve.wait_ge(S["mm"], 4)
                    for c in range(2):
                        dve.tensor_scalar(ckp[:, c, :, :], PS[:, c, 0:16].rearrange("p (n h) -> p h n", h=N_KV),
                                          pe_c[:, c:c + 1], None, ALU.add).then_inc(S["ck"], 1)
                    dve.wait_ge(S["t"], 1)
                    dve.tensor_copy(vtmp[0:16, :], PS[0:16, 2, 0:P]).then_inc(S["vt"], 1)
                    for i in range(4):
                        dve.wait_ge(S["s"], i + 1)
                        if i:
                            dve.wait_ge(S["pt"], i)
                        ch.link(dve.tensor_tensor(sc[:, :, :], PS[:, 3, 0:P].rearrange("p (h n) -> p h n", h=16), bias_cmp[:, i, :, :], ALU.add))
                        ch.link(dve.tensor_reduce(mx[:, 0, :], sc[:, :, :], AXX, ALU.max))
                        ch.link(dve.tensor_scalar(mx[:, 0, :], mx[:, 0, :], 0.1 * MASKED, None, ALU.max))
                        dve.tensor_tensor(sc[:, :, :], sc[:, :, :], mx[:, 0, :].unsqueeze(2).to_broadcast([P, 16, 8]),
                                          ALU.subtract).then_inc(S["x"], 1)
                        dve.wait_ge(S["e"], i + 1)
                        ch.link(dve.tensor_reduce(mx[:, 1, :], sc[:, :, :], AXX, ALU.add))
                        ch.link(dve.tensor_scalar(mx[:, 1, :], mx[:, 1, :], 1e-30, None, ALU.max))
                        ch.link(dve.reciprocal(mx[:, 1, :], mx[:, 1, :]))
                        dve.wait_ge(S["sg"], 1)
                        ch.link(dve.tensor_tensor(mx[:, 1, :], mx[:, 1, :], sg[:, i, :].rearrange("p (h r) -> p h r", r=3)[:, :, 0], ALU.mult))
                        dve.tensor_tensor(sc[:, :, :], sc[:, :, :], mx[:, 1, :].unsqueeze(2).to_broadcast([P, 16, 8]),
                                          ALU.mult).then_inc(S["p"], 1)

        def attend_prompt():
            o = O_FREE
            ktp = at(o, 2, 2, SEQ)
            o += 2048
            mh = at(o, N_KV, SEQ)
            qg = at(o + 2048, 2, SEQ)
            Sx = [at(o + 3072 + 512 * s, SEQ) for s in range(3)]
            PT = [at(o + 4608 + 512 * s, SEQ) for s in range(2)]
            st = at(o + 5632, 4, 4)
            spare = at(o + 5648, 1)
            units = [(kv, br, i) for kv in range(N_KV) for br in range(2) for i in range(4)]
            NU = len(units)
            names = ("qg", "s", "x", "nm", "e", "t", "pt", "o", "b", "d1", "d2", "d3")
            S = {n: sem("pa_" + n) for n in names}
            s_mh = [sem(f"pa_mh{kv}") for kv in range(N_KV)]
            with nc.Block() as block:
                @block.sync
                def _(sp):
                    for g in range(GQA):
                        for kv in range(N_KV):
                            if g:
                                sp.wait_ge(S["x"], NU * (g - 1) + 8 * (kv + 1))
                            sp.dma_start(mh[:, kv, :], bass.AP(scr_t, (4 * kv + g) * P * LEN_T + P - 1, [[LEN_T - 1, P], [1, SEQ]])
                                         ).then_inc(s_mh[kv], 16)

                @block.tensor
                def _(pe):
                    with pe.Fori(0, GQA) as g:
                        base = g * NU

                        def scores(u):
                            kv, br, i = units[u]
                            r, n = 64 * (kv % 2), (i + 1) * P
                            if u >= 2:
                                pe.wait_ge(S["x"], base + u - 1)
                            pe.matmul(PS[:, u % 2, 0:n], qg[r:r + 64, kv // 2, i * P:(i + 1) * P], ktp[r:r + 64, br, kv // 2, 0:n],
                                      start=True, stop=True).then_inc(S["s"], 1)

                        def values(u):
                            kv, br, i = units[u]
                            pe.wait_ge(S["pt"], base + u + 1)
                            if u >= 2:
                                pe.wait_ge(S["b"], base + u)
                            for j in range(i + 1):
                                m = pe.matmul(PS[:, 4 + u % 2, 0:HD], PT[u % 2][:, j * P:(j + 1) * P],
                                              nat[:, 1 + br, j, kv * P + HD:(kv + 1) * P], start=(j == 0), stop=(j == i))
                            m.then_inc(S["o"], 1)
                        pe.wait_ge(S["qg"], g + 1)
                        scores(0)
                        for u in range(NU):
                            if u + 1 < NU:
                                scores(u + 1)
                            pe.wait_ge(S["e"], base + u + 1)
                            if u >= 2:
                                pe.wait_ge(S["pt"], base + u - 1)
                            for j in range(units[u][2] + 1):
                                m = pe.transpose(PS[:, 2 + u % 2, j * P:(j + 1) * P], Sx[u % 3][:, j * P:(j + 1) * P], ident)
                            m.then_inc(S["t"], 1)
                            if u:
                                values(u - 1)
                        values(NU - 1)

                @block.scalar
                def _(act):
                    with act.Fori(0, GQA) as g:
                        base = g * NU

                        def to_sbuf(u):
                            n = (units[u][2] + 1) * P
                            act.wait_ge(S["t"], base + u + 1)
                            if u >= 2:
                                act.wait_ge(S["o"], base + u - 1)
                            act.copy(PT[u % 2][:, 0:n], PS[:, 2 + u % 2, 0:n]).then_inc(S["pt"], 1)
                        for u in range(NU):
                            n = (units[u][2] + 1) * P
                            act.wait_ge(S["nm"], base + u + 1)
                            act.activation(Sx[u % 3][:, 0:n], Sx[u % 3][:, 0:n], ACT.Exp, bias=st[:, u % 4, 1:2],
                                           accum_out=st[:, u % 4, 2:3]).then_inc(S["e"], 1)
                            if u:
                                to_sbuf(u - 1)
                        to_sbuf(NU - 1)

                @block.vector
                def _(dve):
                    dve.memset(spare, 0.0).then_inc(S["b"], 1)
                    with dve.Fori(0, GQA) as g:
                        base = g * NU
                        dve.wait_ge(S["b"], base + 1)
                        for pair in range(2):
                            ins = dve.tensor_copy(qg[:, pair, :], qT[:, bass.ds(4 * pair + g, 1), 0:SEQ].rearrange("p a n -> p (a n)"))
                        ins.then_inc(S["qg"], 1)

                        def invert(u):
                            dve.wait_ge(S["e"], base + u + 1)
                            dve.reciprocal(st[:, u % 4, 3:4], st[:, u % 4, 2:3]).then_inc(S["d1"], 1)

                        def finish(u):
                            kv, br, i = units[u]
                            dve.wait_ge(S["d1"], base + u + 1)
                            dve.tensor_tensor(st[:, u % 4, 3:4], st[:, u % 4, 3:4],
                                              sg[:, i, bass.ds((4 * kv + g) * 3 + 1 + br, 1)], ALU.mult).then_inc(S["d2"], 1)
                            dve.wait_ge(S["d2"], base + u + 1)
                            dve.wait_ge(S["o"], base + u + 1)
                            dst = onat[:, i, bass.ds((4 * kv + g) * HD, HD)]
                            dve.scalar_tensor_tensor(dst, PS[:, 4 + u % 2, 0:HD], st[:, u % 4, 3:4], dst, ALU.mult, ALU.add
                                                     ).then_inc(S["b"], 1)
                        for u in range(NU):
                            kv, br, i = units[u]
                            n = (i + 1) * P
                            dve.wait_ge(s_mh[kv], (g + 1) * 16)
                            dve.wait_ge(S["s"], base + u + 1)
                            if u >= 2:
                                invert(u - 2)
                            else:
                                dve.memset(spare, 0.0)
                            dve.tensor_tensor_reduce(Sx[u % 3][:, 0:n], PS[:, u % 2, 0:n], mh[:, kv, SEQ - n:SEQ], 1.0, 3.0 * MASKED,
                                                     ALU.add, ALU.max, st[:, u % 4, 0:1]).then_inc(S["x"], 1)
                            if u >= 2:
                                finish(u - 2)
                            dve.wait_ge(S["x"], base + u + 1)
                            dve.tensor_scalar(st[:, u % 4, 1:2], st[:, u % 4, 0:1], -1.0, None, ALU.mult).then_inc(S["nm"], 1)
                        for u in (NU - 2, NU - 1):
                            invert(u)
                            finish(u)

        def attend_sample():
            o = O_FREE
            qbd = at(o, DEC_BATCH, 2, P)
            kt = at(o + 2048, 2, PAST_LEN)
            ktw = at(o + 4096, 2, WINDOW)
            Ss = at(o + 5120, PAST_LEN + NS)
            Sw = at(o + 6208, WINDOW + NS)
            bs = at(o + 6784, PAST_LEN)
            bw = at(o + 7808, WINDOW)
            bn = at(o + 8320, 120)
            cb = at(o + 8440, 2, 120)
            pc = at(o + 8680, 2, ALL_PAGES)
            pcT = at(o + 8808, 2, P)
            PTs = at(o + 9064, 9, P)
            PTw = at(o + 10216, 5, P)
            osb = at(o + 10856, 3, HD)
            qb = at(o + 11048, 2, P)
            pgw0 = at(o + 11304, 4, 512)
            st = at(o + 13352, 24)
            sel = at(o + 13376, 4, 16)
            pgs = [at(O_OT, PAGES, 512), at(O_NAT, PAGES, 512)]
            pgw = [pgw0, at(O_NAT + 2 * 5 * 512, 4, 512)]
            names = ("bias", "z", "fill", "qbd", "cbz", "qb", "cs", "nmc", "ec", "pn", "pct", "pctc", "kt", "ktc", "ss", "sw",
                     "nms", "nmw", "es", "ew", "tp", "tpc", "ov", "osc", "og", "dch")
            S = {n: sem("sa_" + n) for n in names}
            lp = [sem(f"sa_pg{s}") for s in range(2)]
            lw = [sem(f"sa_pw{s}") for s in range(2)]
            cache = io["cache_slc_kv"].rearrange("a n p h c d -> (a n) p (h c d)")
            win = io["cache_win_kv"].rearrange("a b (i p) h c d -> (a b) p i (h c d)", p=P)

            with nc.Block() as block:
                @block.sync
                def _(sp):
                    with nc.allow_non_contiguous_dma(reason="strided biases of the compressed blocks"):
                        sp.dma_start(bs, bass.AP(scr_r, TOP_R - PAST_LEN, [[LEN_R, N_HEADS], [-1, DEC_SEQ], [1, PAST_LEN]])).then_inc(S["bias"], 16)
                        sp.dma_start(bw, bass.AP(scr_w, TOP_W - WINDOW, [[LEN_W, N_HEADS], [-1, DEC_SEQ], [1, WINDOW]])).then_inc(S["bias"], 16)
                        sp.wait_ge(S["fill"], 2)
                        sp.dma_start(bn[:, 56:64], bass.AP(scr_r, TOP_R, [[LEN_R, N_HEADS], [-1, DEC_SEQ], [1, DEC_SEQ]])).then_inc(S["bias"], 16)
                    def load(s, b):
                        for j in range(PAGES):
                            page = sp.value_load(page_sb[0:1, bass.ds(b * PAGES + j, 1)], min_val=0, max_val=N_POOL - 1)
                            sp.dma_start(pgs[s][:, j, :], cache[bass.ds(page, 1), :, :].rearrange("a p n -> (a p) n")).then_inc(lp[s], 16)
                        sp.dma_start(pgw[s], win[bass.ds(b, 1), :, :, :].rearrange("a p i n -> (a p) i n")).then_inc(lw[s], 16)
                    for s in range(2):
                        load(s, s)
                    with sp.Fori(0, DEC_BATCH // 2 - 1) as i:
                        for s in range(2):
                            sp.wait_ge(S["ov"], i * 2 + (s + 1))
                            load(s, i * 2 + (s + 2))

                @block.gpsimd
                def _(pool):
                    pool.memset(qbd[:, :, :, :], 0.0).then_inc(S["z"], 1)
                    for b in range(DEC_BATCH):
                        pool.wait_ge(S["osc"], b + 1)
                        for br in range(3):
                            pool.dma_start(bass.AP(scr_o, (br * NS + b * DEC_SEQ) * ATT_WIDTH,
                                                   [[HD, N_HEADS], [ATT_WIDTH, DEC_SEQ], [1, HD]]), osb[:, br, :]).then_inc(S["og"], 16)
                    pool.wait_ge(S["og"], 16 * 3 * DEC_BATCH)


                @block.tensor
                def _(pe):
                    pe.wait_ge(S["z"], 1)
                    for i in turns(pe, True, DEC_BATCH // 2):
                        for s in range(2):
                            b2 = i * 2
                            pe.wait_ge(S["qb"], b2 + (s + 1))
                            for p in range(2):
                                m = pe.matmul(PS[:, 0, 0:P], qb[:, p, :], kc_all[:, p, :, :].rearrange("p a b -> p (a b)"),
                                              start=(p == 0), stop=(p == 1))
                            m.then_inc(S["cs"], 1)
                            for j in range(12):
                                if j == 0:
                                    pe.wait_ge(lp[s], (i + 1) * (16 * PAGES))
                                if j == 8:
                                    pe.wait_ge(lw[s], (i + 1) * 16)
                                if j < 2:
                                    if j == 0 and not (known(i) and s == 0):
                                        pe.wait_ge(S["tpc"], i * 8 + 4 * s)
                                else:
                                    pe.wait_ge(S["ktc"], b2 * 24 + (24 * s + 2 * (j - 1)))
                                src = pgs[s][:, j, :] if j < 8 else pgw[s][:, j - 8, :]
                                kt_transposes(pe, 2 + j % 2, src).then_inc(S["kt"], 1)
                            pe.wait_ge(S["ktc"], b2 * 24 + (24 * s + 16))
                            for half in range(2):
                                for p in range(2):
                                    pe.matmul(PS[:, 4 + half, :], qb[:, p, :], kt[:, p, 512 * half:512 * half + 512], start=(p == 0), stop=(p == 1))
                            pe.wait_ge(S["nmc"], b2 + (s + 1))
                            for p in range(2):
                                m = pe.matmul(PS[:, 0, P:P + NS], qb[:, p, :], ktn[:, 0, p, :], start=(p == 0), stop=(p == 1))
                            m.then_inc(S["ss"], 1)
                            pe.wait_ge(S["ktc"], b2 * 24 + (24 * s + 24))
                            if not (known(i) and s == 0):
                                pe.wait_ge(S["osc"], b2 + s)
                            for p in range(2):
                                pe.matmul(PS[:, 6, :], qb[:, p, :], ktw[:, p, :], start=(p == 0), stop=(p == 1))
                            for p in range(2):
                                m = pe.matmul(PS[:, 0, P + NS:P + 2 * NS], qb[:, p, :], ktn[:, 1, p, :], start=(p == 0), stop=(p == 1))
                            m.then_inc(S["sw"], 1)
                            pe.wait_ge(S["pn"], b2 + (s + 1))
                            pe.matmul(PS[:, 1, 0:16], sq6[:, GROUP, :], pc[:, :, bass.ds(b2 * 8 + 8 * s, 8)], start=True, stop=True)
                            for half in range(2):
                                m = pe.transpose(PS[0:64, 1, P + half * P:2 * P + half * P], pc[:, half, :], ident)
                            m.then_inc(S["pct"], 1)
                            pe.wait_ge(S["pctc"], b2 + (s + 1))
                            for half in range(2):
                                m = pe.matmul(PS[:, 7, 0:256], pcT[0:64, half, :], vc_all[:, half, :], start=(half == 0), stop=(half == 1))
                            pe.wait_ge(S["ew"], b2 + (s + 1))
                            pe.wait_ge(S["es"], b2 + (s + 1))
                            for j in range(4):
                                m = pe.transpose(PS[:, 2, j * P:(j + 1) * P], Sw[:, j * P:(j + 1) * P], ident)
                            m.then_inc(S["tp"], 1)
                            pe.transpose(PS[0:64, 3, 0:P], Sw[:, 512:576], ident)
                            pe.transpose(PS[0:64, 3, P:2 * P], Ss[:, 1024:1088], ident).then_inc(S["tp"], 1)
                            for half in range(2):
                                pe.wait_ge(S["tpc"], i * 8 + (4 * s + half + 1))
                                for j in range(4):
                                    c0 = 512 * half + j * P
                                    m = pe.transpose(PS[:, 2 + half, j * P:(j + 1) * P], Ss[:, c0:c0 + P], ident)
                                m.then_inc(S["tp"], 1)
                            vcols = lambda rows: rows.rearrange("p (h c d) -> p h c d", h=N_KV, c=2)[:, :, 1, :]
                            for j in range(5):
                                v = vcols(pgw[s][:, j, :]) if j < 4 else vcols(nat[0:NS, 2, 4, :])
                                pr = PTw[:, j, :] if j < 4 else PTw[0:NS, 4, :]
                                pe.matmul(PS[:, 6, 0:256], pr, v, start=(j == 0), stop=(j == 4))
                            pe.wait_ge(S["tpc"], i * 8 + (4 * s + 4))
                            for j in range(9):
                                v = vcols(pgs[s][:, j, :]) if j < 8 else vcols(nat[0:NS, 1, 4, :])
                                pr = PTs[:, j, :] if j < 8 else PTs[0:NS, 8, :]
                                m = pe.matmul(PS[:, 7, 256:512], pr, v, start=(j == 0), stop=(j == 8))
                            m.then_inc(S["ov"], 1)

                @block.scalar
                def _(act):
                    act.wait_ge(S["z"], 1)
                    with act.Fori(0, DEC_BATCH // 2) as i:
                        for s in range(2):
                            b2 = i * 2
                            act.wait_ge(S["nmc"], b2 + (s + 1))
                            act.activation(pc[:, :, :], pc[:, :, :], ACT.Exp, bias=st[:, 1:2], accum_out=st[:, 2:3]).then_inc(S["ec"], 1)
                            for j in range(12):
                                act.wait_ge(S["kt"], i * 24 + (12 * s + j + 1))
                                lo, hi = kt_halves(2 + j % 2, P)
                                dst = kt[:, :, j * P:(j + 1) * P] if j < 8 else ktw[:, :, (j - 8) * P:(j - 7) * P]
                                act.copy(dst[0:64], lo).then_inc(S["ktc"], 1)
                                act.copy(dst[64:P], hi).then_inc(S["ktc"], 1)
                            act.wait_ge(S["nmw"], b2 + (s + 1))
                            act.activation(Sw, Sw, ACT.Exp, bias=st[:, 5:6], accum_out=st[:, 6:7]).then_inc(S["ew"], 1)
                            act.wait_ge(S["nms"], b2 + (s + 1))
                            act.activation(Ss, Ss, ACT.Exp, bias=st[:, 9:10], accum_out=st[:, 10:11]).then_inc(S["es"], 1)
                            act.wait_ge(S["tp"], i * 8 + (4 * s + 1))
                            act.copy(PTw[:, 0:4, :].rearrange("p a n -> p (a n)"), PS[:, 2, :]).then_inc(S["tpc"], 1)
                            act.wait_ge(S["tp"], i * 8 + (4 * s + 2))
                            act.copy(PTw[0:NS, 4, :], PS[0:NS, 3, 0:P])
                            act.copy(PTs[0:NS, 8, :], PS[0:NS, 3, P:2 * P]).then_inc(S["tpc"], 1)
                            for half in range(2):
                                act.wait_ge(S["tp"], i * 8 + (4 * s + 3 + half))
                                act.copy(PTs[:, 4 * half:4 * half + 4, :].rearrange("p a n -> p (a n)"), PS[:, 2 + half, :]).then_inc(S["tpc"], 1)

                @block.vector
                def _(dve):
                    ch = Chain(dve, S["dch"])
                    dve.memset(bn, MASKED).then_inc(S["fill"], 1)
                    dve.memset(cb[:, :, :], MASKED).then_inc(S["fill"], 1)
                    dve.wait_ge(S["z"], 1)
                    for p in range(2):
                        for e in range(2):
                            src = qT[64 * e:64 * e + 64, 4 * p:4 * p + 4, SEQ:T].rearrange("p g (b t) -> p g b t", t=DEC_SEQ)
                            c0 = (2 * p + e) * 32
                            dst = qbd[64 * e:64 * e + 64, :, p, c0:c0 + 32].rearrange("p b (g t) -> p g b t", t=DEC_SEQ)
                            for g in range(GQA):
                                ins = dve.tensor_copy(dst[:, g], src[:, g])
                    ins.then_inc(S["qbd"], 1)
                    dve.wait_ge(S["qbd"], 1)
                    dve.wait_ge(S["bias"], 16 * 3)
                    ends = bs.rearrange("p (g a l) -> p a g l", a=2, l=BLK)[:, :, :, BLK - 1]
                    dve.tensor_copy(cb[:, :, 56:64], ends).then_inc(S["cbz"], 1)
                    dve.wait_ge(S["cbz"], 1)
                    PER = 40
                    for i in turns(dve, True, DEC_BATCH // 2):
                        ch.enter(i, PER)
                        for s in range(2):
                            b2 = i * 2
                            off = 56 - (b2 * 8 + 8 * s)
                            dve.tensor_copy(qb[:, :, :], qbd[:, bass.ds(b2 + s, 1), :, :].rearrange("p a b n -> p (a b) n")).then_inc(S["qb"], 1)
                            dve.wait_ge(S["cs"], b2 + (s + 1))
                            ch.link(dve.tensor_tensor(pc[:, :, :], PS[:, 0, 0:P].rearrange("p (a n) -> p a n", a=2),
                                                      cb[:, :, bass.ds(off, 64)], ALU.add))
                            ch.link(dve.tensor_reduce(st[:, 0:1], pc[:, :, :].rearrange("p a n -> p (a n)"), AXX, ALU.max))
                            dve.tensor_scalar(st[:, 1:2], st[:, 0:1], 0.1 * MASKED, -1.0, ALU.max, ALU.mult).then_inc(S["nmc"], 1)
                            dve.wait_ge(S["ec"], b2 + (s + 1))
                            ch.link(dve.tensor_scalar(st[:, 2:3], st[:, 2:3], 1e-30, None, ALU.max))
                            ch.link(dve.reciprocal(st[:, 3:4], st[:, 2:3]))
                            dve.tensor_scalar(pc[:, :, :], pc[:, :, :], st[:, 3:4], None, ALU.mult).then_inc(S["pn"], 1)
                            dve.wait_ge(S["sw"], b2 + (s + 1))
                            ch.link(dve.tensor_tensor(Sw[:, 0:512], PS[:, 6, :], bw, ALU.add))
                            ch.link(dve.tensor_tensor(Sw[:, 512:576], PS[:, 0, P + NS:P + 2 * NS], bn[:, bass.ds(off, 64)], ALU.add))
                            ch.link(dve.tensor_reduce(st[:, 4:5], Sw, AXX, ALU.max))
                            dve.tensor_scalar(st[:, 5:6], st[:, 4:5], -1.0, None, ALU.mult).then_inc(S["nmw"], 1)
                            dve.wait_ge(S["pct"], b2 + (s + 1))
                            dve.tensor_copy(pcT[0:64, :, :], PS[0:64, 1, P:3 * P].rearrange("p (a n) -> p a n", a=2)).then_inc(S["pctc"], 1)
                            ch.link(dve.tensor_tensor(sel[:, 0, :], PS[:, 1, 0:16], crow[:, 1, :], ALU.add))
                            ch.link(dve.tensor_reduce(st[:, 12:13], sel[:, 0, :], AXX, ALU.min))
                            ch.link(dve.scalar_tensor_tensor(sel[:, 1, :], sel[:, 0, :], st[:, 12:13], crow[:, 0, :], ALU.is_equal, ALU.mult))
                            ch.link(dve.tensor_reduce(st[:, 13:14], sel[:, 1, :], AXX, ALU.max))
                            ch.link(dve.tensor_scalar(sel[:, 2, :], crow[:, 0, :], st[:, 13:14], MASKED, ALU.is_equal, ALU.mult))
                            dve.wait_ge(S["ss"], b2 + (s + 1))
                            for half in range(2):
                                ch.link(dve.tensor_tensor(Ss[:, 512 * half:512 * half + 512], PS[:, 4 + half, :],
                                                          bs[:, 512 * half:512 * half + 512], ALU.add))
                            ch.link(dve.tensor_tensor(Ss[:, 1024:1088], PS[:, 0, P:P + NS], bn[:, bass.ds(off, 64)], ALU.add))
                            for half in range(2):
                                v = Ss[:, 0:1024].rearrange("p (g a l) -> p g a l", a=2, l=BLK)[:, :, half, :]
                                ch.link(dve.tensor_tensor(v, v, sel[:, 2, 8 * half:8 * half + 8].unsqueeze(2).to_broadcast([P, 8, BLK]), ALU.add))
                            ch.link(dve.tensor_reduce(st[:, 8:9], Ss, AXX, ALU.max))
                            dve.tensor_scalar(st[:, 9:10], st[:, 8:9], -1.0, None, ALU.mult).then_inc(S["nms"], 1)
                            dve.wait_ge(S["es"], b2 + (s + 1))
                            dve.wait_ge(S["ew"], b2 + (s + 1))
                            ch.link(dve.reciprocal(st[:, 7:8], st[:, 6:7]))
                            ch.link(dve.reciprocal(st[:, 11:12], st[:, 10:11]))
                            if not (known(i) and s == 0):
                                dve.wait_ge(S["og"], i * (2 * 48) + 48 * s)
                            dve.wait_ge(S["ov"], b2 + (s + 1))
                            for h in range(N_KV):
                                r = slice(32 * h, 32 * h + 32)
                                dve.tensor_copy(osb[r, 0, :], PS[r, 7, HD * h:HD * h + HD])
                                dve.tensor_scalar(osb[r, 1, :], PS[r, 7, 256 + HD * h:256 + HD * h + HD], st[r, 11:12], None, ALU.mult)
                                ins = dve.tensor_scalar(osb[r, 2, :], PS[r, 6, HD * h:HD * h + HD], st[r, 7:8], None, ALU.mult)
                            ins.then_inc(S["osc"], 1)
                    ch.leave(DEC_BATCH // 2)

        def attention_out():
            og = at(O_Q, 3, N_HEADS, HD)
            junk = at(O_FREE, ATT_WIDTH)
            st = at(O_FREE + 1024, 5, 2)
            S = {n: sem("ao_" + n) for n in ("dch", "sq", "rt", "n", "t", "c", "z", "ld")}
            with nc.Block() as block:
                @block.sync
                def _(sp):
                    sp.dma_start(og[0:NS, :, :, :].rearrange("p r h d -> p r (h d)"),
                                 scr_o.ap().rearrange("r t n -> t r n")).then_inc(S["ld"], 16)

                @block.vector
                def _(dve):
                    ch = Chain(dve, S["dch"])
                    dve.wait_ge(S["ld"], 16)
                    g3 = sg[0:NS, 4, :].rearrange("p (h r) -> p h r", r=3)
                    for br in range(3):
                        ch.link(dve.tensor_tensor(og[0:NS, br, :, :], og[0:NS, br, :, :],
                                                  g3[:, :, br:br + 1].to_broadcast([NS, 16, HD]), ALU.mult))
                    flat = [og[0:NS, br, :, :].rearrange("p h d -> p (h d)") for br in range(3)]
                    ch.link(dve.tensor_tensor(flat[0], flat[0], flat[1], ALU.add))
                    dve.tensor_tensor(onat[0:NS, 4, :], flat[0], flat[2], ALU.add).then_inc(S["z"], 1)
                    for i, (t0, n) in enumerate(TILES):
                        dve.wait_ge(S["rt"], i + 1)
                        ch.link(dve.reciprocal(st[0:n, i, 1:2], st[0:n, i, 1:2]))
                        dve.tensor_scalar(onat[0:n, i, :], onat[0:n, i, :], st[0:n, i, 1:2], None, ALU.mult).then_inc(S["n"], 1)
                    u = 0
                    for i, (t0, n) in enumerate(TILES):
                        for q in range(2):
                            dve.wait_ge(S["t"], u + 1)
                            for j in range(4):
                                k = 4 * q + j
                                ins = dve.tensor_scalar(oT[:, k, t0:t0 + n], PS[:, u % 4, j * P:j * P + n],
                                                        gT[:, 8 * GATT + k:8 * GATT + k + 1], None, ALU.mult)
                            ins.then_inc(S["c"], 1)
                            u += 1

                @block.scalar
                def _(act):
                    for i, (t0, n) in enumerate(TILES):
                        if i == 4:
                            act.wait_ge(S["z"], 1)
                        act.activation(junk[0:n, :], onat[0:n, i, :], ACT.Square, scale=ATT_WIDTH ** -0.5,
                                       accum_out=st[0:n, i, 0:1]).then_inc(S["sq"], 1)
                        act.wait_ge(S["sq"], i + 1)
                        act.activation(st[0:n, i, 1:2], st[0:n, i, 0:1], ACT.Sqrt, bias=eps_sb[0:n, 0:1]).then_inc(S["rt"], 1)

                @block.tensor
                def _(pe):
                    u = 0
                    for i, (t0, n) in enumerate(TILES):
                        pe.wait_ge(S["n"], i + 1)
                        for q in range(2):
                            if u >= 4:
                                pe.wait_ge(S["c"], u - 3)
                            for j in range(4):
                                m = pe.transpose(PS[:, u % 4, j * P:j * P + n], onat[0:n, i, (4 * q + j) * P:(4 * q + j + 1) * P], ident[0:n, 0:n])
                            m.then_inc(S["t"], 1)
                            u += 1

        def mixer_out():
            x = Split("mo_x", O_Q, D_MIX // P, T)
            o = O_Q + 2 * (D_MIX // P) * T
            kp = D_MIX // P // 2
            project_out("mo", io["w_out"].rearrange("a k n -> (a k) n"), D_MIX // P, x, at(o, KD, T), o + KD * T,
                        o + KD * T + 4 * kp * P, GMPOST, source=oT)

        setup()
        compress_past()
        ffn("f1", io["ffn1_w_in"].rearrange("a k n -> (a k) n"), io["ffn1_w_out"].rearrange("a k n -> (a k) n"), G1PRE, G1POST)
        mixer_in()
        conv()
        ssd()
        ssd_gate_norm()
        recycle_semaphores()
        compress_prompt()
        attend_prompt()
        attend_sample()
        attention_out()
        mixer_out()
        ffn("f2", io["ffn2_w_in"].rearrange("a k n -> (a k) n"), io["ffn2_w_out"].rearrange("a k n -> (a k) n"), G2PRE, G2POST)
        finish_out()


_INS = ['x_prompt', 'x_sample', 'cache_cmp_kv', 'cache_slc_kv', 'cache_win_kv', 'state_ssm', 'state_conv',
        'page_table', 'rel_table', 'ffn1_pre', 'ffn1_post', 'ffn1_w_in', 'ffn1_w_out', 'mix_pre', 'mix_post',
        'w_in', 'w_out', 'att_out_norm', 'cmp_pe', 'w_cmp', 'conv_w', 'conv_b', 'dt_bias', 'a_log', 'd_skip',
        'ssd_norm', 'ffn2_pre', 'ffn2_post', 'ffn2_w_in', 'ffn2_w_out']
_OUTS = [("y_prompt", (1, 512, 1024)), ("y_sample", (8, 8, 1024)),
         ("p_cmp_kv", (1, 1, 512, 4, 2, 64)), ("p_slc_kv", (1, 1, 512, 4, 2, 64)), ("p_win_kv", (1, 1, 512, 4, 2, 64)),
         ("p_ssm", (1, 1, 16, 64, 128)), ("p_conv", (1, 1, 3, 1536)),
         ("s_cmp_kv", (1, 8, 8, 4, 2, 64)), ("s_slc_kv", (1, 8, 8, 4, 2, 64)), ("s_win_kv", (1, 8, 512, 4, 2, 64)),
         ("s_ssm", (1, 8, 16, 64, 128)), ("s_conv", (1, 8, 3, 1536))]


def kernel(**inputs):
    import numpy as _np
    import concourse.bacc as _bacc
    from concourse import mybir as _mybir
    from concourse.bass_utils import run_bass_kernel_spmd as _run

    nc = _bacc.Bacc("TRN2", target_bir_lowering=False, num_devices=1)
    arrays, io = {}, {}
    for name in _INS:
        arrays[f"in_{name}"] = _np.ascontiguousarray(inputs[name])
    for name, value in constants().items():
        arrays[f"in_{name}"] = value
    for name, a in arrays.items():
        io[name[3:]] = nc.dram_tensor(name, a.shape, _mybir.dt.from_np(a.dtype), kind="ExternalInput").ap()
    out = {name: nc.dram_tensor(f"out_{name}", shape, F32, kind="ExternalOutput").ap() for name, shape in _OUTS}
    build(nc, io, out)
    r = _run(nc, [arrays], core_ids=[0])
    return tuple(r.results[0][f"out_{name}"] for name, _ in _OUTS)
```

```python
from contextlib import ExitStack

import numpy as np

import concourse.bass as bass
from concourse import mybir

F32 = mybir.dt.float32
I32 = mybir.dt.int32
F32R = mybir.dt.float32r
ALU = mybir.AluOpType
ACT = mybir.ActivationFunctionType
AXX = mybir.AxisListType.X

D_MODEL, SEQ, DEC_BATCH, DEC_SEQ, PAST_LEN, PAGE = 1024, 512, 8, 8, 1024, 128
N_HEADS, HD, N_KV, GQA = 16, 64, 4, 4
ATT_WIDTH, KV_WIDTH = 1024, 512
BLK, WINDOW, N_BUCKETS, MAX_DISTANCE = 64, 512, 32, 128
SSD_HEADS, SSD_GROUPS, SSD_STATE, CONV_W = 16, 2, 128, 4
SSD_INNER, CONV_DIM, D_MIX, D_FF, N_BRANCH = 1024, 1536, 2048, 2816, 3
N_POOL = 80
EPS = 1e-6
SCALE = HD ** -0.5
MASKED = -1e30

P = 128
NS = DEC_BATCH * DEC_SEQ
T = SEQ + NS
TILES = [(i * P, P) for i in range(SEQ // P)] + [(SEQ, NS)]
KD = D_MODEL // P
KF = D_FF // P
KC_XBC = CONV_DIM // P
PAGES = PAST_LEN // PAGE
ALL_PAGES = DEC_BATCH * PAGES
PAD = CONV_W - 1
XP_S = PAD + SEQ
XP_RUN = PAD + DEC_SEQ
XP = XP_S + DEC_BATCH * XP_RUN
CONV_N = XP - PAD

COL_KV = ATT_WIDTH
COL_GATES = ATT_WIDTH + 3 * KV_WIDTH
COL_Z = COL_GATES + N_BRANCH * N_HEADS
COL_DT = COL_Z + SSD_INNER + CONV_DIM
D_IN = COL_DT + SSD_HEADS

LEN_R, TOP_R = 1664, 1151
LEN_F, LOW_F = 1024, -512
LEN_T = SEQ + P
FIRST_T = TOP_R - (SEQ - P) - (P - 1)
LEN_W, TOP_W = 544, 527


def bucket_of(dist):
    exact = N_BUCKETS // 2
    n = np.maximum(dist, 0)
    f = np.maximum(n, 1).astype(np.float32)
    far = exact + (np.log(f / np.float32(exact)) / np.float32(np.log(MAX_DISTANCE / exact))
                   * np.float32(N_BUCKETS - exact)).astype(np.int32)
    return np.where(n < exact, n, np.minimum(far, N_BUCKETS - 1))


def one_hot(dist, limit):
    b = np.where((dist < 0) | (dist >= limit), N_BUCKETS, bucket_of(dist))
    return (np.arange(N_BUCKETS + 1)[:, None] == b[None, :]).astype(np.float32)


def constants():
    big = 10 ** 9
    hot = np.concatenate([
        one_hot(TOP_R - np.arange(LEN_R), big),
        one_hot(LOW_F + np.arange(LEN_F), big),
        one_hot(TOP_W - np.arange(LEN_W), WINDOW)], axis=1)
    r = np.arange(P)
    same = r[:, None] // DEC_SEQ == r[None, :] // DEC_SEQ
    tri = r[:, None] <= r[None, :]
    group = (r[:, None] // 32 == r[None, :] // 32) & (r[:, None] % DEC_SEQ == r[None, :] % DEC_SEQ)
    squares = np.stack([np.eye(P), tri, np.ones((P, P)), tri & same, same, group], axis=1).astype(np.float32)
    order = np.arange(16)
    block = (2 * (order % PAGES) + order // PAGES).astype(np.float32)
    forced = (block == 0) | (block == 15)
    rows = np.zeros((P, 3, 16), np.float32)
    rows[:, 0, :] = block
    rows[:, 1, :] = np.where(forced, 1e30, 0.0)
    rows[:NS, 2, :DEC_BATCH] = np.arange(NS)[:, None] // DEC_SEQ == np.arange(DEC_BATCH)[None, :]
    return {"c_hot": hot, "c_squares": squares, "c_rows": rows}


IDENT, TRI, ONES, BTRI, BONES, GROUP = range(6)


def turns(eng, only_first, count):
    yield 0
    with eng.Fori(1, count if only_first else count - 1) as i:
        yield i
    if not only_first:
        yield count - 1


def known(i):
    return isinstance(i, int)


class Chain:

    def __init__(self, eng, sem):
        self.eng, self.sem, self.n, self.base, self.per = eng, sem, 0, None, 0

    def link(self, ins):
        self.n += 1
        ins.then_inc(self.sem, 1)
        self.eng.wait_ge(self.sem, self.n if self.base is None else self.base + self.n)

    def enter(self, i, per):
        if self.base is None:
            self.start, self.per = self.n, per
        assert self.n in (self.start, self.start + per), (self.n, self.start, per)
        self.n, self.base = self.start, i * per

    def leave(self, count):
        assert self.n - self.start == self.per, (self.n - self.start, self.per)
        self.n, self.base = self.start + self.per * count, None


def build(nc, io, out):
    with ExitStack() as ctx:
        def sb(name, shape, dt=F32):
            return ctx.enter_context(nc.sbuf_tensor(name, shape, dt))

        stage_sems = []

        def sem(name, lasting=False):
            s = nc.alloc_semaphore(name)
            if not lasting:
                stage_sems.append(s)
            return s

        def recycle_semaphores():
            nc.clear_and_free_semaphores(list(stage_sems))
            stage_sems.clear()
            nc.all_engine_barrier()

        xT = sb("xT", [P, KD, T])
        sq6 = sb("sq6", [P, 6, P])
        crow = sb("crow", [P, 3, 16])
        gT = sb("gT", [P, 64])
        convT = sb("convT", [P, 5 * KC_XBC])
        small = sb("small", [P, 6, SSD_HEADS])
        norm_rows = sb("norm_rows", [P, 4, T])
        rstd, sacc, sqr = norm_rows[:, 0, :], norm_rows[:, 1, :], norm_rows[:, 2:4, :]
        bias_cmp = sb("bias_cmp", [P, 4, N_HEADS, 8])
        kc_all = sb("kc_all", [P, 2, 2, ALL_PAGES])
        vc_all = sb("vc_all", [ALL_PAGES, 2, 256])
        pe_c = sb("pe_c", [P, 2])
        eps_sb = sb("eps_sb", [P, 1])
        page_sb = sb("page_sb", [1, ALL_PAGES], I32)
        AW = 43600
        arena_at = nc.sbuf_base
        arena = sb("arena", [P, AW])

        def part(name, o, *dims, dt=F32):
            v = nc.alloc_sbuf_tensor_at(name, [P] + list(dims), dt, offset=arena_at + 4 * o)
            return v[tuple([slice(None)] * (len(dims) + 1))]
        PS = ctx.enter_context(nc.psum_tensor("PS", [P, 8, 512], F32))

        def at(o, *dims):
            n = int(np.prod(dims))
            assert o + n <= AW, (o, n)
            v = arena[:, o:o + n]
            if len(dims) == 1:
                return v
            names = "abcd"[:len(dims)]
            return v.rearrange("p (" + " ".join(names) + ") -> p " + " ".join(names),
                               **{c: d for c, d in zip(names[1:], dims[1:])})

        ident = sq6[:, IDENT, :]
        scr_r = nc.dram_tensor("scr_r", (N_HEADS, LEN_R), F32)
        scr_o = nc.dram_tensor("scr_o", (N_BRANCH, NS, ATT_WIDTH), F32)
        scr_t = nc.dram_tensor("scr_t", (N_HEADS, P, LEN_T), F32)
        scr_w = nc.dram_tensor("scr_w", (N_HEADS, LEN_W), F32)
        G1PRE, G1POST, GMPRE, GMPOST, GATT, GSSD, G2PRE, G2POST = range(8)

        def halves(v):
            return v[:, 0:SEQ], v[:, SEQ:T]

        s_tables = sem("tables", True)

        def setup(nrm):
            FIRST = 18
            assert FIRST * 512 >= 8800
            pg = at(0, ALL_PAGES * 512 + P)
            o = ALL_PAGES * 512 + P
            QD = 32
            wbd = [at(o + s * QD * P, QD, 2, 64) for s in range(2)]
            ck = at(o + 2 * QD * P, 2, N_KV, ALL_PAGES)
            s_z, s_t, s_k, s_pe, s_added, s_vc, mm, s_ck, ld_p = (
                sem("cp_" + n) for n in ("z", "t", "k", "pe", "added", "vc", "mm", "ck", "pages"))
            ld_w = [sem(f"cp_w{s}") for s in range(2)]
            s_page = sem("cp_page")
            kh = io["w_cmp"].rearrange("a l c d e -> (a l) (c d) e")
            cache = io["cache_cmp_kv"].rearrange("a n p h c d -> (a n) p (h c d)")
            HALFWAY = (FIRST + ALL_PAGES) // 2

            def load_pages(eng, first, count):
                with eng.Fori(0, count) as j:
                    page = eng.value_load(page_sb[0:1, bass.ds(j + first, 1)], min_val=0, max_val=N_POOL - 1)
                    eng.dma_start(pg[:, bass.ds((j + first) * 512, 512)],
                                  cache[bass.ds(page, 1), :, :].rearrange("a p n -> (a p) n")).then_inc(ld_p, 16)
            xnat = at(0, 5, D_MODEL)
            hot = at(5120, LEN_R + LEN_F + LEN_W)
            gnat = at(8400, 2, P)
            tabl = at(8700, N_HEADS)
            fr = norm_rows[:, :, :].rearrange("p a n -> p (a n)")
            ld, s_mm, s_ev, s_scr, s_tab, s_fr = (sem("su_" + n) for n in ("ld", "mm", "ev", "scr", "tab", "fr"))
            s_small, s_ch, s_dch = sem("su_small"), sem("su_ch"), sem("su_dch")
            LOADS = 4 + 5 + 8 + 2
            pieces = [(0, 512), (512, 512), (1024, 512), (1536, LEN_R - 1536)]
            with nc.Block() as block:
                @block.sync
                def _(sp):
                    sp.dma_start(page_sb[0:1, :], io["page_table"].rearrange("b n -> (b n)").rearrange("(a n) -> a n", a=1)).then_inc(s_page, 16)
                    sp.wait_ge(s_tab, 1)
                    sp.dma_start(tabl[0:N_BUCKETS, :], io["rel_table"]).then_inc(ld, 16)
                    sp.dma_start(sq6[:, :, :], io["c_squares"]).then_inc(ld, 16)
                    sp.dma_start(crow[:, :, :], io["c_rows"]).then_inc(ld, 16)
                    sp.dma_start(hot[0:N_BUCKETS + 1, :], io["c_hot"]).then_inc(ld, 16)
                    for i in range(4):
                        sp.dma_start(xnat[:, i, :], io["x_prompt"][0, i * P:(i + 1) * P, :]).then_inc(ld, 16)
                    sp.dma_start(xnat[0:NS, 4, :], io["x_sample"].rearrange("b t d -> (b t) d")).then_inc(ld, 16)
                    sp.wait_ge(s_page, 16)
                    load_pages(sp, FIRST, HALFWAY - FIRST)
                    sp.wait_ge(s_ev, 13)
                    load_pages(sp, 0, FIRST // 2)
                    sp.wait_ge(s_ck, 2)
                    for half in range(2):
                        for odd in range(2):
                            sp.dma_start(kc_all[64 * odd:64 * odd + 64, :, half, :],
                                         ck[64 * half:64 * half + 64, 0, :, :].rearrange("p (a b) n -> p a b n", b=2)[:, :, odd, :]
                                         ).then_inc(s_k, 16)
                    sp.wait_ge(s_k, 64)

                @block.gpsimd
                def _(pool):
                    for s in range(2):
                        pool.memset(wbd[s][0:64, :, 1, :], 0.0).then_inc(s_z, 1)

                @block.scalar
                def _(act):
                    with nc.allow_non_contiguous_dma(reason="rows of 256 bytes; small vectors spread over partitions"):
                        for w, name in enumerate(["ffn1_pre", "ffn1_post", "mix_pre", "mix_post", "att_out_norm",
                                                  "ssd_norm", "ffn2_pre", "ffn2_post"]):
                            act.dma_start(gnat[8 * w:8 * w + 8, 0, :], io[name].rearrange("l (k p) -> (l k) p", p=P)).then_inc(ld, 16)
                        act.dma_start(gnat[0:48, 1, :], io["conv_w"].rearrange("l w (k p) -> (l w k) p", p=P)).then_inc(ld, 16)
                        act.dma_start(gnat[48:60, 1, :], io["conv_b"].rearrange("l (k p) -> (l k) p", p=P)).then_inc(ld, 16)
                        act.wait_ge(s_z, 4)
                        for q in range(2):
                            for half in range(2):
                                act.dma_start(wbd[q][half * 64:half * 64 + 64, :, half, :],
                                              kh[:, QD * q:QD * q + QD, :]).then_inc(ld_w[q], 16)
                        for half in range(2):
                            act.dma_start(pg[half * 64:half * 64 + 64, ALL_PAGES * 512:ALL_PAGES * 512 + P],
                                          io["cmp_pe"].rearrange("a l c d -> (a l) (c d)")).then_inc(s_pe, 16)
                        for k, name in enumerate(["dt_bias", "a_log"]):
                            h = io[name]
                            act.dma_start(small[:, k, :], bass.AP(h.tensor, 0, [[0, P], [1, SSD_HEADS]])).then_inc(s_small, 16)
                        for half in range(2):
                            act.dma_start(small[half * 64:half * 64 + 64, 3, 0:8],
                                          bass.AP(io["d_skip"].tensor, half, [[0, 64], [2, 8]])).then_inc(s_small, 16)
                    act.wait_ge(s_page, 16)
                    load_pages(act, HALFWAY, ALL_PAGES - HALFWAY)
                    act.wait_ge(s_fr, 5)
                    act.wait_ge(s_ev, 1)
                    act.dma_start(scr_r.ap()[:, :], fr[0:N_HEADS, 0:LEN_R]).then_inc(s_scr, 16)
                    act.dma_start(scr_w.ap()[:, :], fr[0:N_HEADS, LEN_R:LEN_R + LEN_W]).then_inc(s_scr, 16)
                    act.wait_ge(s_ev, 13)
                    load_pages(act, FIRST // 2, FIRST - FIRST // 2)
                    act.wait_ge(s_small, 64)
                    act.activation(small[:, 2, :], small[:, 1, :], ACT.Exp).then_inc(s_ch, 1)
                    act.wait_ge(s_ch, 1)
                    act.mul(small[:, 2, :], small[:, 2, :], -1.0).then_inc(s_ch, 1)
                    act.wait_ge(s_ch, 2)
                    act.wait_ge(s_scr, 32)
                    for k in range(KD):
                        nrm.square(act, k)
                    with nc.allow_non_contiguous_dma(reason="rows of 256 bytes"):
                        for q in range(2, 4):
                            act.wait_ge(mm, q - 1)
                            for half in range(2):
                                act.dma_start(wbd[q - 2][half * 64:half * 64 + 64, :, half, :],
                                              kh[:, QD * q:QD * q + QD, :]).then_inc(ld_w[q - 2], 16)
                    nrm.take_root(act)

                @block.tensor
                def _(pe):
                    pe.wait_ge(ld, 16 * LOADS)
                    for k, (a, n) in enumerate(pieces + [(LEN_R + LEN_F, 512), (LEN_R + LEN_F + 512, LEN_W - 512)]):
                        if k == 5:
                            m = pe.matmul(PS[0:N_HEADS, 0, 0:n], tabl[0:33, :], hot[0:33, a:a + n], start=True, stop=True)
                            continue
                        b = [1, 2, 3, 4, 5][k]
                        m = pe.matmul(PS[0:N_HEADS, b, 0:n], tabl[0:33, :], hot[0:33, a:a + n], start=True, stop=True)
                    m.then_inc(s_mm, 1)
                    for i in range(4):
                        for o in range(8):
                            n = 2 * (o % 4) + o // 4
                            v = LEN_R + i * P - BLK * n - (BLK - 1) - LOW_F
                            m = pe.matmul(PS[:, 6, (i * 8 + o) * 16:(i * 8 + o + 1) * 16], hot[0:33, v:v + P],
                                           tabl[0:33, :], start=True, stop=True)
                    m.then_inc(s_mm, 1)
                    pe.transpose(PS[:, 7, 0:64], gnat[0:64, 0, :], ident[0:64, 0:64])
                    pe.transpose(PS[:, 7, 64:124], gnat[0:60, 1, :], ident[0:60, 0:60]).then_inc(s_mm, 1)
                    u = 0
                    for i, (t0, n) in enumerate(TILES):
                        for q in range(2):
                            if u < 2:
                                pe.wait_ge(s_ev, 1)
                            else:
                                pe.wait_ge(s_ev, u - 2 + 4)
                            for j in range(4):
                                m = pe.transpose(PS[:, u % 2, j * P:j * P + n],
                                                  xnat[0:n, i, (4 * q + j) * P:(4 * q + j + 1) * P], ident[0:n, 0:n])
                            m.then_inc(s_mm, 1)
                            u += 1
                    pe.wait_ge(ld_p, 16 * ALL_PAGES)
                    pe.wait_ge(s_pe, 32)
                    NCOL = N_KV * ALL_PAGES + 1
                    for q in range(4):
                        pe.wait_ge(ld_w[q % 2], 32 * (q // 2 + 1))
                        for j in range(QD):
                            c, d = (QD * q + j) // 64, (QD * q + j) % 64
                            rhs = bass.AP(pg.tensor, pg.offset + c * 64 + d, [pg.ap[0], [P, NCOL]])
                            m = pe.matmul(PS[:, 2 + c, 0:NCOL], wbd[q % 2][:, j, :, :].rearrange("p a b -> p (a b)"), rhs,
                                          start=(d == 0), stop=(d == 63))
                        m.then_inc(mm, 1)
                    nrm.total(pe)
                    pe.wait_ge(s_ck, 2)
                    for h in range(N_KV):
                        m = pe.transpose(PS[0:ALL_PAGES, 4, h * P:(h + 1) * P], ck[:, 1, h, :], ident)
                    m.then_inc(s_t, 1)

                @block.vector
                def _(dve):
                    dve.memset(tabl[0:33, :], MASKED).then_inc(s_tab, 1)
                    for s in range(2):
                        dve.memset(wbd[s][64:P, :, 0, :], 0.0).then_inc(s_z, 1)
                    dve.memset(eps_sb[:, :], EPS).then_inc(s_dch, 1)
                    dve.wait_ge(s_mm, 1)
                    for k, (a, n) in enumerate(pieces + [(LEN_R, 512)]):
                        dve.tensor_copy(fr[0:N_HEADS, a:a + n], PS[0:N_HEADS, k + 1, 0:n]).then_inc(s_fr, 1)
                    dve.tensor_copy(fr[0:N_HEADS, LEN_R + 512:LEN_R + LEN_W], PS[0:N_HEADS, 0, 0:LEN_W - 512]).then_inc(s_ev, 1)
                    dve.wait_ge(s_mm, 2)
                    dve.tensor_copy(bias_cmp[:, :, :, :].rearrange("p i h o -> p i o h"),
                                    PS[:, 6, :].rearrange("p (i o h) -> p i o h", i=4, o=8)).then_inc(s_ev, 1)
                    dve.wait_ge(s_mm, 3)
                    dve.tensor_copy(gT[:, :], PS[:, 7, 0:64]).then_inc(s_dch, 1)
                    dve.tensor_copy(convT[:, :], PS[:, 7, 64:124]).then_inc(s_ev, 1)
                    u = 0
                    for i, (t0, n) in enumerate(TILES):
                        for q in range(2):
                            dve.wait_ge(s_mm, 4 + u)
                            dve.tensor_copy(xT[:, 4 * q:4 * q + 4, t0:t0 + n],
                                            PS[:, u % 2, :].rearrange("p (j n) -> p j n", j=4)[:, :, 0:n]).then_inc(s_ev, 1)
                            u += 1
                    dve.wait_ge(s_ev, 13)
                    for w in (G1POST, G2POST):
                        dve.wait_ge(s_dch, 2)
                        dve.tensor_scalar(gT[:, 8 * w:8 * w + 8], gT[:, 8 * w:8 * w + 8], 0.5, None, ALU.mult).then_inc(s_ev, 1)
                    for k in range(1, KD):
                        nrm.add(dve, k)
                    for c in range(2):
                        dve.wait_ge(mm, 2 * c + 2)
                        dve.tensor_copy(pe_c[:, c:c + 1], PS[:, 2 + c, N_KV * ALL_PAGES:N_KV * ALL_PAGES + 1]).then_inc(s_added, 1)
                        dve.wait_ge(s_added, c + 1)
                        dve.tensor_scalar(ck[:, c, :, :], PS[:, 2 + c, 0:N_KV * ALL_PAGES].rearrange("p (n h) -> p h n", h=N_KV),
                                          pe_c[:, c:c + 1], None, ALU.add).then_inc(s_ck, 1)
                    dve.wait_ge(s_t, 1)
                    dve.tensor_copy(vc_all[:, :, :].rearrange("n a (h e) -> n h a e", h=N_KV),
                                    PS[0:ALL_PAGES, 4, :].rearrange("n (h a e) -> n h a e", h=N_KV, a=2)).then_inc(s_vc, 1)

        class Split:

            def __init__(self, name, o, *dims):
                n = int(np.prod(dims))
                self.h, self.l = part(name + "_h", o, *dims, dt=F32R), part(name + "_l", o + n, *dims, dt=F32R)
                self.h_f32 = self.h.bitcast(F32)

        HALF = T // 2

        def both(bank):
            return PS[:, bank:bank + 2, 0:HALF]

        def cut(row):
            return row.rearrange("p (a n) -> p a n", a=2)

        def product(pe, bank, w, wk, x, xk, start, stop):
            passes = [(w.h, x.h), (w.h, x.l), (w.l, x.h)]
            for j, (a, b) in enumerate(passes):
                for half in range(2):
                    m = pe.matmul(PS[:, bank + half, 0:HALF], a[:, wk, :], b[:, xk, half * HALF:(half + 1) * HALF],
                                  start=start and j == 0, stop=stop and j == 2)
            return m

        class Norm:

            def __init__(self, tag, src):
                self.src = src
                self.sq, self.acc, self.tot, self.root, self.r = (sem(tag + n) for n in ("_sq", "_acc", "_tot", "_root", "_rstd"))

            def square(self, act, k):
                if k >= 3:
                    act.wait_ge(self.acc, k - 2)
                act.activation(sqr[:, k % 2, :] if k else sacc[:, :], self.src[:, k, :], ACT.Square,
                               scale=D_MODEL ** -0.5).then_inc(self.sq, 1)

            def add(self, dve, k):
                dve.wait_ge(self.sq, k + 1)
                if k > 1:
                    dve.wait_ge(self.acc, k - 1)
                dve.tensor_tensor(sacc[:, :], sacc[:, :], sqr[:, k % 2, :], ALU.add).then_inc(self.acc, 1)

            def total(self, pe):
                pe.wait_ge(self.acc, KD - 1)
                for half in range(2):
                    m = pe.matmul(PS[:, 6 + half, 0:HALF], sq6[:, ONES, :], sacc[:, half * HALF:(half + 1) * HALF], start=True, stop=True)
                m.then_inc(self.tot, 1)

            def take_root(self, act):
                act.wait_ge(self.tot, 1)
                act.activation(cut(rstd[:, :]), both(6), ACT.Sqrt, bias=eps_sb[:, 0:1]).then_inc(self.root, 1)

            def invert(self, dve):
                dve.wait_ge(self.root, 1)
                dve.reciprocal(rstd[:, :], rstd[:, :]).then_inc(self.r, 1)
                dve.wait_ge(self.r, 1)

        def project_out(tag, w, kc, x, y, o_round, o_raw, gain, source=None, follow=None, beside=None):
            kp = kc // 2
            raw = [part(f"{tag}_raw{s}", o_raw + s * kp * P, kp, P) for s in range(2)]
            ws = [Split(f"{tag}_w{s}", o_round + 2 * s * kp * P, kp, P) for s in range(2)]
            land, s_h, s_l, mm = ([sem(f"{tag}_{n}{s}") for s in range(2)] for n in ("land", "wh", "wl", "mm"))
            done, ev, s_src_h, s_src, s_w, s_res = (sem(f"{tag}_{n}") for n in ("done", "ev", "xh", "xl", "scaled", "res"))
            nrm = Norm(tag + "_post", y)
            wv = w.rearrange("(k p) n -> p k n", p=P)
            with nc.Block() as block:
                @block.sync
                def _(sp):
                    for m in turns(sp, True, KD):
                        for s in range(2):
                            if not known(m):
                                sp.wait_ge(s_l[s], m)
                            sp.dma_start(raw[s], wv[:, s * kp:(s + 1) * kp, bass.ds(m * P, P)]).then_inc(land[s], 16)
                        if beside is not None:
                            beside(sp, m)

                @block.tensor
                def _(pe):
                    for i in turns(pe, True, KD // 2):
                        for c in range(2):
                            m = 2 * i + c
                            for s in range(2):
                                pe.wait_ge(s_l[s], m + 1)
                                if s == 0 and not (known(m) and m < 2):
                                    pe.wait_ge(ev, m - 1)
                                for k in range(kp):
                                    if source is not None and known(m) and m == 0:
                                        pe.wait_ge(s_src, s * kp + k + 1)
                                    last = product(pe, 2 * c, ws[s], k, x, s * kp + k, s == 0 and k == 0, s == 1 and k == kp - 1)
                                last.then_inc(mm[s], 1)
                    nrm.total(pe)
                    if follow is not None:
                        follow.total(pe)

                @block.scalar
                def _(act):
                    def round_piece(s, m):
                        act.wait_ge(land[s], (m + 1) * 16)
                        if not (known(m) and m == 0):
                            act.wait_ge(mm[s], m)
                        act.copy(ws[s].h, raw[s]).then_inc(s_h[s], 1)
                    for s in range(2):
                        round_piece(s, 0)
                    if source is not None:
                        for k in range(kc):
                            act.copy(x.h[:, k, :], source[:, k, :]).then_inc(s_src_h, 1)
                    for m in range(KD):
                        if m + 1 < KD:
                            for s in range(2):
                                round_piece(s, m + 1)
                        act.wait_ge(ev, m + 1)
                        nrm.square(act, m)
                    nrm.take_root(act)
                    if follow is not None:
                        for k in range(KD):
                            act.wait_ge(s_res, k + 1)
                            follow.square(act, k)
                        follow.take_root(act)

                @block.gpsimd
                def _(pool):
                    if follow is not None:
                        for k in range(1, KD):
                            follow.add(pool, k)

                @block.vector
                def _(dve):
                    def rest_of_piece(s, m):
                        dve.wait_ge(s_h[s], m + 1)
                        dve.tensor_tensor(ws[s].l, raw[s], ws[s].h_f32, ALU.subtract).then_inc(s_l[s], 1)
                    for s in range(2):
                        rest_of_piece(s, 0)
                    if source is not None:
                        for k in range(kc):
                            dve.wait_ge(s_src_h, k + 1)
                            dve.tensor_tensor(x.l[:, k, :], source[:, k, :], x.h_f32[:, k, :], ALU.subtract).then_inc(s_src, 1)
                    for m in range(KD):
                        if m + 1 < KD:
                            for s in range(2):
                                rest_of_piece(s, m + 1)
                        dve.wait_ge(mm[1], m + 1)
                        dve.tensor_copy(cut(y[:, m, :]), both(2 * (m % 2))).then_inc(ev, 1)
                        if m > 1:
                            nrm.add(dve, m - 1)
                    nrm.add(dve, KD - 1)
                    nrm.invert(dve)
                    for k in range(KD):
                        dve.scalar_tensor_tensor(y[:, k, :], y[:, k, :], gT[:, 8 * gain + k:8 * gain + k + 1],
                                                 rstd[:, :], ALU.mult, ALU.mult).then_inc(s_w, 1)
                        if k:
                            dve.wait_ge(s_w, k)
                            dve.tensor_tensor(xT[:, k - 1, :], xT[:, k - 1, :], y[:, k - 1, :], ALU.add).then_inc(s_res, 1)
                    dve.wait_ge(s_w, KD)
                    dve.tensor_tensor(xT[:, KD - 1, :], xT[:, KD - 1, :], y[:, KD - 1, :], ALU.add).then_inc(s_res, 1)

        def copies(sp, m):
            sp.dma_start(scr_t.ap()[bass.ds(2 * m, 2), :, :], scr_r.ap()[bass.ds(2 * m, 2), FIRST_T:FIRST_T + LEN_T].unsqueeze(1)
                         .to_broadcast([2, P, LEN_T])).then_inc(s_tables, 16)
            sp.dma_start(out["s_win_kv"][0, bass.ds(m, 1), 0:WINDOW - DEC_SEQ].rearrange("b t h c d -> b t (h c d)"),
                         io["cache_win_kv"][0, bass.ds(m, 1), DEC_SEQ:WINDOW].rearrange("b t h c d -> b t (h c d)")).then_inc(s_out, 16)

        def ffn(tag, w_in, w_out, pre, post, nrm, follow=None, beside=None):
            x = Split(tag + "_x", 0, KD, T)
            h = Split(tag + "_h", 2 * KD * T, KF, T)
            o = 2 * KD * T + 2 * KF * T
            ws = [Split(f"{tag}_w{side}", o + side * 2 * KD * P, KD, P) for side in range(2)]
            raw = [part(f"{tag}_raw{side}", o + (4 + side) * KD * P, KD, P) for side in range(2)]
            o += 6 * KD * P
            silu = [part(f"{tag}_silu{c}", o + c * T, T) for c in range(2)]
            tmp = [part(f"{tag}_prod{c}", o + (2 + c) * T, T) for c in range(2)]
            land, s_h, s_l, mm = ([sem(f"{tag}_{n}{s}") for s in range(2)] for n in ("land", "wh", "wl", "mm"))
            s_silu, s_prod, s_hh, s_hl, s_x, s_xh, s_xl = (sem(f"{tag}_{n}") for n in ("silu", "prod", "hh", "hl", "x", "xh", "xl"))
            wv = w_in.rearrange("(k p) n -> p k n", p=P)
            xt = silu + [tmp[0]]
            with nc.Block() as block:
                @block.sync
                def _(sp):
                    for c in turns(sp, True, KF):
                        for side in range(2):
                            if not known(c):
                                sp.wait_ge(s_l[side], c)
                            sp.dma_start(raw[side], wv[:, :, bass.ds(c * P + side * D_FF, P)]).then_inc(land[side], 16)

                @block.tensor
                def _(pe):
                    for i in turns(pe, True, KF // 2):
                        for j in range(2):
                            c = 2 * i + j
                            for side in range(2):
                                pe.wait_ge(s_l[side], c + 1)
                                if side == 0 and not (known(c) and c < 2):
                                    pe.wait_ge(s_prod, c - 1)
                                for k in range(KD):
                                    if known(c) and c == 0 and side == 0:
                                        pe.wait_ge(s_xl, k + 1)
                                    m = product(pe, 4 * j + 2 * side, ws[side], k, x, k, k == 0, k == KD - 1)
                                m.then_inc(mm[side], 1)

                @block.scalar
                def _(act):
                    def round_piece(side, c):
                        act.wait_ge(land[side], (c + 1) * 16)
                        if not (known(c) and c == 0):
                            act.wait_ge(mm[side], c)
                        act.copy(ws[side].h, raw[side]).then_inc(s_h[side], 1)
                    for side in range(2):
                        round_piece(side, 0)
                    for k in range(KD):
                        act.wait_ge(s_x, k + 1)
                        act.copy(x.h[:, k, :], xt[k % 3]).then_inc(s_xh, 1)
                    for i in turns(act, False, KF // 2):
                        for j in range(2):
                            c = 2 * i + j
                            last = known(c) and c == KF - 1
                            if not last:
                                round_piece(0, c + 1)
                            act.wait_ge(mm[0], c + 1)
                            act.activation(cut(silu[j]), both(4 * j), ACT.Silu).then_inc(s_silu, 1)
                            if not last:
                                round_piece(1, c + 1)
                            act.wait_ge(s_prod, c + 1)
                            act.copy(h.h[:, bass.ds(c, 1), :].rearrange("p a n -> p (a n)"), tmp[j]).then_inc(s_hh, 1)

                @block.vector
                def _(dve):
                    def rest_of_piece(side, c):
                        dve.wait_ge(s_h[side], c + 1)
                        dve.tensor_tensor(ws[side].l, raw[side], ws[side].h_f32, ALU.subtract).then_inc(s_l[side], 1)

                    def rest_of_x(k):
                        dve.wait_ge(s_xh, k + 1)
                        dve.tensor_tensor(x.l[:, k, :], xt[k % 3], x.h_f32[:, k, :], ALU.subtract).then_inc(s_xl, 1)
                    nrm.invert(dve)
                    rest_of_piece(0, 0)
                    for k in range(KD):
                        if k >= 3:
                            dve.wait_ge(s_xl, k - 2)
                        dve.scalar_tensor_tensor(xt[k % 3], xT[:, k, :], gT[:, 8 * pre + k:8 * pre + k + 1],
                                                 rstd[:, :], ALU.mult, ALU.mult).then_inc(s_x, 1)
                        if k:
                            rest_of_x(k - 1)
                    rest_of_x(KD - 1)
                    rest_of_piece(1, 0)
                    for i in turns(dve, False, KF // 2):
                        for j in range(2):
                            c = 2 * i + j
                            last = known(c) and c == KF - 1
                            if not last:
                                rest_of_piece(0, c + 1)
                            dve.wait_ge(s_silu, c + 1)
                            dve.wait_ge(mm[1], c + 1)
                            if not known(c) or c >= 2:
                                dve.wait_ge(s_hl, c - 1)
                            dve.tensor_tensor(cut(tmp[j]), cut(silu[j]), both(4 * j + 2), ALU.mult).then_inc(s_prod, 1)
                            if not last:
                                rest_of_piece(1, c + 1)
                            dve.wait_ge(s_hh, c + 1)
                            row = bass.ds(c, 1)
                            dve.tensor_tensor(h.l[:, row, :].rearrange("p a n -> p (a n)"), tmp[j],
                                              h.h_f32[:, row, :].rearrange("p a n -> p (a n)"), ALU.subtract).then_inc(s_hl, 1)
            kp = KF // 2
            project_out(tag + "_out", w_out, KF, h, at(o - 6 * KD * P, KD, T), 0, o - 6 * KD * P + KD * T, post, follow=follow, beside=beside)
            assert 4 * kp * P <= 2 * KD * T

        O_OT = 0
        O_Q = O_OT + 16 * T
        O_NAT = O_Q + 8 * T
        O_SM = O_NAT + 3 * 5 * 512
        O_Z = O_SM + 5 * 64
        O_U = O_Z + 8 * T
        O_XP = O_U + KC_XBC * T
        O_END = O_XP + KC_XBC * XP
        O_FREE_CMP = O_Z + 5 * ATT_WIDTH + 5 * 48 + 256 + 2 * 2 * SEQ + 2368
        oT, qT, nat, gdt = part("mixed", O_OT, 16, T), at(O_Q, 8, T), at(O_NAT, 3, 5, 512), at(O_SM, 5, 64)
        zT, uT, xp = at(O_Z, 8, T), at(O_U, KC_XBC, T), at(O_XP, KC_XBC, XP)
        w_in = io["w_in"].rearrange("a k n -> (a k) n").rearrange("(k p) n -> p k n", p=P)

        QDP = 32
        wc = [at(O_FREE_CMP + s * QDP * P, QDP, 2, HD) for s in range(2)]
        s_cmp_w = [sem(f"cmp_w{s}", True) for s in range(2)]
        s_cmp_z = [sem(f"cmp_z{s}", True) for s in range(2)]

        def load_cmp(sp, q):
            w = io["w_cmp"].rearrange("a l c d e -> (a l) (c d) e")
            with nc.allow_non_contiguous_dma(reason="rows of 256 bytes"):
                for half in range(2):
                    sp.dma_start(wc[q % 2][64 * half:64 * half + 64, :, half, :], w[:, QDP * q:QDP * q + QDP, :]).then_inc(s_cmp_w[q % 2], 16)

        def mixer_in(nrm):
            xn = part("mk_xn_rows", O_U, KD, T)
            NP, WP = 6, KV_WIDTH // 2
            kvr = [part(f"mk_raw{s}", O_XP + s * KD * WP, KD, WP) for s in range(2)]
            kvw = [Split(f"mk_w{s}", o, KD, WP) for s, o in enumerate((O_Q, O_Z))]
            smw = at(O_U + KD * T, KD, 64)
            gates = at(O_U + KD * T + KD * 64, T)
            raw = [part(f"mq_raw{s}", -(-O_END // 8) * 8 + s * KD * P, KD, P) for s in range(2)]
            land_q = [sem(f"mq_land_q{s}") for s in range(2)]

            def load_q(sp, pair, g):
                for e in range(2):
                    sp.dma_start(raw[pair][:, :, 64 * e:64 * e + 64],
                                 w_in[:, :, bass.ds((8 * pair + 4 * e + g) * 64, 64)]).then_inc(land_q[pair], 16)
            xh = Split("mk_x", O_OT, KD, T)
            s_xn, s_h, s_xl = sem("mk_xn"), sem("mk_xh"), sem("mk_xl")
            land = [sem(f"mk_w{s}") for s in range(2)]
            s_sw, mm, ev, s_wh, s_wl, s_mm2, s_ev2 = (sem("mk_" + n) for n in ("sw", "mm", "ev", "wh", "wl", "mm2", "ev2"))
            NT = len(TILES)
            with nc.Block() as block:
                @block.sync
                def _(sp):
                    with nc.allow_non_contiguous_dma(reason="the narrow columns of gates and dt"):
                        sp.dma_start(smw[:, :, 0:48], w_in[:, :, COL_GATES:COL_GATES + 48]).then_inc(s_sw, 16)
                        sp.dma_start(smw[:, :, 48:64], w_in[:, :, COL_DT:COL_DT + 16]).then_inc(s_sw, 16)
                    for p in range(NP):
                        if p >= 2:
                            sp.wait_ge(mm, NT * (p - 1))
                        sp.dma_start(kvr[p % 2], w_in[:, :, COL_KV + p * WP:COL_KV + (p + 1) * WP]).then_inc(land[p % 2], 16)
                    with nc.allow_non_contiguous_dma(reason="rows of 256 bytes"):
                        for pair in range(2):
                            load_q(sp, pair, 0)
                    for br in range(3):
                        sp.wait_ge(ev, 2 * NT * (br + 1))
                        pdst = [out["p_cmp_kv"], out["p_slc_kv"], out["p_win_kv"]][br]
                        sp.dma_start(pdst.rearrange("a b (i p) h c d -> p (a b i) (h c d)", p=P), nat[:, br, 0:4, :]).then_inc(s_out, 16)
                        if br < 2:
                            sdst = [out["s_cmp_kv"], out["s_slc_kv"]][br]
                            sp.dma_start(sdst.rearrange("a b t h c d -> (a b t) (h c d)"), nat[0:NS, br, 4, :]).then_inc(s_out, 16)
                        else:
                            for b in range(DEC_BATCH):
                                sp.dma_start(out["s_win_kv"][0, b, WINDOW - DEC_SEQ:WINDOW].rearrange("t h c d -> t (h c d)"),
                                               nat[b * 8:b * 8 + 8, 2, 4, :]).then_inc(s_out, 16)
                    outs[0] += 3 + 2 + 8 + DEC_BATCH

                @block.tensor
                def _(pe):
                    pe.wait_ge(s_sw, 32)
                    for k in range(KD):
                        pe.wait_ge(s_xn, k + 1)
                        for half in range(2):
                            m = pe.matmul(PS[0:64, 6 + half, 0:HALF], smw[:, k, :], xn[:, k, half * HALF:(half + 1) * HALF],
                                          start=(k == 0), stop=(k == KD - 1))
                    m.then_inc(s_mm2, 1)
                    pe.wait_ge(s_xl, KD)
                    u = 0
                    for p in range(NP):
                        w, r = kvw[p % 2], kvr[p % 2]
                        pe.wait_ge(s_wl, p + 1)
                        for i, (t0, n) in enumerate(TILES):
                            if u >= 4:
                                pe.wait_ge(ev, u - 3)
                            bank = PS[0:n, u % 4, 0:WP]
                            for k in range(KD):
                                if n < P:
                                    m = pe.matmul(bank, xn[:, k, t0:t0 + n], r[:, k, :], start=(k == 0), stop=(k == KD - 1))
                                    continue
                                for j, (x, y) in enumerate([(xh.h, w.h), (xh.h, w.l), (xh.l, w.h)]):
                                    m = pe.matmul(bank, x[:, k, t0:t0 + n], y[:, k, :], start=(k == 0 and j == 0),
                                                  stop=(k == KD - 1 and j == 2))
                            m.then_inc(mm, 1)
                            u += 1
                        if p == 0:
                            pe.wait_ge(s_ev2, 1)
                            for i, (t0, n) in enumerate(TILES):
                                m = pe.transpose(PS[0:n, 6, i * 64:(i + 1) * 64], gates[0:64, t0:t0 + n], ident[0:64, 0:64])
                            m.then_inc(s_mm2, 1)

                @block.scalar
                def _(act):
                    for k in range(KD):
                        act.wait_ge(s_xn, k + 1)
                        act.copy(xh.h[:, k, :], xn[:, k, :]).then_inc(s_h, 1)

                    def round_piece(p):
                        act.wait_ge(land[p % 2], 16 * (p // 2 + 1))
                        if p >= 2:
                            act.wait_ge(mm, NT * (p - 1))
                        act.copy(kvw[p % 2].h, kvr[p % 2]).then_inc(s_wh, 1)
                    for p in range(2):
                        round_piece(p)
                    for p in range(NP):
                        for i, (t0, n) in enumerate(TILES):
                            u = NT * p + i
                            act.wait_ge(mm, u + 1)
                            c0 = WP * (p % 2)
                            act.copy(nat[0:n, p // 2, i, c0:c0 + WP], PS[0:n, u % 4, 0:WP]).then_inc(ev, 1)
                        if p + 2 < NP:
                            round_piece(p + 2)

                @block.vector
                def _(dve):
                    nrm.invert(dve)
                    for k in range(KD):
                        dve.scalar_tensor_tensor(xn[:, k, :], xT[:, k, :], gT[:, 8 * GMPRE + k:8 * GMPRE + k + 1],
                                                 rstd[:, :], ALU.mult, ALU.mult).then_inc(s_xn, 1)
                    for k in range(KD):
                        dve.wait_ge(s_h, k + 1)
                        dve.tensor_tensor(xh.l[:, k, :], xn[:, k, :], xh.h_f32[:, k, :], ALU.subtract).then_inc(s_xl, 1)

                    def rest_of_piece(p):
                        dve.wait_ge(s_wh, p + 1)
                        dve.tensor_tensor(kvw[p % 2].l, kvr[p % 2], kvw[p % 2].h_f32, ALU.subtract).then_inc(s_wl, 1)
                    rest_of_piece(0)
                    dve.wait_ge(s_mm2, 1)
                    dve.tensor_copy(cut(gates[0:64, :]), both(6)[0:64]).then_inc(s_ev2, 1)
                    rest_of_piece(1)
                    dve.wait_ge(s_mm2, 2)
                    dve.tensor_copy(gdt[:, 0:4, :], PS[:, 6, 0:256].rearrange("p (i n) -> p i n", i=4)).then_inc(s_ev2, 1)
                    dve.tensor_copy(gdt[0:NS, 4, :], PS[0:NS, 6, 256:320]).then_inc(s_ev2, 1)
                    for p in range(2, NP):
                        rest_of_piece(p)

            ws = [Split(f"mq_w{s}", O_U + 2 * s * KD * P, KD, P) for s in range(2)]
            land, s_h, s_l, mm, ev = ([sem(f"mq_{n}{s}") for s in range(2)] for n in ("land", "wh", "wl", "mm", "ev"))
            s_pad, s_in = sem("mq_pad"), sem("mq_in")
            stn = at(O_Z, CONV_DIM)[0:24, :]
            s_tt, s_tc = sem("mq_tt"), sem("mq_tc")
            NC = 10
            with nc.Block() as block:
                @block.sync
                def _(sp):
                    with nc.allow_non_contiguous_dma(reason="rows of 256 bytes"):
                        with sp.Fori(1, GQA) as g:
                            for pair in range(2):
                                sp.wait_ge(s_l[pair], g)
                                load_q(sp, pair, g)
                    with sp.Fori(0, NC) as i:
                        for s in range(2):
                            sp.wait_ge(s_l[s], i + GQA)
                            sp.dma_start(raw[s], w_in[:, :, bass.ds(COL_Z + (2 * i + s) * P, P)]).then_inc(land[s], 16)

                @block.tensor
                def _(pe):
                    def chunk(s, n):
                        pe.wait_ge(s_l[s], n + 1)
                        if not (known(n) and n == 0):
                            pe.wait_ge(ev[s], n)
                        for k in range(KD):
                            m = product(pe, 2 * s, ws[s], k, xh, k, k == 0, k == KD - 1)
                        m.then_inc(mm[s], 1)
                    for g in turns(pe, True, GQA):
                        for s in range(2):
                            chunk(s, g)
                    pe.wait_ge(s_in, 16)
                    for k in range(KC_XBC):
                        m = pe.transpose(PS[:, 7, k * 24:(k + 1) * 24], stn[:, k * P:(k + 1) * P], ident[0:24, 0:24])
                    m.then_inc(s_tt, 1)
                    with pe.Fori(0, NC) as i:
                        for s in range(2):
                            chunk(s, i + GQA)

                @block.scalar
                def _(act):
                    act.dma_start(stn, io["state_conv"].rearrange("a b w n -> (a b w) n")).then_inc(s_in, 16)

                    def round_piece(s, n, land_sem, value):
                        act.wait_ge(land_sem, value)
                        if not (known(n) and n == 0):
                            act.wait_ge(mm[s], n)
                        act.copy(ws[s].h, raw[s]).then_inc(s_h[s], 1)
                    for g in turns(act, True, GQA):
                        for s in range(2):
                            round_piece(s, g, land_q[s], (g + 1) * 32)
                    with act.Fori(0, NC) as i:
                        for s in range(2):
                            round_piece(s, i + GQA, land[s], (i + 1) * 16)

                @block.vector
                def _(dve):
                    def rest_of_piece(s, n):
                        dve.wait_ge(s_h[s], n + 1)
                        dve.tensor_tensor(ws[s].l, raw[s], ws[s].h_f32, ALU.subtract).then_inc(s_l[s], 1)
                    for s in range(2):
                        rest_of_piece(s, 0)
                    dve.memset(xp[:, :, 0:PAD], 0.0).then_inc(s_pad, 1)
                    with dve.Fori(0, GQA) as g:
                        for s in range(2):
                            rest_of_piece(s, g + 1)
                            dve.wait_ge(mm[s], g + 1)
                            row = qT[:, bass.ds(4 * s + g, 1), :].rearrange("p a n -> p (a n)")
                            dve.tensor_scalar(cut(row), both(2 * s), SCALE, None, ALU.mult).then_inc(ev[s], 1)
                    dve.wait_ge(s_tt, 1)
                    runs = xp[:, :, XP_S:XP].rearrange("p k (b r) -> p k b r", r=XP_RUN)
                    for k in range(KC_XBC):
                        dve.tensor_copy(runs[:, k, :, 0:PAD],
                                        PS[:, 7, k * 24:(k + 1) * 24].rearrange("p (b w) -> p b w", w=PAD)).then_inc(s_tc, 1)
                    with dve.Fori(0, 4) as i:
                        for s in range(2):
                            rest_of_piece(s, i + (GQA + 1))
                            dve.wait_ge(mm[s], i + (GQA + 1))
                            row = zT[:, bass.ds(2 * i + s, 1), :].rearrange("p a n -> p (a n)")
                            dve.tensor_copy(cut(row), both(2 * s)).then_inc(ev[s], 1)

                    def xbc(i, s):
                        dve.wait_ge(mm[s], i + (GQA + 5))
                        row = xp[:, bass.ds(2 * i + s, 1), :].rearrange("p a n -> p (a n)")
                        rest = SEQ - HALF
                        dve.tensor_copy(row[:, PAD:PAD + HALF], PS[:, 2 * s, 0:HALF])
                        dve.tensor_copy(row[:, PAD + HALF:XP_S], PS[:, 2 * s + 1, 0:rest])
                        dve.tensor_copy(row[:, XP_S:XP].rearrange("p (b r) -> p b r", r=XP_RUN)[:, :, PAD:XP_RUN],
                                        PS[:, 2 * s + 1, rest:HALF].rearrange("p (b r) -> p b r", r=DEC_SEQ)).then_inc(ev[s], 1)
                    with dve.Fori(0, 5) as i:
                        for s in range(2):
                            rest_of_piece(s, i + (GQA + 5))
                            xbc(i, s)
                    for s in range(2):
                        xbc(5, s)

        def finish_out():
            ynat = at(0, 5, D_MODEL)
            mm, ev = sem("fo_mm"), sem("fo_ev")
            with nc.Block() as block:
                @block.tensor
                def _(pe):
                    u = 0
                    for i, (t0, n) in enumerate(TILES):
                        for q in range(2):
                            if u >= 4:
                                pe.wait_ge(ev, u - 3)
                            for j in range(4):
                                m = pe.transpose(PS[0:n, u % 4, j * P:(j + 1) * P], xT[:, 4 * q + j, t0:t0 + n], ident)
                            m.then_inc(mm, 1)
                            u += 1

                @block.vector
                def _(dve):
                    u = 0
                    for i, (t0, n) in enumerate(TILES):
                        for q in range(2):
                            dve.wait_ge(mm, u + 1)
                            dve.tensor_copy(ynat[0:n, i, 512 * q:512 * q + 512], PS[0:n, u % 4, :]).then_inc(ev, 1)
                            u += 1

                @block.sync
                def _(sp):
                    for i in range(5):
                        sp.wait_ge(ev, 2 * i + 2)
                        if i < 4:
                            sp.dma_start(out["y_prompt"][0, i * P:(i + 1) * P, :], ynat[:, i, :]).then_inc(s_out, 16)
                        else:
                            sp.dma_start(out["y_sample"].rearrange("b t d -> (b t) d"), ynat[0:NS, 4, :]).then_inc(s_out, 16)
                        outs[0] += 1
                    sp.wait_ge(s_out, 16 * outs[0])

        s_out = sem("outputs", True)
        outs = [0]
        def conv():
            cv = [at(O_END, XP), at(O_END + XP, XP)]
            last = at(O_END + 2 * XP, KC_XBC, 27)
            rows = at(O_OT + 8 * T, CONV_DIM)[0:27, :]
            s_cv, s_u, s_last, s_t, s_row, s_z = (sem("cv_" + n) for n in ("taps", "silu", "last", "t", "row", "z"))
            with nc.Block() as block:
                @block.vector
                def _(dve):
                    n = 0
                    for k0 in range(0, KC_XBC, 2):
                        for w in range(CONV_W):
                            for j in range(2):
                                k = k0 + j
                                o = cv[j][:, 0:CONV_N]
                                tap = convT[:, w * KC_XBC + k:w * KC_XBC + k + 1]
                                if w == 0:
                                    if k >= 2:
                                        dve.wait_ge(s_u, k - 1)
                                    ins = dve.tensor_scalar(o, xp[:, k, 0:CONV_N], tap,
                                                            convT[:, 4 * KC_XBC + k:4 * KC_XBC + k + 1], ALU.mult, ALU.add)
                                else:
                                    dve.wait_ge(s_cv, n - 1)
                                    ins = dve.scalar_tensor_tensor(o, xp[:, k, w:w + CONV_N], tap, o, ALU.mult, ALU.add)
                                ins.then_inc(s_cv, 1)
                                n += 1
                    dve.wait_ge(s_t, 1)
                    for b in range(3):
                        dve.tensor_copy(rows[:, 512 * b:512 * b + 512], PS[0:27, b, :]).then_inc(s_row, 1)

                @block.scalar
                def _(act):
                    for k in range(KC_XBC):
                        act.wait_ge(s_cv, 8 * (k // 2) + 7 + k % 2)
                        c = cv[k % 2]
                        act.activation(uT[:, k, 0:SEQ], c[:, 0:SEQ], ACT.Silu)
                        act.activation(uT[:, k, SEQ:T].rearrange("p (b t) -> p b t", t=DEC_SEQ),
                                       c[:, XP_S:XP].rearrange("p (b r) -> p b r", r=XP_RUN)[:, :, 0:DEC_SEQ],
                                       ACT.Silu).then_inc(s_u, 1)
                    act.activation(zT[:, :, :], zT[:, :, :], ACT.Silu).then_inc(s_z, 1)

                @block.gpsimd
                def _(pool):
                    pool.tensor_copy(last[:, :, 0:PAD], xp[:, :, XP_S - PAD:XP_S]).then_inc(s_last, 1)
                    pool.tensor_copy(last[:, :, PAD:27].rearrange("p k (b w) -> p k b w", w=PAD),
                                     xp[:, :, XP_S:XP].rearrange("p k (b r) -> p k b r", r=XP_RUN)[:, :, :, DEC_SEQ:XP_RUN]
                                     ).then_inc(s_last, 1)

                @block.tensor
                def _(pe):
                    pe.wait_ge(s_last, 2)
                    for k in range(KC_XBC):
                        m = pe.transpose(PS[0:27, k // 4, (k % 4) * P:(k % 4 + 1) * P], last[:, k, :], ident)
                    m.then_inc(s_t, 1)

                @block.sync
                def _(sp):
                    sp.wait_ge(s_row, 3)
                    sp.dma_start(out["p_conv"].rearrange("a b w n -> (a b w) n"), rows[0:PAD, :]).then_inc(s_out, 16)
                    sp.dma_start(out["s_conv"].rearrange("a b w n -> (a b w) n"), rows[PAD:27, :]).then_inc(s_out, 16)
                    outs[0] += 2
                    sp.wait_ge(s_out, 16 * outs[0])

        def ssd():
            o = O_XP
            xdt = at(o, N_HEADS, HD)
            xe = at(o + 1024, N_HEADS, HD)
            larep = at(o + 2048, N_HEADS, HD)
            mb = [at(o + 3072, 4, P), at(o + 3584, 4, P)]
            ecs = at(o + 4096, 8, P)
            st = at(o + 5120, N_HEADS, HD)
            bnat = at(o + 6144, 2, P)
            cbm = at(o + 6400, 2, P)
            yt = at(o + 6656, 2, 512)
            bm = at(o + 7680, 2, 256)
            dtv = at(o + 8192, 7, 80)
            ted = at(o + 8752, 2, 16)
            nla = at(o + 8784, 80)
            h0 = [at(O_OT + 1024 * s, 8, P) for s in range(3)]
            h0t = at(O_OT + 3072, 8, P)
            names = ("dch", "ach", "la", "xs", "small", "cb", "cs", "diff", "yoff", "yd", "st", "lar", "xdt", "bn", "cbm",
                     "mn", "mm", "xe", "y", "sup", "te", "ecs", "ee", "h0t", "h0c", "new", "bmk", "hn",
                     "pst", "psc", "e", "l")
            S = {n: sem("ss_" + n) for n in names}
            s_h0 = [sem(f"ss_h0_{s}") for s in range(3)]
            s_ho = [sem(f"ss_ho_{s}") for s in range(3)]
            NC = len(TILES)
            states = io["state_ssm"].rearrange("a b (k e) p n -> (a b) (e p) k n", e=2)
            s_states = out["s_ssm"].rearrange("a b (k e) p n -> (a b) (e p) k n", e=2)

            with nc.Block() as block:
                @block.sync
                def _(sp):
                    for b in range(DEC_BATCH):
                        if b >= 3:
                            sp.wait_ge(s_ho[b % 3], 16 * (b // 3))
                        sp.dma_start(h0[b % 3], states[b]).then_inc(s_h0[b % 3], 16)
                        if b >= 1:
                            sp.wait_ge(S["hn"], b)
                            sp.dma_start(s_states[b - 1], h0[(b - 1) % 3]).then_inc(s_ho[(b - 1) % 3], 16)
                    sp.wait_ge(S["hn"], DEC_BATCH)
                    sp.dma_start(s_states[DEC_BATCH - 1], h0[(DEC_BATCH - 1) % 3]).then_inc(s_ho[(DEC_BATCH - 1) % 3], 16)
                    for s in range(3):
                        sp.wait_ge(s_ho[s], 16 * ((DEC_BATCH + 2 - s) // 3))
                    sp.wait_ge(S["psc"], 2)
                    sp.dma_start(out["p_ssm"][0, 0].rearrange("(k e) p n -> (e p) k n", e=2), h0[0]).then_inc(s_out, 16)
                    outs[0] += 1
                    sp.wait_ge(s_out, 16 * outs[0])

                @block.tensor
                def _(pe):
                    pe.wait_ge(S["la"], 2)
                    for c, (t0, n) in enumerate(TILES):
                        sample = c == NC - 1
                        tri = sq6[0:n, BTRI if sample else TRI, 0:n]
                        one = sq6[0:n, BONES if sample else ONES, 0:n]
                        la = dtv[0:n, 6, 16 * c:16 * c + 16]
                        if c:
                            pe.wait_ge(S["y"], 2 * c)
                            pe.wait_ge(S["sup"], 2 * c)
                        for k in range(8):
                            pe.transpose(PS[0:n, k // 4, (k % 4) * P:(k % 4 + 1) * P], uT[:, k, t0:t0 + n], ident)
                        for g in range(2):
                            m = pe.transpose(PS[0:n, 2, g * P:(g + 1) * P], uT[:, 8 + g, t0:t0 + n], ident)
                        m.then_inc(S["xs"], 1)
                        pe.matmul(PS[0:n, 2, 256:272], one, la, start=True, stop=True)
                        pe.matmul(PS[0:n, 2, 272:288], tri, la, start=True, stop=True).then_inc(S["small"], 1)
                        for g in range(2):
                            m = pe.matmul(PS[0:n, 3, g * P:g * P + n], uT[:, 8 + g, t0:t0 + n], uT[:, 10 + g, t0:t0 + n],
                                          start=True, stop=True)
                        m.then_inc(S["cb"], 1)
                        pe.wait_ge(S["lar"], c + 1)
                        for k in range(8):
                            if k % 4 == 0 and c:
                                pe.wait_ge(S["mn"], 4 * c - 1 + k // 4)
                            m = pe.matmul(PS[:, 4 + k // 4, (k % 4) * P:(k % 4) * P + n],
                                          larep[0:n, 2 * k:2 * k + 2, :].rearrange("p a b -> p (a b)"), tri, start=True, stop=True)
                            if k % 4 == 3:
                                m.then_inc(S["cs"], 1)
                        for q in range(4):
                            if q < 2:
                                pe.wait_ge(S["ecs"], 2 * c + q + 1)
                            else:
                                pe.wait_ge(S["mn"], 4 * c + q - 1)
                            bank = 4 + q % 2
                            for j in range(4):
                                pe.matmul(PS[0:n, bank, j * P:j * P + n], dtv[0:n, 6, 16 * c + 4 * q + j:16 * c + 4 * q + j + 1]
                                          .to_broadcast([n, n]), tri, start=True, stop=False)
                                m = pe.matmul(PS[0:n, bank, j * P:j * P + n], tri,
                                              nla[0:n, 16 * c + 4 * q + j:16 * c + 4 * q + j + 1].to_broadcast([n, n]),
                                              start=False, stop=True)
                            m.then_inc(S["diff"], 1)
                        if not sample:
                            pe.wait_ge(S["xdt"], c + 1)
                            if c == 0:
                                pe.wait_ge(S["e"], 1)
                            for k in range(8):
                                m = pe.matmul(PS[:, k // 4, (k % 4) * P:(k % 4) * P + n],
                                              st[:, 2 * k:2 * k + 2, :].rearrange("p a b -> p (a b)"),
                                              uT[:, 10 + k // 4, t0:t0 + n], start=True, stop=True)
                            m.then_inc(S["yoff"], 1)
                        pe.wait_ge(S["xdt"], c + 1)
                        for q in range(4):
                            pe.wait_ge(S["mm"], 4 * c + q + 1)
                            for j in range(4):
                                h = 4 * q + j
                                m = pe.matmul(PS[64 * (h % 2):64 * (h % 2) + 64, 6 + h // 8, (h // 2 % 4) * P:(h // 2 % 4) * P + n],
                                              xdt[0:n, h, :], mb[q % 2][0:n, j, 0:n], start=True, stop=True)
                            m.then_inc(S["yd"], 1)
                        pe.wait_ge(S["xe"], c + 1)
                        if not sample:
                            pe.wait_ge(S["bn"], c + 1)
                            pe.wait_ge(S["te"], c + 1)
                            pe.wait_ge(S["cbm"], c + 1)
                            for g in range(2):
                                m = pe.matmul(PS[:, 2 + g, :], bnat[0:n, g, :],
                                              xe[0:n, 8 * g:8 * g + 8, :].rearrange("p a b -> p (a b)"), start=True, stop=True)
                            m.then_inc(S["st"], 1)
                    n = NS
                    pe.wait_ge(S["cbm"], NC)
                    for b in range(DEC_BATCH):
                        pe.wait_ge(s_h0[b % 3], 16 * (b // 3 + 1))
                        if b == 0:
                            pe.wait_ge(S["mn"], 4 * NC)
                        else:
                            pe.wait_ge(S["h0c"], 2 * b)
                        for k in range(8):
                            m = pe.transpose(PS[:, 4 + k // 4, (k % 4) * P:(k % 4 + 1) * P], h0[b % 3][:, k, :], ident)
                        m.then_inc(S["h0t"], 1)
                        pe.wait_ge(S["bmk"], b + 1)
                        if b:
                            pe.wait_ge(S["hn"], b)
                        for k in range(8):
                            m = pe.matmul(PS[:, 2 + k // 4, (k % 4) * P:(k % 4 + 1) * P],
                                          xe[0:n, 2 * k:2 * k + 2, :].rearrange("p a b -> p (a b)"),
                                          bm[0:n, b % 2, (k // 4) * P:(k // 4 + 1) * P], start=True, stop=True)
                        m.then_inc(S["new"], 1)
                        pe.wait_ge(S["h0c"], 2 * b + 2)
                        for k in range(8):
                            m = pe.matmul(PS[:, k // 4, (k % 4) * P + 8 * b:(k % 4) * P + 8 * b + 8], h0t[:, k, :],
                                          uT[:, 10 + k // 4, SEQ + 8 * b:SEQ + 8 * b + 8], start=True, stop=True)
                        m.then_inc(S["yoff"], 1)
                    for k in range(8):
                        m = pe.transpose(PS[:, 4 + k // 4, (k % 4) * P:(k % 4 + 1) * P],
                                         st[:, 2 * k:2 * k + 2, :].rearrange("p a b -> p (a b)"), ident)
                    m.then_inc(S["pst"], 1)

                @block.scalar
                def _(act):
                    act.wait_ge(S["l"], 1)
                    act.activation(dtv[:, 2, :], dtv[:, 1, :], ACT.Exp, scale=-1.0).then_inc(S["ach"], 1)
                    act.wait_ge(S["l"], 2)
                    act.activation(dtv[:, 4, :], dtv[:, 3, :], ACT.Ln).then_inc(S["ach"], 1)
                    for c, (t0, n) in enumerate(TILES):
                        act.wait_ge(S["bn"], c + 1)
                        act.activation(ted[0:n, :, :], ted[0:n, :, :], ACT.Exp).then_inc(S["te"], 1)
                        for g in range(2):
                            act.wait_ge(S["cs"], 2 * c + g + 1)
                            act.activation(ecs[:, 4 * g:4 * g + 4, 0:n],
                                           PS[:, 4 + g, :].rearrange("p (a n) -> p a n", a=4)[:, :, 0:n], ACT.Exp).then_inc(S["ecs"], 1)
                        for q in range(4):
                            act.wait_ge(S["mn"], 4 * c + q + 1)
                            act.activation(mb[q % 2][0:n, :, 0:n], mb[q % 2][0:n, :, 0:n], ACT.Exp).then_inc(S["ee"], 1)
                    for b in range(DEC_BATCH):
                        act.wait_ge(S["h0t"], b + 1)
                        if b:
                            act.wait_ge(S["yoff"], NC - 1 + b)
                        for g in range(2):
                            act.copy(h0t[:, 4 * g:4 * g + 4, :].rearrange("p a b -> p (a b)"), PS[:, 4 + g, :]).then_inc(S["h0c"], 1)

                @block.vector
                def _(dve):
                    ch = Chain(dve, S["dch"])
                    sm = gdt[:, :, 48:64]
                    v = lambda k: dtv[:, k, :].rearrange("p (c h) -> p c h", c=NC)
                    ch.link(dve.memset(gdt[64:P, 4, :], 0.0))
                    dve.memset(st[:, :, :], 0.0).then_inc(S["e"], 1)
                    ch.link(dve.tensor_tensor(v(0), sm, small[:, 0:1, :].to_broadcast([P, NC, 16]), ALU.add))
                    dve.scalar_tensor_tensor(v(1), v(0), -1.0, v(0), ALU.mult, ALU.max).then_inc(S["l"], 1)
                    dve.wait_ge(S["ach"], 1)
                    dve.tensor_scalar(dtv[:, 3, :], dtv[:, 2, :], 1.0, None, ALU.add).then_inc(S["l"], 1)
                    dve.wait_ge(S["ach"], 2)
                    ch.link(dve.tensor_scalar(dtv[:, 1, :], dtv[:, 3, :], -1.0, None, ALU.add))
                    ch.link(dve.tensor_tensor(dtv[:, 4, :], dtv[:, 4, :], dtv[:, 2, :], ALU.mult))
                    ch.link(dve.scalar_tensor_tensor(dtv[:, 2, :], dtv[:, 1, :], 0.0, dtv[:, 2, :], ALU.is_equal, ALU.mult))
                    ch.link(dve.tensor_scalar(dtv[:, 1, :], dtv[:, 1, :], 1e-30, None, ALU.max))
                    ch.link(dve.reciprocal(dtv[:, 1, :], dtv[:, 1, :]))
                    ch.link(dve.tensor_tensor(dtv[:, 4, :], dtv[:, 4, :], dtv[:, 1, :], ALU.mult))
                    ch.link(dve.tensor_tensor(dtv[:, 4, :], dtv[:, 4, :], dtv[:, 2, :], ALU.add))
                    ch.link(dve.scalar_tensor_tensor(dtv[:, 5, :], dtv[:, 0, :], 0.0, dtv[:, 4, :], ALU.max, ALU.add))
                    dve.tensor_tensor(v(6), v(5), small[:, 2:3, :].to_broadcast([P, NC, 16]), ALU.mult).then_inc(S["la"], 1)
                    dve.wait_ge(S["la"], 1)
                    dve.tensor_scalar(nla[:, :], dtv[:, 6, :], -1.0, None, ALU.mult).then_inc(S["la"], 1)
                    for c, (t0, n) in enumerate(TILES):
                        sample = c == NC - 1
                        tri = sq6[0:n, BTRI if sample else TRI, 0:n]
                        dt = dtv[0:n, 5, 16 * c:16 * c + 16]
                        if c:
                            dve.wait_ge(S["cs"], 2 * c)
                        dve.tensor_copy(larep[0:n, :, :], dtv[0:n, 6, 16 * c:16 * c + 16].unsqueeze(2).to_broadcast([n, 16, 64])
                                        ).then_inc(S["lar"], 1)
                        dve.wait_ge(S["xs"], c + 1)
                        for g in range(2):
                            ins = dve.tensor_tensor(xdt[0:n, 8 * g:8 * g + 8, :], PS[0:n, g, :].rearrange("p (h d) -> p h d", d=HD),
                                                    dt[:, 8 * g:8 * g + 8].unsqueeze(2).to_broadcast([n, 8, 64]), ALU.mult)
                        ins.then_inc(S["xdt"], 1)
                        dve.wait_ge(S["small"], c + 1)
                        ch.link(dve.tensor_copy(bnat[0:n, :, :], PS[0:n, 2, 0:256].rearrange("p (g n) -> p g n", g=2)))
                        if c:
                            dve.wait_ge(S["sup"], 2 * c)
                        ch.link(dve.tensor_copy(ted[0:n, 0, :], PS[0:n, 2, 256:272]))
                        dve.tensor_tensor(ted[0:n, 1, :], ted[0:n, 0, :], PS[0:n, 2, 272:288], ALU.subtract).then_inc(S["bn"], 1)
                        dve.wait_ge(S["cb"], c + 1)
                        dve.tensor_tensor(cbm[0:n, :, 0:n], PS[0:n, 3, 0:256].rearrange("p (g n) -> p g n", g=2)[:, :, 0:n],
                                          tri.unsqueeze(1).to_broadcast([n, 2, n]), ALU.mult).then_inc(S["cbm"], 1)

                        def gate(q):
                            dve.wait_ge(S["ee"], 4 * c + q + 1)
                            dve.wait_ge(S["cbm"], c + 1)
                            dve.tensor_tensor(mb[q % 2][0:n, :, 0:n], mb[q % 2][0:n, :, 0:n],
                                              cbm[0:n, q // 2, 0:n].unsqueeze(1).to_broadcast([n, 4, n]), ALU.mult).then_inc(S["mm"], 1)
                        for q in range(4):
                            dve.wait_ge(S["diff"], 4 * c + q + 1)
                            if 4 * c + q >= 2:
                                dve.wait_ge(S["yd"], 4 * c + q - 1)
                            dve.tensor_scalar(mb[q % 2][0:n, :, 0:n],
                                              PS[0:n, 4 + q % 2, :].rearrange("p (a n) -> p a n", a=4)[:, :, 0:n],
                                              0.0, None, ALU.min).then_inc(S["mn"], 1)
                            if q:
                                gate(q - 1)
                        dve.wait_ge(S["te"], c + 1)
                        dve.wait_ge(S["xdt"], c + 1)
                        dve.tensor_tensor(xe[0:n, :, :], xdt[0:n, :, :], ted[0:n, 1, :].unsqueeze(2).to_broadcast([n, 16, 64]),
                                          ALU.mult).then_inc(S["xe"], 1)
                        gate(3)
                        if sample:
                            for b in range(DEC_BATCH):
                                if b >= 2:
                                    dve.wait_ge(S["new"], b - 1)
                                dve.tensor_scalar(bm[0:n, b % 2, :], bnat[0:n, :, :].rearrange("p a b -> p (a b)"),
                                                  crow[0:n, 2, b:b + 1], None, ALU.mult).then_inc(S["bmk"], 1)
                                dve.wait_ge(S["new"], b + 1)
                                dve.wait_ge(S["h0t"], b + 1)
                                dve.wait_ge(S["ecs"], 2 * NC)
                                for k in range(8):
                                    ins = dve.scalar_tensor_tensor(
                                        h0[b % 3][:, k, :], h0[b % 3][:, k, :], ecs[:, k, 8 * b + 7:8 * b + 8],
                                        PS[:, 2 + k // 4, (k % 4) * P:(k % 4 + 1) * P], ALU.mult, ALU.add)
                                ins.then_inc(S["hn"], 1)
                            dve.wait_ge(S["yoff"], NC - 1 + DEC_BATCH)
                        else:
                            dve.wait_ge(S["yoff"], c + 1)
                        for g in range(2):
                            dve.wait_ge(S["ecs"], 2 * c + g + 1)
                            yv = yt[:, g, :].rearrange("p (a n) -> p a n", a=4)[:, :, 0:n]
                            ch.link(dve.tensor_tensor(yv, PS[:, g, :].rearrange("p (a n) -> p a n", a=4)[:, :, 0:n],
                                                      ecs[:, 4 * g:4 * g + 4, 0:n], ALU.mult))
                            dve.wait_ge(S["yd"], 4 * c + 2 * g + 2)
                            ch.link(dve.tensor_tensor(yv, yv, PS[:, 6 + g, :].rearrange("p (a n) -> p a n", a=4)[:, :, 0:n], ALU.add))
                            for j in range(4):
                                k = 4 * g + j
                                ins = dve.scalar_tensor_tensor(oT[:, 8 + k, t0:t0 + n], uT[:, k, t0:t0 + n], small[:, 3, k:k + 1],
                                                               yv[:, j, :], ALU.mult, ALU.add)
                            ins.then_inc(S["y"], 1)
                        if not sample:
                            dve.wait_ge(S["te"], c + 1)
                            dve.wait_ge(S["e"], 1)
                            if c:
                                dve.wait_ge(S["sup"], 2 * c)
                            ch.link(dve.tensor_tensor(st[:, :, :], st[:, :, :], ted[:, 0, :].unsqueeze(2).to_broadcast([P, 16, 64]),
                                                      ALU.mult))
                            dve.wait_ge(S["st"], c + 1)
                            for g in range(2):
                                sv = st[:, 8 * g:8 * g + 8, :].rearrange("p a b -> p (a b)")
                                dve.tensor_tensor(sv, sv, PS[:, 2 + g, :], ALU.add).then_inc(S["sup"], 1)
                    dve.wait_ge(S["pst"], 1)
                    dve.wait_ge(s_ho[0], 16 * ((DEC_BATCH + 2) // 3))
                    for g in range(2):
                        dve.tensor_copy(h0[0][:, 4 * g:4 * g + 4, :].rearrange("p a b -> p (a b)"), PS[:, 4 + g, :]).then_inc(S["psc"], 1)

        def ssd_gate_norm():
            s_g, s_sq, s_use, s_root, s_r, s_f = (sem("sn_" + n) for n in ("g", "sq", "use", "root", "r", "f"))
            gs = [at(O_END, T), at(O_END + T, T)]
            with nc.Block() as block:
                @block.gpsimd
                def _(pool):
                    for s in range(2):
                        pool.memset(wc[s][0:64, :, 1, :], 0.0).then_inc(s_cmp_z[s], 1)
                        pool.memset(wc[s][64:P, :, 0, :], 0.0).then_inc(s_cmp_z[s], 1)

                @block.sync
                def _(sp):
                    for q in range(2):
                        sp.wait_ge(s_cmp_z[q], 2)
                        load_cmp(sp, q)

                @block.vector
                def _(dve):
                    for k in range(8):
                        dve.tensor_tensor(oT[:, 8 + k, :], oT[:, 8 + k, :], zT[:, k, :], ALU.mult).then_inc(s_g, 1)
                    for g in range(2):
                        dve.wait_ge(s_root, 2 * g + 2)
                        dve.reciprocal(gs[g], gs[g]).then_inc(s_r, 1)
                        dve.wait_ge(s_r, g + 1)
                        for k in range(4 * g, 4 * g + 4):
                            dve.scalar_tensor_tensor(oT[:, 8 + k, :], oT[:, 8 + k, :], gT[:, 8 * GSSD + k:8 * GSSD + k + 1],
                                                     gs[g], ALU.mult, ALU.mult).then_inc(s_f, 1)

                @block.scalar
                def _(act):
                    for k in range(8):
                        act.wait_ge(s_g, k + 1)
                        if k >= 2:
                            act.wait_ge(s_use, k - 1)
                        act.activation(sqr[:, k % 2, :], oT[:, 8 + k, :], ACT.Square,
                                       scale=(SSD_INNER // SSD_GROUPS) ** -0.5).then_inc(s_sq, 1)
                    for g in range(2):
                        act.wait_ge(s_use, 4 * g + 4)
                        act.activation(gs[g][:, 0:SEQ], PS[:, 2 * g, :], ACT.Sqrt, bias=eps_sb[:, 0:1]).then_inc(s_root, 1)
                        act.activation(gs[g][:, SEQ:T], PS[:, 2 * g + 1, 0:NS], ACT.Sqrt, bias=eps_sb[:, 0:1]).then_inc(s_root, 1)

                @block.tensor
                def _(pe):
                    for k in range(8):
                        pe.wait_ge(s_sq, k + 1)
                        g = k // 4
                        pe.matmul(PS[:, 2 * g, :], sq6[:, ONES, :], sqr[:, k % 2, 0:SEQ], start=(k % 4 == 0), stop=(k % 4 == 3))
                        pe.matmul(PS[:, 2 * g + 1, 0:NS], sq6[:, ONES, :], sqr[:, k % 2, SEQ:T], start=(k % 4 == 0),
                                  stop=(k % 4 == 3)).then_inc(s_use, 1)

        O_ON = O_Z
        O_SG = O_ON + 5 * ATT_WIDTH
        O_KTN = O_SG + 5 * 48
        O_FREE = O_KTN + 256
        onat, sg, ktn = at(O_ON, 5, ATT_WIDTH), at(O_SG, 5, 48), at(O_KTN, 2, 2, NS)

        def kt_transposes(pe, bank, rows, row0=0):
            for h in range(N_KV):
                c0 = h * P - (HD if h % 2 else 0)
                m = pe.transpose(PS[:, bank, h * P:h * P + rows.shape[0]], rows[:, c0:c0 + P], ident[0:rows.shape[0], 0:rows.shape[0]])
            return m

        def kt_halves(bank, n):
            v = PS[:, bank, :].rearrange("p (a e n) -> p a e n", a=2, e=2)
            return v[0:64, :, 0, 0:n], v[64:P, :, 1, 0:n]

        def compress_prompt():
            o = O_FREE
            ktp = at(o, 2, 2, SEQ)
            o += 2048
            ckp = at(o, 2, N_KV, 4)
            kcp = at(o + 32, 2, 2, 8)
            vtmp = at(o + 64, P)
            vbd = at(o + 192, 16 * HD)
            sc = at(o + 1216, 4, P)
            mx = at(o + 1728, 2, 4 * N_HEADS)
            pT = at(o + 1856, 4, P)
            raw = at(-(-O_END // 8) * 8, 2, P)
            names = ("mm", "raw", "rt", "ck", "kc", "t", "vt", "z", "vb", "kt", "ktc", "s", "x", "e", "p", "pt", "ptc", "o", "oc", "dch", "sg")
            S = {n: sem("pc_" + n) for n in names}
            heads = lambda v: v.rearrange("p i (h n) -> p (i h) n", n=8)

            def spread(eng, half):
                for h in range(N_HEADS):
                    eng.dma_start(vbd[8 * h + 4 * half:8 * h + 4 * half + 4, HD * h:HD * h + HD],
                                  vtmp[4 * (h // GQA):4 * (h // GQA) + 4, 64 * half:64 * half + 64]).then_inc(S["vb"], 16)
            with nc.Block() as block:
                @block.sync
                def _(sp):
                    for q in range(2, 4):
                        sp.wait_ge(S["mm"], q - 1)
                        load_cmp(sp, q)
                    sp.wait_ge(S["z"], 2)
                    sp.wait_ge(S["ck"], 1)
                    for half in range(2):
                        for odd in range(2):
                            sp.dma_start(kcp[64 * odd:64 * odd + 64, :, odd, 4 * half:4 * half + 4],
                                         ckp[64 * half:64 * half + 64, 0, :, :].rearrange("p (a b) n -> p a b n", b=2)[:, :, odd, :]
                                         ).then_inc(S["kc"], 16)
                    sp.wait_ge(S["vt"], 1)
                    spread(sp, 0)

                @block.gpsimd
                def _(pool):
                    pool.memset(kcp[:, :, :, :], 0.0).then_inc(S["z"], 1)
                    pool.memset(vbd, 0.0).then_inc(S["z"], 1)

                @block.tensor
                def _(pe):
                    for q in range(4):
                        pe.wait_ge(s_cmp_w[q % 2], 32 * (q // 2 + 1))
                        for j in range(QDP):
                            c, d = (QDP * q + j) // 64, (QDP * q + j) % 64
                            base = nat[:, 0, 0:4, :]
                            rows = bass.AP(base.tensor, base.offset + c * 64 + d, [base.ap[0], [P, 16]])
                            m = pe.matmul(PS[0:16, c, 0:P], rows, wc[q % 2][:, j, :, :].rearrange("p a b -> p (a b)"),
                                          start=(d == 0), stop=(d == 63))
                        m.then_inc(S["mm"], 1)
                    pe.wait_ge(S["raw"], 2)
                    for c in range(2):
                        m = pe.transpose(PS[:, 6, 16 * c:16 * c + 16], raw[0:16, c, :], ident[0:16, 0:16])
                    m.then_inc(S["rt"], 1)
                    pe.wait_ge(S["ck"], 2)
                    pe.transpose(PS[0:16, 2, 0:P], ckp[:, 1, :, :].rearrange("p a b -> p (a b)"), ident).then_inc(S["t"], 1)
                    pe.wait_ge(S["kc"], 64)
                    for i in range(4):
                        sv = PS[:, 3, i * P:(i + 1) * P].rearrange("p (a e g n) -> p a e g n", a=2, e=2, g=GQA)
                        for c in range(8):
                            m = pe.matmul(sv[:, c // GQA, :, c % GQA, :], qT[:, c, i * P:(i + 1) * P], kcp[:, c // GQA, :, :],
                                          start=True, stop=True)
                    m.then_inc(S["s"], 1)
                    for i, (t0, n) in enumerate(TILES):
                        if i >= 2:
                            pe.wait_ge(S["ktc"], 2 * (i - 1))
                        kt_transposes(pe, 4 + i % 2, nat[0:n, 1, i, :]).then_inc(S["kt"], 1)
                    pe.wait_ge(S["vt"], 1)
                    pe.wait_ge(S["p"], 1)
                    for i in range(4):
                        m = pe.transpose(PS[:, 2, i * P:(i + 1) * P], sc[:, i, :], ident)
                    m.then_inc(S["pt"], 1)
                    pe.wait_ge(S["ptc"], 1)
                    pe.wait_ge(S["vb"], 16 * 32)
                    banks = (0, 1, 6, 7)
                    for i in range(4):
                        for g in range(2):
                            u = 2 * i + g
                            if u >= 4:
                                pe.wait_ge(S["oc"], u - 3)
                            pe.matmul(PS[:, banks[u % 4], :], pT[:, i, :], vbd[:, 512 * g:512 * g + 512], start=True, stop=True
                                      ).then_inc(S["o"], 1)

                @block.scalar
                def _(act):
                    act.activation(sg[:, :, :], gdt[:, :, 0:48], ACT.Sigmoid).then_inc(S["sg"], 1)
                    act.wait_ge(S["z"], 2)
                    act.wait_ge(S["vt"], 1)
                    spread(act, 1)
                    for i, (t0, n) in enumerate(TILES):
                        act.wait_ge(S["kt"], i + 1)
                        lo, hi = kt_halves(4 + i % 2, n)
                        dst = ktp[:, 0, :, t0:t0 + n] if i < 4 else ktn[:, 0, :, :]
                        act.copy(dst[0:64], lo).then_inc(S["ktc"], 1)
                        act.copy(dst[64:P], hi).then_inc(S["ktc"], 1)
                    act.wait_ge(S["x"], 1)
                    act.activation(sc[:, :, :], sc[:, :, :], ACT.Exp).then_inc(S["e"], 1)
                    act.wait_ge(S["pt"], 1)
                    act.copy(pT[:, :, :].rearrange("p i n -> p (i n)"), PS[:, 2, :]).then_inc(S["ptc"], 1)
                    banks = (0, 1, 6, 7)
                    for u in range(8):
                        act.wait_ge(S["o"], u + 1)
                        act.copy(onat[:, u // 2, 512 * (u % 2):512 * (u % 2) + 512], PS[:, banks[u % 4], :]).then_inc(S["oc"], 1)

                @block.vector
                def _(dve):
                    ch = Chain(dve, S["dch"])
                    for c in range(2):
                        dve.wait_ge(S["mm"], 2 * c + 2)
                        dve.tensor_copy(raw[0:16, c, :], PS[0:16, c, 0:P]).then_inc(S["raw"], 1)
                    dve.wait_ge(S["rt"], 1)
                    for c in range(2):
                        dve.tensor_scalar(ckp[:, c, :, :], PS[:, 6, 16 * c:16 * c + 16].rearrange("p (n h) -> p h n", h=N_KV),
                                          pe_c[:, c:c + 1], None, ALU.add).then_inc(S["ck"], 1)
                    dve.wait_ge(S["t"], 1)
                    dve.tensor_copy(vtmp[0:16, :], PS[0:16, 2, 0:P]).then_inc(S["vt"], 1)
                    dve.wait_ge(S["s"], 1)
                    rows = heads(sc[:, :, :])
                    spread_out = lambda v: v.unsqueeze(2).to_broadcast([P, 64, 8])
                    ch.link(dve.tensor_tensor(rows, heads(PS[:, 3, :].rearrange("p (i m) -> p i m", i=4)),
                                              bias_cmp[:, :, :, :].rearrange("p i h n -> p (i h) n"), ALU.add))
                    ch.link(dve.tensor_reduce(mx[:, 0, :], rows, AXX, ALU.max))
                    ch.link(dve.tensor_scalar(mx[:, 0, :], mx[:, 0, :], 0.1 * MASKED, None, ALU.max))
                    dve.tensor_tensor(rows, rows, spread_out(mx[:, 0, :]), ALU.subtract).then_inc(S["x"], 1)
                    dve.wait_ge(S["e"], 1)
                    ch.link(dve.tensor_reduce(mx[:, 1, :], rows, AXX, ALU.add))
                    ch.link(dve.tensor_scalar(mx[:, 1, :], mx[:, 1, :], 1e-30, None, ALU.max))
                    ch.link(dve.reciprocal(mx[:, 1, :], mx[:, 1, :]))
                    dve.wait_ge(S["sg"], 1)
                    gate = mx[:, 1, :].rearrange("p (i h) -> p i h", i=4)
                    ch.link(dve.tensor_tensor(gate, gate, sg[:, 0:4, :].rearrange("p i (h r) -> p i h r", r=3)[:, :, :, 0], ALU.mult))
                    dve.tensor_tensor(rows, rows, spread_out(mx[:, 1, :]), ALU.mult).then_inc(S["p"], 1)

        def attend_prompt():
            o = O_FREE
            ktp = at(o, 2, 2, SEQ)
            o += 2048
            mh = at(o, N_KV, SEQ)
            Sx = [at(o + 3072 + 512 * s, SEQ) for s in range(4)]
            PT = [at(o + 5120 + 512 * s, SEQ) for s in range(3)]
            st = at(o + 6656, 8, 4)
            spare = at(o + 6688, 1)
            BT, BO = 3, 6
            LAG = 4
            units = [(g, kv, br, i) for g in range(GQA) for kv in range(N_KV) for br in range(2) for i in range(4)]
            PER_G = N_KV * 2 * 4
            NU = len(units)
            names = ("kt", "ktc", "s", "x", "nm", "e", "t", "pt", "o", "b", "d1", "d2", "d3")
            S = {n: sem("pa_" + n) for n in names}
            s_mh = [sem(f"pa_mh{kv}") for kv in range(N_KV)]
            with nc.Block() as block:
                @block.sync
                def _(sp):
                    sp.wait_ge(s_tables, 16 * KD)
                    for g in range(GQA):
                        for kv in range(N_KV):
                            if g:
                                sp.wait_ge(S["x"], PER_G * (g - 1) + 8 * (kv + 1))
                            sp.dma_start(mh[:, kv, :], bass.AP(scr_t, (4 * kv + g) * P * LEN_T + P - 1, [[LEN_T - 1, P], [1, SEQ]])
                                         ).then_inc(s_mh[kv], 16)

                @block.tensor
                def _(pe):
                    for i, (t0, n) in enumerate(TILES):
                        if i >= 2:
                            pe.wait_ge(S["ktc"], 2 * (i - 1))
                        kt_transposes(pe, BO + i % 2, nat[0:n, 2, i, :]).then_inc(S["kt"], 1)
                    pe.wait_ge(S["ktc"], 2 * len(TILES))

                    def scores(u):
                        g, kv, br, i = units[u]
                        r, n = 64 * (kv % 2), (i + 1) * P
                        if u >= 3:
                            pe.wait_ge(S["x"], u - 2)
                        pe.matmul(PS[:, u % 3, 0:n], qT[r:r + 64, 4 * (kv // 2) + g, i * P:(i + 1) * P], ktp[r:r + 64, br, kv // 2, 0:n],
                                  start=True, stop=True).then_inc(S["s"], 1)

                    def values(u):
                        g, kv, br, i = units[u]
                        pe.wait_ge(S["pt"], u + 1)
                        if u >= 2:
                            pe.wait_ge(S["b"], u - 1)
                        for j in range(i + 1):
                            m = pe.matmul(PS[:, BO + u % 2, 0:HD], PT[u % 3][:, j * P:(j + 1) * P],
                                          nat[:, 1 + br, j, kv * P + HD:(kv + 1) * P], start=(j == 0), stop=(j == i))
                        m.then_inc(S["o"], 1)
                    for u in range(2):
                        scores(u)
                    for u in range(NU):
                        if u + 2 < NU:
                            scores(u + 2)
                        pe.wait_ge(S["e"], u + 1)
                        if u >= 3:
                            pe.wait_ge(S["pt"], u - 2)
                        for j in range(units[u][3] + 1):
                            m = pe.transpose(PS[:, BT + u % 3, j * P:(j + 1) * P], Sx[u % 4][:, j * P:(j + 1) * P], ident)
                        m.then_inc(S["t"], 1)
                        if u >= 2:
                            values(u - 2)
                    for u in range(NU - 2, NU):
                        values(u)

                @block.scalar
                def _(act):
                    for i, (t0, n) in enumerate(TILES):
                        act.wait_ge(S["kt"], i + 1)
                        lo, hi = kt_halves(BO + i % 2, n)
                        dst = ktp[:, 1, :, t0:t0 + n] if i < 4 else ktn[:, 1, :, :]
                        act.copy(dst[0:64], lo).then_inc(S["ktc"], 1)
                        act.copy(dst[64:P], hi).then_inc(S["ktc"], 1)

                    def to_sbuf(u):
                        n = (units[u][3] + 1) * P
                        act.wait_ge(S["t"], u + 1)
                        if u >= 3:
                            act.wait_ge(S["o"], u - 2)
                        act.copy(PT[u % 3][:, 0:n], PS[:, BT + u % 3, 0:n]).then_inc(S["pt"], 1)
                    for u in range(NU):
                        n = (units[u][3] + 1) * P
                        act.wait_ge(S["nm"], u + 1)
                        act.activation(Sx[u % 4][:, 0:n], Sx[u % 4][:, 0:n], ACT.Exp, bias=st[:, u % 8, 1:2],
                                       accum_out=st[:, u % 8, 2:3]).then_inc(S["e"], 1)
                        if u:
                            to_sbuf(u - 1)
                    to_sbuf(NU - 1)

                @block.vector
                def _(dve):
                    def invert(u):
                        dve.wait_ge(S["e"], u + 1)
                        dve.reciprocal(st[:, u % 8, 3:4], st[:, u % 8, 2:3]).then_inc(S["d1"], 1)

                    def finish(u):
                        g, kv, br, i = units[u]
                        dve.wait_ge(S["d1"], u + 1)
                        dve.tensor_tensor(st[:, u % 8, 3:4], st[:, u % 8, 3:4],
                                          sg[:, i, (4 * kv + g) * 3 + 1 + br:(4 * kv + g) * 3 + 2 + br], ALU.mult).then_inc(S["d2"], 1)
                        dve.wait_ge(S["d2"], u + 1)
                        dve.wait_ge(S["o"], u + 1)
                        dst = onat[:, i, (4 * kv + g) * HD:(4 * kv + g + 1) * HD]
                        dve.scalar_tensor_tensor(dst, PS[:, BO + u % 2, 0:HD], st[:, u % 8, 3:4], dst, ALU.mult, ALU.add
                                                 ).then_inc(S["b"], 1)
                    for u in range(NU):
                        g, kv, br, i = units[u]
                        n = (i + 1) * P
                        dve.wait_ge(s_mh[kv], (g + 1) * 16)
                        dve.wait_ge(S["s"], u + 1)
                        if u >= LAG:
                            invert(u - LAG)
                        else:
                            dve.memset(spare, 0.0)
                        dve.tensor_tensor_reduce(Sx[u % 4][:, 0:n], PS[:, u % 3, 0:n], mh[:, kv, SEQ - n:SEQ], 1.0, 3.0 * MASKED,
                                                 ALU.add, ALU.max, st[:, u % 8, 0:1]).then_inc(S["x"], 1)
                        if u >= LAG:
                            finish(u - LAG)
                        dve.wait_ge(S["x"], u + 1)
                        dve.tensor_scalar(st[:, u % 8, 1:2], st[:, u % 8, 0:1], -1.0, None, ALU.mult).then_inc(S["nm"], 1)
                    for u in range(NU - LAG, NU):
                        invert(u)
                        finish(u)

        def attend_sample():
            o = O_FREE
            qbd = at(o, DEC_BATCH, 2, P)
            kt = at(o + 2048, 2, PAST_LEN)
            ktw = at(o + 4096, 2, WINDOW)
            Ss = at(o + 5120, PAST_LEN + NS)
            Sw = at(o + 6208, WINDOW + NS)
            bs = at(o + 6784, PAST_LEN)
            bw = at(o + 7808, WINDOW)
            bn = at(o + 8320, 120)
            cb = at(o + 8440, 2, 120)
            pc = at(o + 8680, 2, ALL_PAGES)
            pcT = at(o + 8808, 2, P)
            PTs = at(o + 9064, 9, P)
            PTw = at(o + 10216, 5, P)
            osb = at(o + 10856, 3, HD)
            qb = [at(o + 11048, 2, P), at(o + 13440, 2, P)]
            pgw0 = at(o + 11304, 4, 512)
            st = at(o + 13352, 24)
            sel = at(o + 13376, 4, 16)
            pgs = [at(O_OT, PAGES, 512), at(O_NAT, PAGES, 512)]
            pgw = [pgw0, at(O_NAT + 2 * 5 * 512, 4, 512)]
            names = ("bias", "z", "fill", "qbd", "cbz", "qb", "cs", "nmc", "ec", "pn", "pct", "pctc", "kt", "ktc", "ss", "sw",
                     "nms", "nmw", "es", "ew", "tp", "tpc", "ov", "osc", "og", "dch")
            S = {n: sem("sa_" + n) for n in names}
            lp = [[sem(f"sa_pg{s}_{part}") for part in range(2)] for s in range(2)]
            lw = [sem(f"sa_pw{s}") for s in range(2)]
            cache = io["cache_slc_kv"].rearrange("a n p h c d -> (a n) p (h c d)")
            win = io["cache_win_kv"].rearrange("a b (i p) h c d -> (a b) p i (h c d)", p=P)

            with nc.Block() as block:
                @block.sync
                def _(sp):
                    with nc.allow_non_contiguous_dma(reason="strided biases of the compressed blocks"):
                        sp.dma_start(bs, bass.AP(scr_r, TOP_R - PAST_LEN, [[LEN_R, N_HEADS], [-1, DEC_SEQ], [1, PAST_LEN]])).then_inc(S["bias"], 16)
                        sp.dma_start(bw, bass.AP(scr_w, TOP_W - WINDOW, [[LEN_W, N_HEADS], [-1, DEC_SEQ], [1, WINDOW]])).then_inc(S["bias"], 16)
                        sp.wait_ge(S["fill"], 2)
                        sp.dma_start(bn[:, 56:64], bass.AP(scr_r, TOP_R, [[LEN_R, N_HEADS], [-1, DEC_SEQ], [1, DEC_SEQ]])).then_inc(S["bias"], 16)
                    def load(s, b):
                        for j in range(PAGES):
                            page = sp.value_load(page_sb[0:1, bass.ds(b * PAGES + j, 1)], min_val=0, max_val=N_POOL - 1)
                            sp.dma_start(pgs[s][:, j, :], cache[bass.ds(page, 1), :, :].rearrange("a p n -> (a p) n")).then_inc(lp[s][j // 4], 16)
                        sp.dma_start(pgw[s], win[bass.ds(b, 1), :, :, :].rearrange("a p i n -> (a p) i n")).then_inc(lw[s], 16)
                    for s in range(2):
                        load(s, s)
                    with sp.Fori(0, DEC_BATCH // 2 - 1) as i:
                        for s in range(2):
                            sp.wait_ge(S["ov"], i * 2 + (s + 1))
                            load(s, i * 2 + (s + 2))

                @block.gpsimd
                def _(pool):
                    pool.memset(qbd[:, :, :, :], 0.0).then_inc(S["z"], 1)
                    for b in range(DEC_BATCH):
                        pool.wait_ge(S["osc"], b + 1)
                        for br in range(3):
                            pool.dma_start(bass.AP(scr_o, (br * NS + b * DEC_SEQ) * ATT_WIDTH,
                                                   [[HD, N_HEADS], [ATT_WIDTH, DEC_SEQ], [1, HD]]), osb[:, br, :]).then_inc(S["og"], 16)
                    pool.wait_ge(S["og"], 16 * 3 * DEC_BATCH)


                @block.tensor
                def _(pe):
                    pe.wait_ge(S["z"], 1)

                    def keys(s, i):
                        first = known(i) and i == 0
                        for j in range(12):
                            if j in (0, 4):
                                pe.wait_ge(lp[s][j // 4], (i + 1) * (16 * 4))
                            if j == 8:
                                pe.wait_ge(lw[s], (i + 1) * 16)
                            if j >= 2:
                                pe.wait_ge(S["ktc"], i * 48 + (24 * s + 2 * (j - 1)))
                            elif j == 0 and not first:
                                pe.wait_ge(S["tpc"], i * 8 + (4 * s - 4))
                            src = pgs[s][:, j, :] if j < 8 else pgw[s][:, j - 8, :]
                            kt_transposes(pe, 2 + j % 2, src).then_inc(S["kt"], 1)
                    keys(0, 0)
                    for i in turns(pe, False, DEC_BATCH // 2):
                        for s in range(2):
                            b2 = i * 2
                            pe.wait_ge(S["qb"], b2 + (s + 1))
                            for p in range(2):
                                m = pe.matmul(PS[:, 0, 0:P], qb[s][:, p, :], kc_all[:, p, :, :].rearrange("p a b -> p (a b)"),
                                              start=(p == 0), stop=(p == 1))
                            m.then_inc(S["cs"], 1)
                            pe.wait_ge(S["ktc"], b2 * 24 + (24 * s + 16))
                            for half in range(2):
                                for p in range(2):
                                    pe.matmul(PS[:, 4 + half, :], qb[s][:, p, :], kt[:, p, 512 * half:512 * half + 512], start=(p == 0), stop=(p == 1))
                            pe.wait_ge(S["nmc"], b2 + (s + 1))
                            for p in range(2):
                                m = pe.matmul(PS[:, 0, P:P + NS], qb[s][:, p, :], ktn[:, 0, p, :], start=(p == 0), stop=(p == 1))
                            m.then_inc(S["ss"], 1)
                            pe.wait_ge(S["ktc"], b2 * 24 + (24 * s + 24))
                            if not (known(i) and i == 0 and s == 0):
                                pe.wait_ge(S["osc"], b2 + s)
                            for p in range(2):
                                pe.matmul(PS[:, 6, :], qb[s][:, p, :], ktw[:, p, :], start=(p == 0), stop=(p == 1))
                            for p in range(2):
                                m = pe.matmul(PS[:, 0, P + NS:P + 2 * NS], qb[s][:, p, :], ktn[:, 1, p, :], start=(p == 0), stop=(p == 1))
                            m.then_inc(S["sw"], 1)
                            pe.wait_ge(S["pn"], b2 + (s + 1))
                            pe.matmul(PS[:, 1, 0:16], sq6[:, GROUP, :], pc[:, :, bass.ds(b2 * 8 + 8 * s, 8)], start=True, stop=True)
                            for half in range(2):
                                m = pe.transpose(PS[0:64, 1, P + half * P:2 * P + half * P], pc[:, half, :], ident)
                            m.then_inc(S["pct"], 1)
                            pe.wait_ge(S["pctc"], b2 + (s + 1))
                            for half in range(2):
                                m = pe.matmul(PS[:, 7, 0:256], pcT[0:64, half, :], vc_all[:, half, :], start=(half == 0), stop=(half == 1))
                            if s == 0:
                                keys(1, i)
                            elif not (known(i) and i):
                                keys(0, i + 1)
                            pe.wait_ge(S["ktc"], b2 * 24 + (24 * s + (24 if known(i) and i and s else 48)))
                            pe.wait_ge(S["ew"], b2 + (s + 1))
                            pe.wait_ge(S["es"], b2 + (s + 1))
                            for j in range(4):
                                m = pe.transpose(PS[:, 2, j * P:(j + 1) * P], Sw[:, j * P:(j + 1) * P], ident)
                            m.then_inc(S["tp"], 1)
                            pe.transpose(PS[0:64, 3, 0:P], Sw[:, 512:576], ident)
                            pe.transpose(PS[0:64, 3, P:2 * P], Ss[:, 1024:1088], ident).then_inc(S["tp"], 1)
                            for half in range(2):
                                pe.wait_ge(S["tpc"], i * 8 + (4 * s + half + 1))
                                for j in range(4):
                                    c0 = 512 * half + j * P
                                    m = pe.transpose(PS[:, 2 + half, j * P:(j + 1) * P], Ss[:, c0:c0 + P], ident)
                                m.then_inc(S["tp"], 1)
                            vcols = lambda rows: rows.rearrange("p (h c d) -> p h c d", h=N_KV, c=2)[:, :, 1, :]
                            for j in range(5):
                                v = vcols(pgw[s][:, j, :]) if j < 4 else vcols(nat[0:NS, 2, 4, :])
                                pr = PTw[:, j, :] if j < 4 else PTw[0:NS, 4, :]
                                pe.matmul(PS[:, 6, 0:256], pr, v, start=(j == 0), stop=(j == 4))
                            pe.wait_ge(S["tpc"], i * 8 + (4 * s + 4))
                            for j in range(9):
                                v = vcols(pgs[s][:, j, :]) if j < 8 else vcols(nat[0:NS, 1, 4, :])
                                pr = PTs[:, j, :] if j < 8 else PTs[0:NS, 8, :]
                                m = pe.matmul(PS[:, 7, 256:512], pr, v, start=(j == 0), stop=(j == 8))
                            m.then_inc(S["ov"], 1)

                @block.scalar
                def _(act):
                    act.wait_ge(S["z"], 1)

                    def keys(which, tiles):
                        i, s = which
                        for j in tiles:
                            act.wait_ge(S["kt"], i * 24 + (12 * s + j + 1))
                            lo, hi = kt_halves(2 + j % 2, P)
                            dst = kt[:, :, j * P:(j + 1) * P] if j < 8 else ktw[:, :, (j - 8) * P:(j - 7) * P]
                            act.copy(dst[0:64], lo).then_inc(S["ktc"], 1)
                            act.copy(dst[64:P], hi).then_inc(S["ktc"], 1)
                    keys((0, 0), range(12))
                    for i in turns(act, False, DEC_BATCH // 2):
                        for s in range(2):
                            b2 = i * 2
                            act.wait_ge(S["nmc"], b2 + (s + 1))
                            act.activation(pc[:, :, :], pc[:, :, :], ACT.Exp, bias=st[:, 1:2], accum_out=st[:, 2:3]).then_inc(S["ec"], 1)
                            act.wait_ge(S["pct"], b2 + (s + 1))
                            act.copy(pcT[0:64, :, :], PS[0:64, 1, P:3 * P].rearrange("p (a n) -> p a n", a=2)).then_inc(S["pctc"], 1)
                            act.wait_ge(S["nmw"], b2 + (s + 1))
                            act.activation(Sw, Sw, ACT.Exp, bias=st[:, 5:6], accum_out=st[:, 6:7]).then_inc(S["ew"], 1)
                            more = s == 0 or not (known(i) and i)
                            if more:
                                keys((i, 1) if s == 0 else (i + 1, 0), range(8))
                            act.wait_ge(S["nms"], b2 + (s + 1))
                            act.activation(Ss, Ss, ACT.Exp, bias=st[:, 9:10], accum_out=st[:, 10:11]).then_inc(S["es"], 1)
                            if more:
                                keys((i, 1) if s == 0 else (i + 1, 0), range(8, 12))
                            act.wait_ge(S["tp"], i * 8 + (4 * s + 1))
                            act.copy(PTw[:, 0:4, :].rearrange("p a n -> p (a n)"), PS[:, 2, :]).then_inc(S["tpc"], 1)
                            act.wait_ge(S["tp"], i * 8 + (4 * s + 2))
                            act.copy(PTw[0:NS, 4, :], PS[0:NS, 3, 0:P])
                            act.copy(PTs[0:NS, 8, :], PS[0:NS, 3, P:2 * P]).then_inc(S["tpc"], 1)
                            for half in range(2):
                                act.wait_ge(S["tp"], i * 8 + (4 * s + 3 + half))
                                act.copy(PTs[:, 4 * half:4 * half + 4, :].rearrange("p a n -> p (a n)"), PS[:, 2 + half, :]).then_inc(S["tpc"], 1)

                @block.vector
                def _(dve):
                    ch = Chain(dve, S["dch"])
                    dve.memset(bn, MASKED).then_inc(S["fill"], 1)
                    dve.memset(cb[:, :, :], MASKED).then_inc(S["fill"], 1)
                    dve.wait_ge(S["z"], 1)
                    for p in range(2):
                        for e in range(2):
                            src = qT[64 * e:64 * e + 64, 4 * p:4 * p + 4, SEQ:T].rearrange("p g (b t) -> p g b t", t=DEC_SEQ)
                            c0 = (2 * p + e) * 32
                            dst = qbd[64 * e:64 * e + 64, :, p, c0:c0 + 32].rearrange("p b (g t) -> p g b t", t=DEC_SEQ)
                            for g in range(GQA):
                                ins = dve.tensor_copy(dst[:, g], src[:, g])
                    ins.then_inc(S["qbd"], 1)
                    dve.wait_ge(S["qbd"], 1)
                    dve.wait_ge(S["bias"], 16 * 3)
                    ends = bs.rearrange("p (g a l) -> p a g l", a=2, l=BLK)[:, :, :, BLK - 1]
                    dve.tensor_copy(cb[:, :, 56:64], ends).then_inc(S["cbz"], 1)
                    dve.wait_ge(S["cbz"], 1)
                    PER = 40

                    def query(s, b):
                        dve.tensor_copy(qb[s], qbd[:, bass.ds(b, 1), :, :].rearrange("p a b n -> p (a b) n")).then_inc(S["qb"], 1)
                    query(0, 0)
                    for i in turns(dve, False, DEC_BATCH // 2):
                        ch.enter(i, PER)
                        for s in range(2):
                            b2 = i * 2
                            off = 56 - (b2 * 8 + 8 * s)
                            dve.wait_ge(S["cs"], b2 + (s + 1))
                            ch.link(dve.tensor_tensor(pc[:, :, :], PS[:, 0, 0:P].rearrange("p (a n) -> p a n", a=2),
                                                      cb[:, :, bass.ds(off, 64)], ALU.add))
                            ch.link(dve.tensor_reduce(st[:, 0:1], pc[:, :, :].rearrange("p a n -> p (a n)"), AXX, ALU.max))
                            dve.tensor_scalar(st[:, 1:2], st[:, 0:1], 0.1 * MASKED, -1.0, ALU.max, ALU.mult).then_inc(S["nmc"], 1)
                            dve.wait_ge(S["ec"], b2 + (s + 1))
                            ch.link(dve.tensor_scalar(st[:, 2:3], st[:, 2:3], 1e-30, None, ALU.max))
                            ch.link(dve.reciprocal(st[:, 3:4], st[:, 2:3]))
                            dve.tensor_scalar(pc[:, :, :], pc[:, :, :], st[:, 3:4], None, ALU.mult).then_inc(S["pn"], 1)
                            dve.wait_ge(S["sw"], b2 + (s + 1))
                            ch.link(dve.tensor_tensor(Sw[:, 0:512], PS[:, 6, :], bw, ALU.add))
                            ch.link(dve.tensor_tensor(Sw[:, 512:576], PS[:, 0, P + NS:P + 2 * NS], bn[:, bass.ds(off, 64)], ALU.add))
                            ch.link(dve.tensor_reduce(st[:, 4:5], Sw, AXX, ALU.max))
                            dve.tensor_scalar(st[:, 5:6], st[:, 4:5], -1.0, None, ALU.mult).then_inc(S["nmw"], 1)
                            dve.wait_ge(S["pctc"], b2 + (s + 1))
                            ch.link(dve.tensor_tensor(sel[:, 0, :], PS[:, 1, 0:16], crow[:, 1, :], ALU.add))
                            ch.link(dve.tensor_reduce(st[:, 12:13], sel[:, 0, :], AXX, ALU.min))
                            ch.link(dve.scalar_tensor_tensor(sel[:, 1, :], sel[:, 0, :], st[:, 12:13], crow[:, 0, :], ALU.is_equal, ALU.mult))
                            ch.link(dve.tensor_reduce(st[:, 13:14], sel[:, 1, :], AXX, ALU.max))
                            ch.link(dve.tensor_scalar(sel[:, 2, :], crow[:, 0, :], st[:, 13:14], MASKED, ALU.is_equal, ALU.mult))
                            dve.wait_ge(S["ss"], b2 + (s + 1))
                            for half in range(2):
                                ch.link(dve.tensor_tensor(Ss[:, 512 * half:512 * half + 512], PS[:, 4 + half, :],
                                                          bs[:, 512 * half:512 * half + 512], ALU.add))
                            ch.link(dve.tensor_tensor(Ss[:, 1024:1088], PS[:, 0, P:P + NS], bn[:, bass.ds(off, 64)], ALU.add))
                            for half in range(2):
                                v = Ss[:, 0:1024].rearrange("p (g a l) -> p g a l", a=2, l=BLK)[:, :, half, :]
                                ch.link(dve.tensor_tensor(v, v, sel[:, 2, 8 * half:8 * half + 8].unsqueeze(2).to_broadcast([P, 8, BLK]), ALU.add))
                            ch.link(dve.tensor_reduce(st[:, 8:9], Ss, AXX, ALU.max))
                            dve.tensor_scalar(st[:, 9:10], st[:, 8:9], -1.0, None, ALU.mult).then_inc(S["nms"], 1)
                            if s == 0 or not (known(i) and i):
                                query(1 - s, b2 + (s + 1))
                            dve.wait_ge(S["es"], b2 + (s + 1))
                            dve.wait_ge(S["ew"], b2 + (s + 1))
                            ch.link(dve.reciprocal(st[:, 7:8], st[:, 6:7]))
                            ch.link(dve.reciprocal(st[:, 11:12], st[:, 10:11]))
                            if not (known(i) and i == 0 and s == 0):
                                dve.wait_ge(S["og"], i * (2 * 48) + 48 * s)
                            dve.wait_ge(S["ov"], b2 + (s + 1))
                            for h in range(N_KV):
                                r = slice(32 * h, 32 * h + 32)
                                dve.tensor_copy(osb[r, 0, :], PS[r, 7, HD * h:HD * h + HD])
                                dve.tensor_scalar(osb[r, 1, :], PS[r, 7, 256 + HD * h:256 + HD * h + HD], st[r, 11:12], None, ALU.mult)
                                ins = dve.tensor_scalar(osb[r, 2, :], PS[r, 6, HD * h:HD * h + HD], st[r, 7:8], None, ALU.mult)
                            ins.then_inc(S["osc"], 1)
                    ch.leave(DEC_BATCH // 2)

        def attention_out():
            og = at(O_Q, 3, N_HEADS, HD)
            junk = at(O_FREE, ATT_WIDTH)
            st = at(O_FREE + 1024, 5, 2)
            S = {n: sem("ao_" + n) for n in ("dch", "sq", "rt", "n", "t", "c", "z", "ld")}
            with nc.Block() as block:
                @block.sync
                def _(sp):
                    sp.dma_start(og[0:NS, :, :, :].rearrange("p r h d -> p r (h d)"),
                                 scr_o.ap().rearrange("r t n -> t r n")).then_inc(S["ld"], 16)

                @block.vector
                def _(dve):
                    ch = Chain(dve, S["dch"])
                    dve.wait_ge(S["ld"], 16)
                    g3 = sg[0:NS, 4, :].rearrange("p (h r) -> p h r", r=3)
                    for br in range(3):
                        ch.link(dve.tensor_tensor(og[0:NS, br, :, :], og[0:NS, br, :, :],
                                                  g3[:, :, br:br + 1].to_broadcast([NS, 16, HD]), ALU.mult))
                    flat = [og[0:NS, br, :, :].rearrange("p h d -> p (h d)") for br in range(3)]
                    ch.link(dve.tensor_tensor(flat[0], flat[0], flat[1], ALU.add))
                    dve.tensor_tensor(onat[0:NS, 4, :], flat[0], flat[2], ALU.add).then_inc(S["z"], 1)
                    for i, (t0, n) in enumerate(TILES):
                        dve.wait_ge(S["rt"], i + 1)
                        ch.link(dve.reciprocal(st[0:n, i, 1:2], st[0:n, i, 1:2]))
                        dve.tensor_scalar(onat[0:n, i, :], onat[0:n, i, :], st[0:n, i, 1:2], None, ALU.mult).then_inc(S["n"], 1)
                    u = 0
                    for i, (t0, n) in enumerate(TILES):
                        for q in range(2):
                            dve.wait_ge(S["t"], u + 1)
                            for j in range(4):
                                k = 4 * q + j
                                ins = dve.tensor_scalar(oT[:, k, t0:t0 + n], PS[:, u % 4, j * P:j * P + n],
                                                        gT[:, 8 * GATT + k:8 * GATT + k + 1], None, ALU.mult)
                            ins.then_inc(S["c"], 1)
                            u += 1

                @block.scalar
                def _(act):
                    for i, (t0, n) in enumerate(TILES):
                        if i == 4:
                            act.wait_ge(S["z"], 1)
                        act.activation(junk[0:n, :], onat[0:n, i, :], ACT.Square, scale=ATT_WIDTH ** -0.5,
                                       accum_out=st[0:n, i, 0:1]).then_inc(S["sq"], 1)
                        act.wait_ge(S["sq"], i + 1)
                        act.activation(st[0:n, i, 1:2], st[0:n, i, 0:1], ACT.Sqrt, bias=eps_sb[0:n, 0:1]).then_inc(S["rt"], 1)

                @block.tensor
                def _(pe):
                    u = 0
                    for i, (t0, n) in enumerate(TILES):
                        pe.wait_ge(S["n"], i + 1)
                        for q in range(2):
                            if u >= 4:
                                pe.wait_ge(S["c"], u - 3)
                            for j in range(4):
                                m = pe.transpose(PS[:, u % 4, j * P:j * P + n], onat[0:n, i, (4 * q + j) * P:(4 * q + j + 1) * P], ident[0:n, 0:n])
                            m.then_inc(S["t"], 1)
                            u += 1

        def mixer_out():
            x = Split("mo_x", O_Q, D_MIX // P, T)
            o = O_Q + 2 * (D_MIX // P) * T
            kp = D_MIX // P // 2
            nrm = Norm("f2_pre", xT)
            project_out("mo", io["w_out"].rearrange("a k n -> (a k) n"), D_MIX // P, x, at(o, KD, T), o + KD * T,
                        o + KD * T + 4 * kp * P, GMPOST, source=oT, follow=nrm)
            return nrm

        f1_norm, mix_norm = Norm("f1_pre", xT), Norm("mix_pre", xT)
        setup(f1_norm)
        ffn("f1", io["ffn1_w_in"].rearrange("a k n -> (a k) n"), io["ffn1_w_out"].rearrange("a k n -> (a k) n"), G1PRE, G1POST,
            f1_norm, follow=mix_norm, beside=copies)
        mixer_in(mix_norm)
        conv()
        ssd()
        ssd_gate_norm()
        recycle_semaphores()
        compress_prompt()
        attend_prompt()
        attend_sample()
        attention_out()
        f2_norm = mixer_out()
        ffn("f2", io["ffn2_w_in"].rearrange("a k n -> (a k) n"), io["ffn2_w_out"].rearrange("a k n -> (a k) n"), G2PRE, G2POST,
            f2_norm)
        finish_out()


_INS = ['x_prompt', 'x_sample', 'cache_cmp_kv', 'cache_slc_kv', 'cache_win_kv', 'state_ssm', 'state_conv',
        'page_table', 'rel_table', 'ffn1_pre', 'ffn1_post', 'ffn1_w_in', 'ffn1_w_out', 'mix_pre', 'mix_post',
        'w_in', 'w_out', 'att_out_norm', 'cmp_pe', 'w_cmp', 'conv_w', 'conv_b', 'dt_bias', 'a_log', 'd_skip',
        'ssd_norm', 'ffn2_pre', 'ffn2_post', 'ffn2_w_in', 'ffn2_w_out']
_OUTS = [("y_prompt", (1, 512, 1024)), ("y_sample", (8, 8, 1024)),
         ("p_cmp_kv", (1, 1, 512, 4, 2, 64)), ("p_slc_kv", (1, 1, 512, 4, 2, 64)), ("p_win_kv", (1, 1, 512, 4, 2, 64)),
         ("p_ssm", (1, 1, 16, 64, 128)), ("p_conv", (1, 1, 3, 1536)),
         ("s_cmp_kv", (1, 8, 8, 4, 2, 64)), ("s_slc_kv", (1, 8, 8, 4, 2, 64)), ("s_win_kv", (1, 8, 512, 4, 2, 64)),
         ("s_ssm", (1, 8, 16, 64, 128)), ("s_conv", (1, 8, 3, 1536))]


def kernel(**inputs):
    import numpy as _np
    import concourse.bacc as _bacc
    from concourse import mybir as _mybir
    from concourse.bass_utils import run_bass_kernel_spmd as _run

    nc = _bacc.Bacc("TRN2", target_bir_lowering=False, num_devices=1)
    arrays, io = {}, {}
    for name in _INS:
        arrays[f"in_{name}"] = _np.ascontiguousarray(inputs[name])
    for name, value in constants().items():
        arrays[f"in_{name}"] = value
    for name, a in arrays.items():
        io[name[3:]] = nc.dram_tensor(name, a.shape, _mybir.dt.from_np(a.dtype), kind="ExternalInput").ap()
    out = {name: nc.dram_tensor(f"out_{name}", shape, F32, kind="ExternalOutput").ap() for name, shape in _OUTS}
    build(nc, io, out)
    r = _run(nc, [arrays], core_ids=[0])
    return tuple(r.results[0][f"out_{name}"] for name, _ in _OUTS)
```
